# Optimizing a Trainium2 kernel written in Bass

```python
import math
import jax, jax.numpy as jnp
from jax import lax
import numpy as np
import jax
import jax.numpy as jnp

D_MODEL = 2048
BATCH = 1
SEQ = 256
DEPTH = 1

DILATED_GROUPS = ((128, 1), (512, 4), (2048, 16))
N_ATTN_GROUPS = len(DILATED_GROUPS)
HEADS_PER_GROUP = 4
HEAD_DIM = 128
N_ATTN_HEADS = N_ATTN_GROUPS * HEADS_PER_GROUP
QKV_W = N_ATTN_HEADS * HEAD_DIM
ATTN_OUT = HEADS_PER_GROUP * HEAD_DIM
REL_BUCKETS = 32
REL_MAX_DIST = 2048
D_INNER = 2 * D_MODEL
SSM_HEAD_DIM = 64
SSM_HEADS = D_INNER // SSM_HEAD_DIM
SSM_GROUPS = 8
HEADS_PER_SSM_GROUP = SSM_HEADS // SSM_GROUPS
D_STATE = 128
CONV_K = 4
CHUNK = 128
CONV_DIM = D_INNER + 2 * SSM_GROUPS * D_STATE
D_FF = ((8 * D_MODEL // 3 + 255) // 256) * 256
SPLITS = (QKV_W, QKV_W, QKV_W, D_INNER, CONV_DIM, SSM_HEADS, D_MODEL, D_MODEL)
N_IN = sum(SPLITS)
EPS = 1e-6


def rmsnorm(x, w):
    x32 = x.astype(jnp.float32)
    y = x32 * lax.rsqrt(jnp.mean(x32 * x32, axis=-1, keepdims=True) + EPS)
    return (y * w.astype(jnp.float32)).astype(x.dtype)

def t5_bucket(dist):
    exact = REL_BUCKETS // 2
    n = jnp.maximum(dist, 1).astype(jnp.float32)
    large = exact + (jnp.log(n / exact) / math.log(REL_MAX_DIST / exact)
                     * (REL_BUCKETS - exact)).astype(jnp.int32)
    large = jnp.minimum(large, REL_BUCKETS - 1)
    return jnp.where(dist < exact, dist, large)

def dilated_window_attention(q, k, v, bias_table, window, dilation):
    B, S, Hg, Dh = q.shape
    blk = window // dilation
    unit = blk * dilation
    Sp = -(-S // unit) * unit
    L = Sp // dilation
    nb = L // blk

    def to_blocks(t):
        t = jnp.pad(t, ((0, 0), (0, Sp - S), (0, 0), (0, 0)))
        t = t.reshape(B, L, dilation, Hg, Dh).transpose(0, 2, 1, 3, 4)
        return t.reshape(B, dilation, nb, blk, Hg, Dh)

    qb, kb, vb = to_blocks(q), to_blocks(k), to_blocks(v)

    def with_prev(t):
        prev = jnp.pad(t[:, :, :-1], ((0, 0), (0, 0), (1, 0), (0, 0), (0, 0), (0, 0)))
        return jnp.concatenate([prev, t], axis=3)

    kk, vv = with_prev(kb), with_prev(vb)
    logits = jnp.einsum('brnqhd,brnkhd->brnhqk', qb, kk).astype(jnp.float32) / math.sqrt(Dh)

    qi = jnp.arange(blk)[:, None]
    kj = jnp.arange(2 * blk)[None, :]
    steps = blk + qi - kj
    band = (steps >= 0) & (steps <= blk)
    first = (jnp.arange(nb) == 0)[:, None, None]
    valid = band[None] & ~(first & (kj < blk)[None])
    bucket = t5_bucket(jnp.clip(steps, 0, blk) * dilation)
    bias = bias_table[bucket].astype(jnp.float32).transpose(2, 0, 1)

    logits = jnp.where(valid[None, None, :, None], logits + bias[None, None, None], -jnp.inf)
    m = jnp.max(logits, axis=-1, keepdims=True)
    p = jnp.exp(logits - m)
    s = jnp.sum(p, axis=-1, keepdims=True)
    o = jnp.einsum('brnhqk,brnkhd->brnqhd', (p / s).astype(v.dtype), vv)
    lse = (m + jnp.log(s))[..., 0]

    o = o.reshape(B, dilation, L, Hg, Dh).transpose(0, 2, 1, 3, 4).reshape(B, Sp, Hg, Dh)[:, :S]
    lse = lse.transpose(0, 1, 2, 4, 3).reshape(B, dilation, L, Hg)
    lse = lse.transpose(0, 2, 1, 3).reshape(B, Sp, Hg)[:, :S]
    return o, lse

def ssd_chunked(xs, dt, A, Bm, Cm):
    Bsz, S, H, P = xs.shape
    G, N = Bm.shape[2], Bm.shape[3]
    R = H // G
    nc = S // CHUNK
    f32 = jnp.float32
    x = xs.astype(f32).reshape(Bsz, nc, CHUNK, G, R, P)
    dtc = dt.astype(f32).reshape(Bsz, nc, CHUNK, G, R)
    Bc = Bm.astype(f32).reshape(Bsz, nc, CHUNK, G, N)
    Cc = Cm.astype(f32).reshape(Bsz, nc, CHUNK, G, N)
    acum = jnp.cumsum(dtc * A.astype(f32).reshape(G, R), axis=2)
    xdt = x * dtc[..., None]

    at = jnp.moveaxis(acum, 2, -1)
    seg = at[..., :, None] - at[..., None, :]
    tril = jnp.tril(jnp.ones((CHUNK, CHUNK), dtype=bool))
    Ldec = jnp.exp(jnp.where(tril, seg, -jnp.inf))
    cb = jnp.einsum('bclgn,bcsgn->bcgls', Cc, Bc)
    y_diag = jnp.einsum('bcgrls,bcsgrp->bclgrp', cb[:, :, :, None] * Ldec, xdt)

    decay_states = jnp.exp(acum[:, :, -1:] - acum)
    states = jnp.einsum('bclgn,bclgrp->bcgrpn', Bc, xdt * decay_states[..., None])
    chunk_decay = jnp.exp(acum[:, :, -1])

    def step(h, inp):
        st, dec = inp
        return h * dec[..., None, None] + st, h

    h0 = jnp.zeros_like(states[:, 0])
    _, prev = lax.scan(step, h0, (jnp.moveaxis(states, 1, 0), jnp.moveaxis(chunk_decay, 1, 0)))
    prev = jnp.moveaxis(prev, 0, 1)

    y_off = jnp.einsum('bclgn,bcgrpn,bclgr->bclgrp', Cc, prev, jnp.exp(acum))
    return (y_diag + y_off).reshape(Bsz, S, H, P)

def causal_depthwise_conv(u, w, b):
    S = u.shape[1]
    up = jnp.pad(u, ((0, 0), (CONV_K - 1, 0), (0, 0)))
    out = b
    for j in range(CONV_K):
        out = out + up[:, j:j + S] * w[j]
    return out

def mixer(h, rel_bias, w_in, conv_w, conv_b, dt_bias, a_log, d_skip, ssm_norm_w,
          w_attn_proj, w_ssm_proj, w_out):
    B, S, _ = h.shape
    proj = h @ w_in
    q, k, v, z, xbc, dt_raw, g_attn, g_ssm = jnp.split(
        proj, np.cumsum(SPLITS)[:-1].tolist(), axis=-1)

    q = q.reshape(B, S, N_ATTN_GROUPS, HEADS_PER_GROUP, HEAD_DIM)
    k = k.reshape(B, S, N_ATTN_GROUPS, HEADS_PER_GROUP, HEAD_DIM)
    v = v.reshape(B, S, N_ATTN_GROUPS, HEADS_PER_GROUP, HEAD_DIM)
    outs, lses = [], []
    for g, (window, dilation) in enumerate(DILATED_GROUPS):
        o, lse = dilated_window_attention(
            q[:, :, g], k[:, :, g], v[:, :, g],
            rel_bias[:, g * HEADS_PER_GROUP:(g + 1) * HEADS_PER_GROUP], window, dilation)
        outs.append(o)
        lses.append(lse)
    wts = jax.nn.softmax(jnp.stack(lses, axis=0), axis=0)
    attn = jnp.sum(wts[..., None] * jnp.stack(outs, axis=0).astype(jnp.float32), axis=0)
    attn = attn.astype(h.dtype).reshape(B, S, ATTN_OUT)

    xbc = jax.nn.silu(causal_depthwise_conv(xbc, conv_w, conv_b))
    xs, Bm, Cm = jnp.split(xbc, [D_INNER, D_INNER + SSM_GROUPS * D_STATE], axis=-1)
    xs = xs.reshape(B, S, SSM_HEADS, SSM_HEAD_DIM)
    dt = jax.nn.softplus(dt_raw.astype(jnp.float32) + dt_bias.astype(jnp.float32))
    A = -jnp.exp(a_log.astype(jnp.float32))
    y = ssd_chunked(xs, dt, A, Bm.reshape(B, S, SSM_GROUPS, D_STATE),
                    Cm.reshape(B, S, SSM_GROUPS, D_STATE))
    y = y + d_skip.astype(jnp.float32)[:, None] * xs.astype(jnp.float32)
    y = y.reshape(B, S, D_INNER) * jax.nn.silu(z.astype(jnp.float32))
    y = y.reshape(B, S, SSM_GROUPS, D_INNER // SSM_GROUPS)
    y = y * lax.rsqrt(jnp.mean(y * y, axis=-1, keepdims=True) + EPS)
    y = (y.reshape(B, S, D_INNER) * ssm_norm_w.astype(jnp.float32)).astype(h.dtype)

    merged = jax.nn.sigmoid(g_attn) * (attn @ w_attn_proj) + jax.nn.sigmoid(g_ssm) * (y @ w_ssm_proj)
    return merged @ w_out

def swiglu(h, w_ffn_in, w_ffn_out):
    hg, hu = jnp.split(h @ w_ffn_in, 2, axis=-1)
    return (jax.nn.silu(hg) * hu) @ w_ffn_out

def first_inputs(seed: int = 0) -> dict:
    key = jax.random.key(seed)
    ks = jax.random.split(key, 24)
    f32 = jnp.float32

    def nrm(k, shape, s):
        return jax.random.normal(k, shape, f32) * s

    dt0 = jnp.exp(jax.random.uniform(ks[10], (DEPTH, SSM_HEADS), f32)
                  * (math.log(0.1) - math.log(0.001)) + math.log(0.001))
    return {
        "x": nrm(ks[0], (BATCH, SEQ, D_MODEL), 1.0),
        "c": nrm(ks[1], (BATCH, D_MODEL), 1.0),
        "rel_bias": nrm(ks[2], (REL_BUCKETS, N_ATTN_HEADS), 0.5),
        "norm1_w": 1.0 + nrm(ks[3], (DEPTH, D_MODEL), 0.05),
        "norm2_w": 1.0 + nrm(ks[4], (DEPTH, D_MODEL), 0.05),
        "w_mod": nrm(ks[5], (DEPTH, D_MODEL, 6 * D_MODEL), D_MODEL ** -0.5),
        "b_mod": nrm(ks[6], (DEPTH, 6 * D_MODEL), 0.01),
        "w_in": nrm(ks[7], (DEPTH, D_MODEL, N_IN), D_MODEL ** -0.5),
        "conv_w": nrm(ks[8], (DEPTH, CONV_K, CONV_DIM), CONV_K ** -0.5),
        "conv_b": nrm(ks[9], (DEPTH, CONV_DIM), 0.01),
        "dt_bias": dt0 + jnp.log(-jnp.expm1(-dt0)),
        "a_log": jnp.log(jax.random.uniform(ks[11], (DEPTH, SSM_HEADS), f32, 1.0, 16.0)),
        "d_skip": 1.0 + nrm(ks[12], (DEPTH, SSM_HEADS), 0.1),
        "ssm_norm_w": 1.0 + nrm(ks[13], (DEPTH, D_INNER), 0.05),
        "w_attn_proj": nrm(ks[14], (DEPTH, ATTN_OUT, D_MODEL), ATTN_OUT ** -0.5),
        "w_ssm_proj": nrm(ks[15], (DEPTH, D_INNER, D_MODEL), D_INNER ** -0.5),
        "w_out": nrm(ks[16], (DEPTH, D_MODEL, D_MODEL), D_MODEL ** -0.5),
        "w_ffn_in": nrm(ks[17], (DEPTH, D_MODEL, 2 * D_FF), D_MODEL ** -0.5),
        "w_ffn_out": nrm(ks[18], (DEPTH, D_FF, D_MODEL), D_FF ** -0.5),
        "final_norm_w": 1.0 + nrm(ks[19], (D_MODEL,), 0.05),
    }

def first_block(x, c, rel_bias, norm1_w, norm2_w, w_mod, b_mod, w_in, conv_w, conv_b,
              dt_bias, a_log, d_skip, ssm_norm_w, w_attn_proj, w_ssm_proj, w_out,
              w_ffn_in, w_ffn_out, final_norm_w):
    c_act = jax.nn.silu(c)
    for l in range(DEPTH):
        mod = (c_act @ w_mod[l] + b_mod[l])[:, None, :]
        sh1, sc1, g1, sh2, sc2, g2 = jnp.split(mod, 6, axis=-1)
        h = rmsnorm(x, norm1_w[l]) * (1.0 + sc1) + sh1
        x = x + g1 * mixer(h, rel_bias, w_in[l], conv_w[l], conv_b[l], dt_bias[l], a_log[l],
                           d_skip[l], ssm_norm_w[l], w_attn_proj[l], w_ssm_proj[l], w_out[l])
        h = rmsnorm(x, norm2_w[l]) * (1.0 + sc2) + sh2
        x = x + g2 * swiglu(h, w_ffn_in[l], w_ffn_out[l])
    return rmsnorm(x, final_norm_w)


BRANCH_WIDTH = D_MODEL // 2
N_BRANCH = 3
PLE_DIM = 256
NORM_EPS = 1e-6

LRU_BLOCK = 64
LRU_BLOCKS = BRANCH_WIDTH // LRU_BLOCK
CONV_WIDTH = 4
LRU_C = 8.0

NSA_HEADS = BRANCH_WIDTH // HEAD_DIM
NSA_KV_HEADS = 2
NSA_GROUP = NSA_HEADS // NSA_KV_HEADS
NSA_KV_WIDTH = NSA_KV_HEADS * HEAD_DIM
CMP_BLOCK = 32
CMP_STRIDE = 16
CMP_HIDDEN = 256
SEL_BLOCK = 64
SEL_TOPK = 16
WINDOW = 512
NSA_Q_BLOCK = 32

FOX_HEADS = BRANCH_WIDTH // HEAD_DIM
FOX_Q_BLOCK = 128
FORGET_BIAS = 3.0

IN_SPLITS = (
    ('lru_x', BRANCH_WIDTH), ('lru_gate', BRANCH_WIDTH),
    ('nsa_q', BRANCH_WIDTH),
    ('nsa_k_cmp', NSA_KV_WIDTH), ('nsa_v_cmp', NSA_KV_WIDTH),
    ('nsa_k_slc', NSA_KV_WIDTH), ('nsa_v_slc', NSA_KV_WIDTH),
    ('nsa_k_win', NSA_KV_WIDTH), ('nsa_v_win', NSA_KV_WIDTH),
    ('nsa_bgate', NSA_HEADS * 3), ('nsa_gate', BRANCH_WIDTH),
    ('fox_q', BRANCH_WIDTH), ('fox_k', BRANCH_WIDTH), ('fox_v', BRANCH_WIDTH),
    ('fox_f', FOX_HEADS), ('fox_gate', BRANCH_WIDTH),
    ('merge', N_BRANCH * D_MODEL),
)
N_IN_2 = sum(size for _, size in IN_SPLITS)


def column_offsets():
    offs, start = {}, 0
    for name, size in IN_SPLITS:
        offs[name] = (start, size)
        start += size
    return offs

def split_columns(z):
    return {name: z[..., s:s + n] for name, (s, n) in column_offsets().items()}

def split_heads(t, n_heads):
    b, s, _ = t.shape
    return t.reshape(b, s, n_heads, HEAD_DIM)

def rms_norm(x, gain):
    xf = x.astype(jnp.float32)
    y = xf * lax.rsqrt(jnp.mean(xf * xf, axis=-1, keepdims=True) + NORM_EPS)
    return (y * gain.astype(jnp.float32)).astype(x.dtype)

def masked_softmax(logits, mask):
    logits = jnp.where(mask, logits.astype(jnp.float32), -jnp.inf)
    m = jnp.max(logits, axis=-1, keepdims=True)
    m = jnp.where(jnp.isfinite(m), m, 0.0)
    e = jnp.exp(logits - m)
    return e / jnp.maximum(jnp.sum(e, axis=-1, keepdims=True), 1e-30)

def linear_combine(left, right):
    a_l, b_l = left
    a_r, b_r = right
    return a_l * a_r, a_r * b_l + b_r

def rglru_branch(u, conv_w, conv_b, wa, ba, wx, bx, lam):
    b, s, w = u.shape
    taps = conv_w[:, None, :].astype(u.dtype)
    uc = lax.conv_general_dilated(u, taps, (1,), ((CONV_WIDTH - 1, 0),),
                                  dimension_numbers=('NWC', 'WIO', 'NWC'),
                                  feature_group_count=w) + conv_b
    ub = uc.reshape(b, s, LRU_BLOCKS, LRU_BLOCK)
    rec = jax.nn.sigmoid((jnp.einsum('bsnk,nkj->bsnj', ub, wa).reshape(b, s, w) + ba).astype(jnp.float32))
    inp = jax.nn.sigmoid((jnp.einsum('bsnk,nkj->bsnj', ub, wx).reshape(b, s, w) + bx).astype(jnp.float32))
    log_a = -LRU_C * rec * jax.nn.softplus(-lam.astype(jnp.float32))
    a = jnp.exp(log_a)
    drive = jnp.sqrt(-jnp.expm1(2.0 * log_a)) * (inp * uc.astype(jnp.float32))
    _, hseq = lax.associative_scan(linear_combine, (a, drive), axis=1)
    return hseq.astype(u.dtype)

def compress(t, pos, w1, w2):
    b, s, hk, dk = t.shape
    n_chunk = s // CMP_STRIDE
    ratio = CMP_BLOCK // CMP_STRIDE
    n_cmp = n_chunk - ratio + 1
    chunks = t.reshape(b, n_chunk, CMP_STRIDE, hk, dk)
    blocks = jnp.concatenate([chunks[:, r:r + n_cmp] for r in range(ratio)], axis=2)
    blocks = blocks + pos[:, None, :]
    flat = blocks.transpose(0, 1, 3, 2, 4).reshape(b, n_cmp, hk, CMP_BLOCK * dk)
    return jax.nn.silu(flat @ w1) @ w2

def nsa_branch(q, kc, vc, ks, vs, kw, vw, gates):
    b, s, h, dk = q.shape
    scale = dk ** -0.5
    n_cmp = kc.shape[1]
    n_sel = s // SEL_BLOCK
    n_top = min(SEL_TOPK, n_sel)
    nb = s // NSA_Q_BLOCK
    cmp_start = jnp.arange(n_cmp) * CMP_STRIDE
    cmp_end = cmp_start + CMP_BLOCK - 1
    sel_ids = jnp.arange(n_sel)
    sel_start = sel_ids * SEL_BLOCK
    overlap = ((cmp_start[:, None] < sel_start[None, :] + SEL_BLOCK)
               & (cmp_start[:, None] + CMP_BLOCK > sel_start[None, :])).astype(jnp.float32)
    ks_blk = ks.reshape(b, n_sel, SEL_BLOCK, NSA_KV_HEADS, dk).transpose(0, 3, 1, 2, 4)
    vs_blk = vs.reshape(b, n_sel, SEL_BLOCK, NSA_KV_HEADS, dk).transpose(0, 3, 1, 2, 4)
    bi = jnp.arange(b)[:, None, None, None]
    gi = jnp.arange(NSA_KV_HEADS)[None, None, :, None]
    pad = ((0, 0), (WINDOW, 0), (0, 0), (0, 0))
    kw_pad = jnp.pad(kw, pad)
    vw_pad = jnp.pad(vw, pad)
    win_off = jnp.arange(WINDOW + NSA_Q_BLOCK) - WINDOW
    q_blocks = q.reshape(b, nb, NSA_Q_BLOCK, NSA_KV_HEADS, NSA_GROUP, dk).swapaxes(0, 1)
    g_blocks = gates.reshape(b, nb, NSA_Q_BLOCK, NSA_KV_HEADS, NSA_GROUP, 3).swapaxes(0, 1)
    t0s = jnp.arange(nb, dtype=jnp.int32) * NSA_Q_BLOCK
    flat_sel = n_top * SEL_BLOCK

    def block(args):
        qb, gb, t0 = args
        tq = t0 + jnp.arange(NSA_Q_BLOCK)
        s_c = jnp.einsum('btgqd,bcgd->btgqc', qb, kc) * scale
        m_c = (cmp_end[None, :] <= tq[:, None])[None, :, None, None, :]
        p_c = masked_softmax(s_c, m_c)
        o_c = jnp.einsum('btgqc,bcgd->btgqd', p_c.astype(vc.dtype), vc)
        imp = jnp.einsum('btgqc,cj->btgj', p_c, overlap)
        cur = (tq // SEL_BLOCK)[:, None]
        valid = sel_ids[None, :] <= cur
        forced = (sel_ids[None, :] == 0) | (sel_ids[None, :] == cur) | (sel_ids[None, :] == cur - 1)
        score = jnp.where(forced[None, :, None, :], jnp.inf,
                          jnp.where(valid[None, :, None, :], imp, -jnp.inf))
        _, idx = lax.top_k(score, n_top)
        k_sel = ks_blk[bi, gi, idx]
        v_sel = vs_blk[bi, gi, idx]
        s_s = jnp.einsum('btgqd,btgnkd->btgqnk', qb, k_sel) * scale
        kpos = idx[..., None] * SEL_BLOCK + jnp.arange(SEL_BLOCK)
        m_s = kpos <= tq[None, :, None, None, None]
        p_s = masked_softmax(s_s.reshape(b, NSA_Q_BLOCK, NSA_KV_HEADS, NSA_GROUP, flat_sel),
                             m_s.reshape(b, NSA_Q_BLOCK, NSA_KV_HEADS, 1, flat_sel))
        o_s = jnp.einsum('btgqm,btgmd->btgqd', p_s.astype(vs.dtype),
                         v_sel.reshape(b, NSA_Q_BLOCK, NSA_KV_HEADS, flat_sel, dk))
        k_w = lax.dynamic_slice_in_dim(kw_pad, t0, WINDOW + NSA_Q_BLOCK, axis=1)
        v_w = lax.dynamic_slice_in_dim(vw_pad, t0, WINDOW + NSA_Q_BLOCK, axis=1)
        wpos = t0 + win_off
        m_w = ((wpos[None, :] >= 0) & (wpos[None, :] <= tq[:, None])
               & (wpos[None, :] > tq[:, None] - WINDOW))[None, :, None, None, :]
        s_w = jnp.einsum('btgqd,bkgd->btgqk', qb, k_w) * scale
        p_w = masked_softmax(s_w, m_w)
        o_w = jnp.einsum('btgqk,bkgd->btgqd', p_w.astype(vw.dtype), v_w)
        return gb[..., 0:1] * o_c + gb[..., 1:2] * o_s + gb[..., 2:3] * o_w

    out = lax.map(block, (q_blocks, g_blocks, t0s))
    return out.swapaxes(0, 1).reshape(b, s, h * dk)

def fox_branch(q, k, v, log_f):
    b, s, h, dk = q.shape
    scale = dk ** -0.5
    nb = s // FOX_Q_BLOCK
    c = jnp.cumsum(log_f, axis=1)
    ck = c.transpose(0, 2, 1)
    kpos = jnp.arange(s)
    q_blocks = q.reshape(b, nb, FOX_Q_BLOCK, h, dk).swapaxes(0, 1)
    c_blocks = c.reshape(b, nb, FOX_Q_BLOCK, h).swapaxes(0, 1)
    t0s = jnp.arange(nb, dtype=jnp.int32) * FOX_Q_BLOCK

    def block(args):
        qb, cb, t0 = args
        tq = t0 + jnp.arange(FOX_Q_BLOCK)
        logits = jnp.einsum('bqhd,bkhd->bhqk', qb, k).astype(jnp.float32) * scale
        logits = logits + (cb.transpose(0, 2, 1)[..., None] - ck[:, :, None, :])
        p_att = masked_softmax(logits, kpos[None, :] <= tq[:, None])
        return jnp.einsum('bhqk,bkhd->bqhd', p_att.astype(v.dtype), v)

    out = lax.map(block, (q_blocks, c_blocks, t0s))
    return out.swapaxes(0, 1).reshape(b, s, h * dk)

def second_inputs(seed: int = 0) -> dict:
    key = jax.random.key(seed)
    ks = jax.random.split(key, 26)
    f32 = jnp.float32

    def nrm(k, shape, fan_in):
        return jax.random.normal(k, shape, f32) * (fan_in ** -0.5)

    def gain(k, shape):
        return 1.0 + 0.05 * jax.random.normal(k, shape, f32)

    def small(k, shape):
        return 0.02 * jax.random.normal(k, shape, f32)

    x = jax.random.normal(ks[0], (BATCH, SEQ, D_MODEL), f32)
    p = jax.random.normal(ks[1], (DEPTH, BATCH, SEQ, PLE_DIM), f32)
    ln_gain = gain(ks[2], (DEPTH, D_MODEL))
    w_in = nrm(ks[3], (DEPTH, D_MODEL, N_IN_2), D_MODEL)
    f_off = column_offsets()['fox_f'][0]
    b_in = small(ks[4], (DEPTH, N_IN_2)).at[:, f_off:f_off + FOX_HEADS].add(FORGET_BIAS)
    conv_w = nrm(ks[5], (DEPTH, CONV_WIDTH, BRANCH_WIDTH), CONV_WIDTH)
    conv_b = small(ks[6], (DEPTH, BRANCH_WIDTH))
    lru_wa = nrm(ks[7], (DEPTH, LRU_BLOCKS, LRU_BLOCK, LRU_BLOCK), LRU_BLOCK)
    lru_ba = small(ks[8], (DEPTH, BRANCH_WIDTH))
    lru_wx = nrm(ks[9], (DEPTH, LRU_BLOCKS, LRU_BLOCK, LRU_BLOCK), LRU_BLOCK)
    lru_bx = small(ks[10], (DEPTH, BRANCH_WIDTH))
    a0 = jax.random.uniform(ks[11], (DEPTH, BRANCH_WIDTH), f32, minval=0.9, maxval=0.999)
    root = a0 ** (1.0 / LRU_C)
    lru_lambda = jnp.log(root) - jnp.log1p(-root)
    cmp_w1 = nrm(ks[12], (DEPTH, 2, CMP_BLOCK * HEAD_DIM, CMP_HIDDEN), CMP_BLOCK * HEAD_DIM)
    cmp_w2 = nrm(ks[13], (DEPTH, 2, CMP_HIDDEN, HEAD_DIM), CMP_HIDDEN)
    cmp_pos = small(ks[14], (DEPTH, 2, CMP_BLOCK, HEAD_DIM))
    nsa_q_gain = gain(ks[15], (DEPTH, HEAD_DIM))
    nsa_k_gain = gain(ks[16], (DEPTH, HEAD_DIM))
    fox_q_gain = gain(ks[17], (DEPTH, HEAD_DIM))
    fox_k_gain = gain(ks[18], (DEPTH, HEAD_DIM))
    w_branch = nrm(ks[19], (DEPTH, N_BRANCH, BRANCH_WIDTH, D_MODEL), BRANCH_WIDTH)
    w_out = nrm(ks[20], (DEPTH, D_MODEL, D_MODEL), D_MODEL)
    w_ple = nrm(ks[21], (DEPTH, PLE_DIM, D_MODEL), PLE_DIM)
    ple_gain = gain(ks[22], (DEPTH, D_MODEL))
    w_ple_gate = nrm(ks[23], (DEPTH, D_MODEL, D_MODEL), D_MODEL)
    return {'x': x, 'p': p, 'ln_gain': ln_gain, 'w_in': w_in, 'b_in': b_in,
            'conv_w': conv_w, 'conv_b': conv_b, 'lru_wa': lru_wa, 'lru_ba': lru_ba,
            'lru_wx': lru_wx, 'lru_bx': lru_bx, 'lru_lambda': lru_lambda,
            'cmp_w1': cmp_w1, 'cmp_w2': cmp_w2, 'cmp_pos': cmp_pos,
            'nsa_q_gain': nsa_q_gain, 'nsa_k_gain': nsa_k_gain,
            'fox_q_gain': fox_q_gain, 'fox_k_gain': fox_k_gain,
            'w_branch': w_branch, 'w_out': w_out, 'w_ple': w_ple,
            'ple_gain': ple_gain, 'w_ple_gate': w_ple_gate}

def second_block(x, p, ln_gain, w_in, b_in, conv_w, conv_b, lru_wa, lru_ba, lru_wx, lru_bx,
              lru_lambda, cmp_w1, cmp_w2, cmp_pos, nsa_q_gain, nsa_k_gain, fox_q_gain,
              fox_k_gain, w_branch, w_out, w_ple, ple_gain, w_ple_gate):
    b, s, _ = x.shape
    h = x
    for l in range(DEPTH):
        hn = rms_norm(h, ln_gain[l])
        z = split_columns(hn @ w_in[l] + b_in[l])
        y_a = rglru_branch(z['lru_x'], conv_w[l], conv_b[l], lru_wa[l], lru_ba[l],
                           lru_wx[l], lru_bx[l], lru_lambda[l]) * jax.nn.silu(z['lru_gate'])
        q_b = rms_norm(split_heads(z['nsa_q'], NSA_HEADS), nsa_q_gain[l])
        k_c = rms_norm(compress(split_heads(z['nsa_k_cmp'], NSA_KV_HEADS), cmp_pos[l, 0],
                                cmp_w1[l, 0], cmp_w2[l, 0]), nsa_k_gain[l])
        v_c = compress(split_heads(z['nsa_v_cmp'], NSA_KV_HEADS), cmp_pos[l, 1],
                       cmp_w1[l, 1], cmp_w2[l, 1])
        k_s = rms_norm(split_heads(z['nsa_k_slc'], NSA_KV_HEADS), nsa_k_gain[l])
        v_s = split_heads(z['nsa_v_slc'], NSA_KV_HEADS)
        k_w = rms_norm(split_heads(z['nsa_k_win'], NSA_KV_HEADS), nsa_k_gain[l])
        v_w = split_heads(z['nsa_v_win'], NSA_KV_HEADS)
        g_b = jax.nn.sigmoid(z['nsa_bgate']).reshape(b, s, NSA_HEADS, 3)
        y_b = nsa_branch(q_b, k_c, v_c, k_s, v_s, k_w, v_w, g_b) * jax.nn.silu(z['nsa_gate'])
        log_f = jax.nn.log_sigmoid(z['fox_f'].astype(jnp.float32))
        y_c = fox_branch(rms_norm(split_heads(z['fox_q'], FOX_HEADS), fox_q_gain[l]),
                         rms_norm(split_heads(z['fox_k'], FOX_HEADS), fox_k_gain[l]),
                         split_heads(z['fox_v'], FOX_HEADS), log_f) * jax.nn.silu(z['fox_gate'])
        mg = jax.nn.sigmoid(z['merge']).reshape(b, s, N_BRANCH, D_MODEL)
        merged = (mg[:, :, 0] * (y_a @ w_branch[l, 0])
                  + mg[:, :, 1] * (y_b @ w_branch[l, 1])
                  + mg[:, :, 2] * (y_c @ w_branch[l, 2]))
        h = h + merged @ w_out[l]
        e = rms_norm(p[l] @ w_ple[l], ple_gain[l])
        h = h + jax.nn.sigmoid(h @ w_ple_gate[l]) * e
    return h


def setup_inputs(seed=0):
    out = dict(first_inputs(seed))
    for name, value in second_inputs(seed + 1).items():
        if name != "x":
            out[name + "_2"] = value
    return out


def reference(
    x, c, rel_bias, norm1_w, norm2_w, w_mod, b_mod, w_in, conv_w, conv_b, dt_bias, a_log,
    d_skip, ssm_norm_w, w_attn_proj, w_ssm_proj, w_out, w_ffn_in, w_ffn_out, final_norm_w, p_2,
    ln_gain_2, w_in_2, b_in_2, conv_w_2, conv_b_2, lru_wa_2, lru_ba_2, lru_wx_2, lru_bx_2,
    lru_lambda_2, cmp_w1_2, cmp_w2_2, cmp_pos_2, nsa_q_gain_2, nsa_k_gain_2, fox_q_gain_2,
    fox_k_gain_2, w_branch_2, w_out_2, w_ple_2, ple_gain_2, w_ple_gate_2,
):
    x = first_block(
        x, c, rel_bias, norm1_w, norm2_w, w_mod, b_mod, w_in, conv_w, conv_b, dt_bias, a_log,
        d_skip, ssm_norm_w, w_attn_proj, w_ssm_proj, w_out, w_ffn_in, w_ffn_out, final_norm_w,
    )
    return second_block(
        x, p_2, ln_gain_2, w_in_2, b_in_2, conv_w_2, conv_b_2, lru_wa_2, lru_ba_2, lru_wx_2,
        lru_bx_2, lru_lambda_2, cmp_w1_2, cmp_w2_2, cmp_pos_2, nsa_q_gain_2, nsa_k_gain_2,
        fox_q_gain_2, fox_k_gain_2, w_branch_2, w_out_2, w_ple_2, ple_gain_2, w_ple_gate_2,
    )


_drawn_inputs = setup_inputs


def setup_inputs(seed=0):
    import zlib

    import numpy as np

    out = dict(_drawn_inputs(seed))
    spreads = {}
    factors = {'b_mod': 3.621,
     'conv_b': 8.0,
     'd_skip': 4.404,
     'ssm_norm_w': 3.161,
     'conv_b_2': 2.744,
     'lru_ba_2': 52.161,
     'lru_bx_2': 22.084,
     'cmp_pos_2': 8.0,
     'nsa_q_gain_2': 8.0,
     'nsa_k_gain_2': 8.0,
     'fox_q_gain_2': 8.0,
     'fox_k_gain_2': 8.0}
    for name, (base, spread) in spreads.items():
        noise = np.random.default_rng([zlib.crc32(name.encode()), seed]).standard_normal(out[name].shape)
        drawn = base * np.exp(spread * noise) if base else spread * noise
        out[name] = jnp.asarray(drawn.astype(out[name].dtype))
    for name, factor in factors.items():
        out[name] = (out[name] * factor).astype(out[name].dtype)
    return out
```

```python
from contextlib import ExitStack

import numpy as np
import concourse.bass as bass
from concourse import mybir

F32 = mybir.dt.float32
F32R = mybir.dt.float32r
ALU = mybir.AluOpType
ACT = mybir.ActivationFunctionType
AX = mybir.AxisListType

P = 128
S = 256
D = 2048
DT = D // P
EPS = 1e-6
NEG = -1e30
ATT_SCALE = float(128) ** -0.5
FF_T = 5632 // P
SG = 8
LRU_T = 8

PHASES = [
    ("qkv", 36, 36), ("dt", 1, 1),
    ("ssm0", 40, 40), ("sp0", 16, 16), ("ssm1", 40, 40), ("sp1", 16, 16),
    ("ap", 4, 8), ("gs", 16, 16), ("ga", 16, 16), ("wo", 16, 16),
    ("fi", 88, 88), ("fo", 64, 16),
    ("lx", 8, 8), ("lg", 8, 8), ("wba", 8, 16), ("mga", 16, 16),
    ("bf", 1, 1), ("nq", 20, 20), ("cmp", 8, 4), ("ng", 8, 8), ("wbb", 8, 16), ("mgb", 16, 16),
    ("fx", 24, 24), ("fg", 8, 8), ("wbc", 8, 16), ("mgc", 16, 16),
    ("w2", 16, 16), ("ple", 2, 8), ("pg", 16, 16),
]
C0, E0 = {}, {}
_c = _e = 0
for _n, _k, _r in PHASES:
    C0[_n], E0[_n] = _c, _e
    _c, _e = _c + _k, _e + _r
CHUNKS = _c
KFO = 11
NFO = 64

CST = [
    ("c", 16), ("bmod", 96), ("n1", 16), ("n2", 16), ("fin", 16), ("cw", 48 * 4), ("cb", 48),
    ("dtb", 1), ("alog", 1), ("dsk", 32), ("ssmn", 32), ("rel", 12),
    ("b2", 125), ("cw2", 32), ("cb2", 8), ("ba", 8), ("bx", 8), ("lam", 8), ("pos", 64),
    ("gnq", 1), ("gnk", 1), ("gfq", 1), ("gfk", 1), ("ln2", 16), ("pleg", 16),
    ("ident", 128), ("tri", 256), ("tri01", 128), ("cmask", 60),
]
CO = {}
_o = 0
for _n, _k in CST:
    CO[_n] = _o
    _o += _k
NCST = _o


class At:

    def __init__(self, base, *terms):
        self.base, self.terms = base, terms

    def __add__(self, n):
        return At(self.base + n, *self.terms)

    def slot(self, n):
        return self.base % n

    def times(self, k, add=0):
        v = self.base * k + add
        for reg, stride in self.terms:
            v = reg * (stride * k) + v
        return v

    def round(self, n, k, add=0):
        v = (self.base // n) * k + add
        for reg, stride in self.terms:
            v = reg * (stride // n * k) + v
        return v


def at(base, i, stride):
    return At(base + i * stride) if isinstance(i, int) else At(base, (i, stride))


def one(i):
    return slice(i, i + 1) if isinstance(i, int) else bass.ds(i, 1)


def span(i, n):
    return slice(i, i + n) if isinstance(i, int) else bass.ds(i, n)


def wide(i, n):
    return slice(i * n, i * n + n) if isinstance(i, int) else bass.ds(i * n, n)


def first_and_second_block(nc, w16, w11, wm, cst_d, onehot, xt, pt, wab, cw2, out):
    ctx = ExitStack()
    with ctx:
        BASE = 16512
        CSTB = BASE + 98304
        W = CSTB + 9216

        def sb(name, shape, offset, dt=F32):
            return nc.alloc_sbuf_tensor_at(name, shape, dt, offset=offset)

        def sem(name):
            return ctx.enter_context(nc.semaphore(name))

        raw = sb("raw", [P, 4, 16, P], BASE)
        whi = sb("whi", [P, 2, 16, P], BASE + 32768, F32R)
        wlo = sb("wlo", [P, 2, 16, P], BASE + 49152, F32R)
        act_hi = sb("act_hi", [P, DT, S], BASE + 65536, F32R)
        act_lo = sb("act_lo", [P, DT, S], BASE + 81920, F32R)
        cst = sb("cst", [P, NCST], CSTB)
        ones = sb("ones", [P, P], CSTB + 5376)
        modT = sb("modT", [P, 96], CSTB + 5888)
        dtn = sb("dtn", [P, 2, 64], CSTB + 6272)
        acn = sb("acn", [P, 2, 64], CSTB + 6784)
        decn = sb("decn", [P, 64], CSTB + 7296)
        gain1 = sb("gain1", [P, DT], CSTB + 7552)
        gain2 = sb("gain2", [P, DT], CSTB + 7616)
        mx = sb("mx", [P, 2, 4], CSTB + 7680)
        nmx = sb("nmx", [P, 2, 4], CSTB + 7712)
        sums = sb("sums", [P, 2, 4], CSTB + 7744)
        rsum = sb("rsum", [P, 2, 4], CSTB + 7776)
        cact = sb("cact", [P, 16], CSTB + 7808)
        aneg = sb("aneg", [P, 1], CSTB + 7872)
        nudge = sb("nudge", [P, 8], CSTB + 7904)
        spl = sb("spl", [P, 8], CSTB + 7936)
        rstd = sb("rstd", [P, S], CSTB + 8192)

        def C(name, a=0, n=1):
            return cst[:, CO[name] + a:CO[name] + a + n]

        def Cd(name, a):
            return cst[:, CO[name] + a:CO[name] + a + 1] if isinstance(a, int) else cst[:, bass.ds(a + CO[name], 1)]

        ident = C("ident", 0, 128)

        xT = sb("xT", [P, DT, S], W)
        sqT = sb("sqT", [P, DT, S], W + 16384)
        mraw = sb("mraw", [P, 2, 4, 512], W + 57344)
        macc = sb("macc", [P, 512], W + 73728)
        qkv = sb("qkv", [P, 36, S], W)
        vnat = sb("vnat", [P, 2, 12, P], W + 36864)
        att_hi = sb("att_hi", [P, 4, S], W + 49152, F32R)
        att_lo = sb("att_lo", [P, 4, S], W + 53248, F32R)
        dtr = sb("dtr", [64, S], W + 57344)
        dts = sb("dts", [64, 6, S], W + 58368)
        biasT = sb("biasT", [P, 2, 3, S], W + 75776)
        lgt = sb("lgt", [P, 2, 4, S], W + 81920)
        pT = sb("pT", [P, 2, 8, P], W + 90112)
        ovec = sb("ovec", [P, 2, P], W + 64512)
        brow = sb("brow", [4, 3, 512], W + 98304)
        oneh = sb("oneh", [33, 3, 512], W + 81920)
        y_hi = sb("y_hi", [P, 16, S], W, F32R)
        y_lo = sb("y_lo", [P, 16, S], W + 16384, F32R)
        accS = sb("accS", [P, DT, S], W + 32768)
        Z = W + 57344
        ub = sb("ub", [P, 2, 259], Z)
        cv = sb("cv", [P, 2, S], Z + 2080)
        bct = sb("bct", [P, 2, 2, S], Z + 4128)
        xs = sb("xs", [P, 2, 4, S], Z + 8224)
        sz = sb("sz", [P, 4, S], Z + 16416)
        acb = sb("acb", [P, 8, 2, P], Z + 20512)
        dec = sb("dec", [P, 8, 2, P], Z + 28704)
        xdt = sb("xdt", [P, 2, 512], Z + 36896)
        xdd = sb("xdd", [P, 512], Z + 40992)
        st0 = sb("st0", [P, 512], Z + 43040)
        cbm = sb("cbm", [P, 2, P], Z + 45088)
        bnat = sb("bnat", [P, P], Z + 46112)
        sq = sb("sq", [P, S], Z + 46624)
        accA = sb("accA", [P, DT, S], W + 16384)
        mg_hi = sb("mg_hi", [P, DT, S], W, F32R)
        mg_lo = sb("mg_lo", [P, DT, S], W + 75776, F32R)
        tm = sb("tm", [P, 4, S], W + 92160)
        t2 = sb("t2", [P, 2, S], W + 96256)
        x1 = sb("x1", [P, DT, S], W + 32768)
        xq = sb("xq", [P, DT, S], W)
        sq1 = sb("sq1", [P, DT, S], W + 16384)
        hid_hi = sb("hid_hi", [P, FF_T, S], W, F32R)
        hid_lo = sb("hid_lo", [P, FF_T, S], W + 45056, F32R)
        tf = sb("tf", [P, 4, S], W + 90112)
        hf = sb("hf", [P, 2, S], W + 94208)
        x1r = sb("x1r", [P, DT, S], BASE + 65536)

        x2T = sb("x2T", [P, DT, S], W)
        accM = sb("accM", [P, DT, S], W + 16384)
        sqF = sb("sqF", [P, DT, S], W + 49152)
        yb_hi = sb("yb_hi", [P, 8, S], W + 32768, F32R)
        yb_lo = sb("yb_lo", [P, 8, S], W + 40960, F32R)
        R2 = W + 49152
        proj = sb("proj", [P, DT, S], R2)
        tm2 = sb("tm2", [P, 4, S], W + 98304)
        t3 = sb("t3", [P, 2, S], W + 102400)
        uc = sb("uc", [P, 8, S], R2)
        gl = sb("gl", [P, 4, S], R2 + 8192)
        lr, li, lt, la, lw = (sb(n, [P, 4, S], R2 + 12288 + 4096 * k) for k, n in enumerate(("lr", "li", "lt", "la", "lw")))
        wabs = sb("wabs", [P, 4, 2, P], R2 + 32768)
        ub2 = sb("ub2", [P, 2, 259], R2 + 36864)
        lcon = sb("lcon", [P, 6, 8], R2 + 38976)
        zf = sb("zf", [P, S], CSTB + 6272)
        gn = sb("gn", [P, 2, 24], CSTB + 7296)
        cn = sb("cn", [P, 2, 8], CSTB + 7488)
        sft = sb("sft", [P, 5, S], W + 32768)
        nk = sb("nk", [P, 20, S], R2)
        kp = sb("kp", [P, 2, 32, 30], R2 + 20480)
        kp_hi = sb("kp_hi", [P, 2, 32, 30], R2 + 28160, F32R)
        kp_lo = sb("kp_lo", [P, 2, 32, 30], R2 + 35840, F32R)
        cw2s = sb("cw2s", [P, 2, 2, P], R2 + 43520)
        hc = sb("hc", [P, 2, 2, 30], R2 + 45568)
        vcn = sb("vcn", [15, 2, P], R2 + 46080)
        kcT = sb("kcT", [P, 30], R2 + 47104)
        kcs = sb("kcs", [P, 5, 30], R2 + 47232)
        hq_ = sb("hsq", [P, 2, 512], W + 32768)
        hr_, hv_, ht_, he_ = (sb(n, [P, 512], W + 36864 + 2048 * k) for k, n in enumerate(("hroot", "hval", "htmp", "hrec")))
        lg2 = sb("lg2", [P, 2, 4, S], R2 + 20480)
        pT2 = sb("pT2", [P, 2, 8, P], R2 + 28672)
        vn2 = sb("vn2", [P, 2, 4, P], R2 + 36864)
        fx = sb("fx", [P, 24, S], R2)
        vn3 = sb("vn3", [P, 2, 8, P], R2 + 24576)
        lg3 = sb("lg3", [P, 2, 4, S], R2 + 32768)
        pT3 = sb("pT3", [P, 2, 8, P], R2 + 40960)
        m2_hi = sb("m2_hi", [P, DT, S], W + 65536, F32R)
        m2_lo = sb("m2_lo", [P, DT, S], W + 81920, F32R)
        eT = sb("eT", [P, DT, S], W + 16384)
        p_in = sb("p_in", [P, 2, S], W + 32768)
        p_hi = sb("p_hi", [P, 2, S], W + 34816, F32R)
        p_lo = sb("p_lo", [P, 2, S], W + 36864, F32R)

        accp = ctx.enter_context(nc.psum_tensor("accp", [P, 2, 512], F32))
        pw = ctx.enter_context(nc.psum_tensor("pw", [P, 6, 512], F32))

        x1_d = nc.dram_tensor("x1_d", [P, DT * S], F32, kind="Internal").ap()
        ac_d = nc.dram_tensor("ac_d", [SG, 8 * S], F32, kind="Internal").ap()
        br_d = nc.dram_tensor("br_d", [4, 3 * 512], F32, kind="Internal").ap()
        bw_d = nc.dram_tensor("bw_d", [4, P, 3 * 512], F32, kind="Internal").ap()

        raw_in = [sem(f"raw_in{i}") for i in range(4)]
        hi_done = sem("hi_done")
        lo_a = sem("lo_a")
        lo_b = sem("lo_b")
        used = sem("used")
        evac = sem("evac")
        post = sem("post")
        cst_in = sem("cst_in")
        x_in = sem("x_in")
        ones_ok = sem("ones_ok")
        mod_in = [sem("mod_in0"), sem("mod_in1")]
        mod_used = sem("mod_used")
        cact_ok = sem("cact_ok")
        macc_ok = sem("macc_ok")
        mod_mm = sem("mod_mm")
        mod_ok = sem("mod_ok")
        rq, rm, rv, rs = sem("rms_squares"), sem("rms_sum"), sem("rms_recip"), sem("rms_root")
        acts_ok = sem("acts_ok")
        spx, spe = sem("sp_abs"), sem("sp_exp")
        tp_mm, tp_ev = sem("tp_mm"), sem("tp_ev")
        aL, aA, aX, aB, aT, aC, aO, aF = (sem("att_" + n) for n in (
            "logits", "biased", "exp", "scaled", "turned", "copied", "out", "moved"))
        brow_mm, brow_ev, brow_st = sem("brow_mm"), sem("brow_ev"), sem("brow_st")
        oneh_in = sem("oneh_in")
        bias_in = [sem("bias_in0"), sem("bias_in1")]
        ac_ok, ac_st, acb_in = sem("ac_ok"), sem("ac_st"), sem("acb_in")
        dt_mm, dt_ev, dt_ex = sem("dt_mm"), sem("dt_ev"), sem("dt_ex")
        conv_d, silu_d = sem("conv_done"), sem("silu_done")
        dec_in, dec_ex = sem("dec_ready"), sem("dec_exp")
        cb_mm, cb_ev = sem("cb_mm"), sem("cb_ev")
        m_ok, ce_ok = sem("m_ok"), sem("ce_ok")
        xt_mm, xt_ev = sem("xt_mm"), sem("xt_ev")
        xdd_ok, s0_mm, s0_ev = sem("xdd_ok"), sem("s0_mm"), sem("s0_ev")
        y_mm, y_ev, sq_ok = sem("y_mm"), sem("y_ev"), sem("sq_ok")
        ssq_mm, ssq_v, ssq_r, grp = sem("ssq_mm"), sem("ssq_v"), sem("ssq_r"), sem("grp_done")
        x1_st, x1_in = sem("x1_st"), sem("x1_in")
        pad_ok = sem("pad_ok")
        out_ok, out_st = sem("out_ok"), sem("out_st")

        uc_ok, wab_in, lru_mm, lru_g, lru_l, lru_e, lru_w, lru_q, lru_y = (sem("lru_" + n) for n in (
            "conv", "weights", "mm", "gates", "logs", "exps", "squares", "roots", "y"))
        lam_x = sem("lam")
        zf_ok, gn_mm, gn_ok = sem("zf_ok"), sem("gn_mm"), sem("gn_ok")
        kp_ok, cw2_in, kc_mm, kc_ev = sem("kp_ok"), sem("cw2_in"), sem("kc_mm"), sem("kc_ev")
        hq, hm, hv, hr = sem("head_squares"), sem("head_sum"), sem("head_recip"), sem("head_root")
        hn_ok = sem("head_normed")
        p_ok, p_land, h_ok = sem("p_ok"), sem("p_land"), sem("h_ok")
        POST0, _p = {}, 0
        for name, n in (("sp1", 16), ("gs", 16), ("ga", 16), ("wo", 16), ("fi", 88), ("fo", 16),
                        ("lx", 8), ("mga", 16), ("ng", 8), ("mgb", 16), ("fg", 8), ("mgc", 16), ("w2", 16), ("pg", 16)):
            POST0[name] = _p
            _p += n
        NMOD1 = 8
        YB = (3, 4, 0, 1)
        B2, _b = {}, 0
        for name, n in (("lx", 8), ("lg", 8), ("mga", 16), ("bf", 1), ("nq", 20), ("ng", 8), ("mgb", 16),
                        ("fx", 24), ("fg", 8), ("mgc", 16)):
            B2[name] = _b
            _b += n
        BATCH = [(kind, 4 * g, q) for g in range(2) for q in (1, 0) for kind in range(3)]
        BATCH += [(3, 4 * g, q) for g in range(2) for q in (1, 0)]
        NSA_B = 12
        CLOSED = [n for n, b in enumerate(BATCH) if b[0] >= 2]
        UNITS = [(j, q) for j in range(4) for q in (1, 0)]

        block = ctx.enter_context(nc.Block())

        @block.sync
        def _(sp):
            sp.dma_start(cst[:, :], cst_d).then_inc(cst_in, 16)
            sp.dma_start(xT[:, :, :], xt).then_inc(x_in, 16)

            def piece(b, j, free=True):
                if free:
                    sp.wait_ge(mod_used, (b * 4 + (j - 1)))
                sp.dma_start(mraw[:, j % 2], wm[one(b), j].rearrange("a p k n -> p (a k) n")).then_inc(mod_in[j % 2], 16)

            def load(c, src, k=16, free=True):
                if free:
                    sp.wait_ge(lo_a, c.times(1, -3))
                    sp.wait_ge(lo_b, c.times(1, -3))
                sp.dma_start(raw[:, c.slot(4), 0:k, :], src.rearrange("a p k n -> p (a k) n")).then_inc(raw_in[c.slot(4)], 16)

            for j in range(4):
                piece(0, j, free=j >= 2)
            with sp.Fori(1, NMOD1) as b:
                for j in range(4):
                    piece(b, j)
            for j in range(4):
                load(At(j), w16[j:j + 1], free=False)

            def riding(i0, i1, c0, b0):
                with sp.Fori(i0, i1) as i:
                    for j in range(4):
                        load(at(c0 + j, i, 4), w16[one(i * 4 + (c0 + j))])
                        piece(i + b0, j)

            def plain(a, b, arr=None, off=0, k=16):
                arr = w16 if arr is None else arr
                n = (b - a) // 4
                if n > 0:
                    with sp.Fori(0, n) as i:
                        for j in range(4):
                            load(at(a + j, i, 4), arr[one(i * 4 + (a + j - off))], k)
                for c in range(a + 4 * n, b):
                    load(At(c), arr[c - off:c - off + 1], k)

            riding(0, 8, 4, NMOD1)
            plain(36, C0["gs"])
            riding(0, 8, C0["gs"], 16)
            plain(C0["wo"], C0["fo"])
            plain(C0["fo"], C0["fo"] + NFO, w11, C0["fo"], KFO)
            plain(C0["lx"], CHUNKS, w16, NFO)
            sp.wait_ge(out_ok, 1)
            sp.dma_start(out, x2T[:, :, :].rearrange("p k n -> p (k n)")).then_inc(out_st, 16)
            sp.wait_ge(out_st, 16)

        NRUN = CHUNKS

        @block.gpsimd
        def _(pool):
            def lo(c):
                pool.wait_ge(hi_done, c.times(2, 1))
                nc.gpsimd.tensor_tensor(wlo[:, c.slot(2), 0:8, :], raw[:, c.slot(4), 0:8, :],
                                        whi[:, c.slot(2), 0:8, :].bitcast(F32), ALU.subtract).then_inc(lo_a, 1)

            with pool.Fori(0, NRUN // 4) as i:
                for j in range(4):
                    lo(at(j, i, 4))
            for c in range(NRUN // 4 * 4, NRUN):
                lo(At(c))

        @block.tensor
        def _(pe):
            def chunk(c, e, rhs, nk=16, start=True, stop=True, n=S):
                if start and (e.terms or e.base >= 2):
                    pe.wait_ge(evac, e.times(1, -1))
                acc = accp[:, e.slot(2), 0:n]
                for h in range(2):
                    pe.wait_ge(lo_b if h else lo_a, c.times(1, 1))
                    for k in range(8 * h, min(nk, 8 * h + 8)):
                        xh, xl = rhs(k)
                        wh, wl = whi[:, c.slot(2), k, :], wlo[:, c.slot(2), k, :]
                        first = start and k == 0
                        last = stop and k == nk - 1
                        pe.matmul(acc, wh, xh, start=first, stop=False)
                        pe.matmul(acc, wh, xl, start=False, stop=False)
                        mm = pe.matmul(acc, wl, xh, start=False, stop=last)
                    mm.then_inc(used, 1)

            def acts(k):
                return act_hi[:, k, :], act_lo[:, k, :]

            def mod_block():
                for j in range(4):
                    mm = pe.matmul(pw[:, 5, j:j + 1], macc[:, j * P:(j + 1) * P], ones[:, 0:1], start=True, stop=True)
                mm.then_inc(mod_mm, 1)

            def rms(n, src):
                pe.wait_ge(rq, n)
                for k in range(DT):
                    mm = pe.matmul(pw[:, 4, 0:S], ones[:, :], src[:, k, :], start=k == 0, stop=k == DT - 1)
                mm.then_inc(rm, 1)

            pe.wait_ge(ones_ok, 1)
            rms(1, sqT)
            with pe.Fori(0, NMOD1) as b:
                pe.wait_ge(macc_ok, b + 1)
                mod_block()
            pe.wait_ge(acts_ok, 1)

            def qkv_part(i, ride):
                for j in range(4):
                    chunk(at(j, i, 4), at(j, i, 4), acts)
                if ride:
                    pe.wait_ge(macc_ok, i + (NMOD1 + 1))
                    mod_block()

            qkv_part(0, True)
            with pe.Fori(1, 8) as i:
                qkv_part(i, True)
            qkv_part(8, False)
            chunk(At(36), At(36), acts)

            pe.wait_ge(oneh_in, 16)
            pe.wait_ge(mod_ok, 16)
            for g in range(3):
                mm = pe.matmul(pw[0:4, g, :], C("rel", 4 * g, 4)[0:33, :], oneh[0:33, g, :], start=True, stop=True)
            mm.then_inc(brow_mm, 1)
            pe.wait_ge(evac, 36)
            for n in range(6):
                if n >= 2:
                    pe.wait_ge(tp_ev, n - 1)
                for m in range(2):
                    for t in range(2):
                        mm = pe.transpose(pw[:, 4 + n % 2, (2 * m + t) * P:(2 * m + t + 1) * P],
                                          qkv[:, 24 + 2 * n + m, t * P:(t + 1) * P], ident)
                mm.then_inc(tp_mm, 1)

            def logits(u):
                j, q = UNITS[u]
                nk = P * (q + 1)
                if u == 0:
                    pe.wait_ge(brow_ev, 1)
                else:
                    pe.wait_ge(aA, u)
                flat = pw[:, 0:2, :].rearrange("p b n -> p (b n)")
                for g in range(3):
                    mm = pe.matmul(flat[:, g * S:g * S + nk], qkv[:, 4 * g + j, q * P:(q + 1) * P],
                                   qkv[:, 12 + 4 * g + j, 0:nk], start=True, stop=True)
                mm.then_inc(aL, 1)

            def turn(u):
                j, q = UNITS[u]
                pe.wait_ge(aB, u + 1)
                if u:
                    pe.wait_ge(aC, u)
                flat = pw[:, 2:4, :].rearrange("p b n -> p (b n)")
                for g in range(3):
                    for t in range(q + 1):
                        mm = pe.transpose(flat[:, (2 * g + t) * P:(2 * g + t + 1) * P],
                                          lgt[:, u % 2, g, t * P:(t + 1) * P], ident)
                mm.then_inc(aT, 1)

            def values(u):
                j, q = UNITS[u]
                pe.wait_ge(aC, u + 1)
                if u:
                    pe.wait_ge(aF, u)
                else:
                    pe.wait_ge(tp_ev, 6)
                n = 0
                for g in range(3):
                    for t in range(q + 1):
                        n += 1
                        mm = pe.matmul(pw[:, 4, 0:P], vnat[:, t, 4 * g + j, :], pT[:, u % 2, 2 * g + t, :],
                                       start=n == 1, stop=n == 3 * (q + 1))
                mm.then_inc(aO, 1)

            logits(0)
            for u in range(8):
                if u + 1 < 8:
                    logits(u + 1)
                if u:
                    values(u - 1)
                turn(u)
            values(7)
            pe.wait_ge(dt_ex, 1)
            pe.wait_ge(aA, 8)
            for t in range(2):
                pe.transpose(pw[:, 0, 64 * t:64 * t + 64], dts[:, 0, t * P:(t + 1) * P], ident[0:64, 0:64])
                pe.transpose(pw[:, 0, 128 + 64 * t:192 + 64 * t], dts[:, 1, t * P:(t + 1) * P], ident[0:64, 0:64])
            pe.transpose(pw[:, 0, 256:320], dts[:, 2, 0:P], ident[0:64, 0:64]).then_inc(dt_mm, 1)

            def group(i, h, gg):
                g = at(4 * h + gg, i, 2)
                ph = f"ssm{h}"
                bc, x = bct[:, gg], xs[:, gg]
                for j in range(10):
                    chunk(at(C0[ph] + 10 * gg + j, i, 20), at(E0[ph] + 10 * gg + j, i, 20), acts)
                    if j == 2:
                        pe.wait_ge(silu_d, g.times(6, 2 + 2))
                        pe.wait_ge(cb_ev, g.times(1, 1))
                        pe.wait_ge(y_ev, g.times(4, 1))
                        for t in range(2):
                            pe.matmul(pw[:, 0, t * P:(t + 1) * P], bc[:, 0, t * P:(t + 1) * P],
                                      bc[:, 1, t * P:(t + 1) * P], start=True, stop=True)
                        pe.transpose(pw[:, 0, 256:384], bc[:, 0, 0:P], ident).then_inc(cb_mm, 1)
                    if 4 <= j < 8:
                        t = j - 4
                        pe.wait_ge(silu_d, g.times(6, 2 + 3 + t))
                        pe.wait_ge(xt_ev, g.times(4, t + 1))
                        for q in range(2):
                            mm = pe.transpose(pw[:, 5 if t % 2 else 1, q * P:(q + 1) * P],
                                              x[:, t, q * P:(q + 1) * P], ident)
                        mm.then_inc(xt_mm, 1)
                    if j == 8:
                        pe.wait_ge(xdd_ok, g.times(1, 1))
                        pe.wait_ge(s0_ev, g.times(1, 1))
                        pe.matmul(pw[:, 2, :], bnat[:, :], xdd[:, :], start=True, stop=True).then_inc(s0_mm, 1)
                pe.wait_ge(m_ok, g.times(1, 1))
                pe.wait_ge(ce_ok, g.times(1, 1))
                pe.wait_ge(s0_ev, g.times(1, 2))
                pe.wait_ge(y_ev, g.times(4, 1))
                for t in range(4):
                    for r in range(2):
                        hh = 2 * t + r
                        o = pw[64 * r:64 * r + 64, YB[t], 0:S]
                        hc = slice(hh * 64, hh * 64 + 64)
                        pe.matmul(o[:, 0:P], xdt[:, 0, hc], dec[:, hh, 0, :], start=True, stop=True)
                        pe.matmul(o[:, P:S], xdt[:, 1, hc], dec[:, hh, 1, :], start=True, stop=False)
                        mm = pe.matmul(o[:, P:S], st0[:, hc], acb[:, hh, 1, :], start=False, stop=True)
                    mm.then_inc(y_mm, 1)
                for t in range(4):
                    pe.wait_ge(sq_ok, g.times(4, t + 1))
                    pe.matmul(pw[:, 5, 0:S], ones[:, :], sq[:, :], start=t == 0, stop=t == 3).then_inc(ssq_mm, 1)

            def ys(k):
                return y_hi[:, k, :], y_lo[:, k, :]

            for h in range(2):
                with pe.Fori(0, 2) as i:
                    group(i, h, 0)
                    group(i, h, 1)
                pe.wait_ge(grp, 4 * h + 5)
                with pe.Fori(0, 4) as i:
                    for j in range(4):
                        chunk(at(C0[f"sp{h}"] + j, i, 4), at(E0[f"sp{h}"] + j, i, 4), ys)

            for c in range(4):
                for h in range(2):
                    e = E0["ap"] + 2 * c + h
                    pe.wait_ge(evac, e - 1)
                    pe.wait_ge(lo_b if h else lo_a, C0["ap"] + c + 1)
                    for m in range(2):
                        for k in range(4):
                            kk, s2 = 8 * h + 4 * m + k, (C0["ap"] + c) % 2
                            acc = accp[:, e % 2, m * S:(m + 1) * S]
                            pe.matmul(acc, whi[:, s2, kk, :], att_hi[:, k, :], start=k == 0, stop=False)
                            pe.matmul(acc, whi[:, s2, kk, :], att_lo[:, k, :], start=False, stop=False)
                            mm = pe.matmul(acc, wlo[:, s2, kk, :], att_hi[:, k, :], start=False, stop=k == 3)
                    mm.then_inc(used, 1)
            for n, ph in enumerate(("gs", "ga")):
                with pe.Fori(0, 4) as i:
                    for j in range(4):
                        chunk(at(C0[ph] + j, i, 4), at(E0[ph] + j, i, 4), acts)
                    pe.wait_ge(macc_ok, i + (16 + 4 * n + 1))
                    mod_block()
            pe.wait_ge(acts_ok, 2)
            with pe.Fori(0, 4) as i:
                for j in range(4):
                    chunk(at(C0["wo"] + j, i, 4), at(E0["wo"] + j, i, 4), lambda k: (mg_hi[:, k, :], mg_lo[:, k, :]))
            rms(2, sq1)
            pe.wait_ge(acts_ok, 3)
            with pe.Fori(0, FF_T // 2) as i:
                for j in range(4):
                    chunk(at(C0["fi"] + j, i, 4), at(E0["fi"] + j, i, 4), acts)
            pe.wait_ge(acts_ok, 4)
            with pe.Fori(0, 8) as i:
                for m in range(2):
                    for q in range(4):
                        chunk(at(C0["fo"] + 4 * m + q, i, 8), at(E0["fo"] + m, i, 2),
                              lambda k, q=q: (hid_hi[:, KFO * q + k, :], hid_lo[:, KFO * q + k, :]),
                              nk=KFO, start=q == 0, stop=q == 3)


            rms(3, sqF)
            rms(4, sqF)
            pe.wait_ge(acts_ok, 6)

            def loop4(ph, n, rhs=acts):
                with pe.Fori(0, n) as i:
                    for j in range(4):
                        chunk(at(C0[ph] + j, i, 4), at(E0[ph] + j, i, 4), rhs)

            def halves(c, e, rhs, kts, ms=1):
                for h in range(2):
                    pe.wait_ge(lo_b if h else lo_a, c.times(1, 1))
                    n = 8 // kts // ms
                    for r in range(n):
                        eh = e + (h * n + r)
                        pe.wait_ge(evac, eh.times(1, -1))
                        for m in range(ms):
                            for k in range(kts):
                                kk = 8 * h + (r * ms + m) * kts + k
                                xh, xl = rhs(k)
                                acc = accp[:, eh.slot(2), m * S:(m + 1) * S]
                                pe.matmul(acc, whi[:, c.slot(2), kk, :], xh, start=k == 0, stop=False)
                                pe.matmul(acc, whi[:, c.slot(2), kk, :], xl, start=False, stop=False)
                                mm = pe.matmul(acc, wlo[:, c.slot(2), kk, :], xh, start=False, stop=k == kts - 1)
                    mm.then_inc(used, 1)

            def branch(ph, n):
                pe.wait_ge(acts_ok, n)
                with pe.Fori(0, 2) as i:
                    for j in range(4):
                        halves(at(C0["wb" + ph] + j, i, 4), at(E0["wb" + ph] + 2 * j, i, 8),
                               lambda k: (yb_hi[:, k, :], yb_lo[:, k, :]), 8)
                loop4("mg" + ph, 4)

            loop4("lx", 2)
            for i in range(2):
                pe.wait_ge(uc_ok, 1)
                pe.wait_ge(wab_in, 16 * (i + 1))
                if i:
                    pe.wait_ge(lru_g, i)
                for t in range(4):
                    for w in range(2):
                        mm = pe.matmul(pw[:, t, w * S:(w + 1) * S], wabs[:, t, w, :], uc[:, 4 * i + t, :], start=True, stop=True)
                mm.then_inc(lru_mm, 1)
                for j in range(4):
                    chunk(At(C0["lg"] + 4 * i + j), At(E0["lg"] + 4 * i + j), acts)
            branch("a", 7)
            chunk(At(C0["bf"]), At(E0["bf"]), acts)
            pe.wait_ge(zf_ok, 2)
            for t in range(2):
                mm = pe.transpose(pw[:, 5, t * P:(t + 1) * P], zf[:, t * P:(t + 1) * P], ident)
            mm.then_inc(gn_mm, 1)
            loop4("nq", 5)

            def head_sum(n, cols=512):
                pe.wait_ge(hq, n + 1)
                if n:
                    pe.wait_ge(hv, n)
                else:
                    pe.wait_ge(gn_ok, 1)
                src = hq_[:, n % 2, :] if cols == 512 else kcs[:, 0, :]
                pe.matmul(pw[:, 5, 0:cols], ones[:, :], src, start=True, stop=True).then_inc(hm, 1)

            def transposes(srcs, n0):
                for n in range(len(srcs) // 2):
                    if n0 + n >= 2:
                        pe.wait_ge(tp_ev, n0 + n - 1)
                    for m in range(2):
                        for t in range(2):
                            mm = pe.transpose(pw[:, 2 + (n0 + n) % 2, (2 * m + t) * P:(2 * m + t + 1) * P],
                                              srcs[2 * n + m][:, t * P:(t + 1) * P], ident)
                    mm.then_inc(tp_mm, 1)

            pe.wait_ge(kp_ok, 1)
            for j in range(8):
                x, m = j // 4, j // 2 % 2
                chunk(At(C0["cmp"] + j), At(E0["cmp"] + j // 2),
                      lambda k: (kp_hi[:, x, 16 * (j % 2) + k, :], kp_lo[:, x, 16 * (j % 2) + k, :]),
                      start=j % 2 == 0, stop=j % 2 == 1, n=30)
                if j < 6:
                    head_sum(j)
            pe.wait_ge(cw2_in, 16)
            pe.wait_ge(evac, E0["cmp"] + 4)
            for m in range(2):
                pe.matmul(pw[:, 0, 0:30], cw2s[:, 0, m, :], hc[:, 0, m, :], start=m == 0, stop=m == 1)
            for x in range(2):
                for m in range(2):
                    mm = pe.matmul(pw[0:15, 1, x * P:(x + 1) * P], hc[:, 1, m, 15 * x:15 * x + 15], cw2s[:, 1, m, :], start=m == 0, stop=m == 1)
            mm.then_inc(kc_mm, 1)
            transposes([nk[:, n, :] for n in (14, 15, 18, 19)], 6)
            head_sum(6, 30)

            def att_logits(b):
                kind, h0, q = BATCH[b]
                n = P * (q + 1) if kind else 15
                if b in (0, NSA_B):
                    pe.wait_ge(hn_ok, 7 if b == 0 else 15)
                    pe.wait_ge(tp_ev, 8 if b == 0 else 12)
                if b:
                    pe.wait_ge(aA, 8 + b)
                for r in range(4):
                    h = h0 + r
                    kv = h0 // 4
                    o = pw[:, r // 2, (r % 2) * S:(r % 2) * S + n]
                    qq = (fx if kind == 3 else nk)[:, h, q * P:(q + 1) * P]
                    kk = (kcT[:, 15 * kv:15 * kv + 15], nk[:, 12 + kv, 0:n], nk[:, 16 + kv, 0:n], fx[:, 8 + h, 0:n])[kind]
                    mm = pe.matmul(o, qq, kk, start=True, stop=kind != 3)
                    if kind == 3:
                        mm = pe.matmul(o, nudge[:, h:h + 1].to_broadcast([P, P]), zf[:, 0:n], start=False, stop=True)
                mm.then_inc(aL, 1)

            def att_turn(b):
                kind, h0, q = BATCH[b]
                pe.wait_ge(aB, 8 + b + 1)
                pe.wait_ge(aC, 8 + b)
                src = (lg3 if kind == 3 else lg2)[:, b % 2]
                for r in range(4):
                    for t in range(q + 1 if kind else 1):
                        rows, n = (P, P) if kind else (15, 15)
                        mm = pe.transpose(pw[0:rows, 2 + r // 2, (2 * (r % 2) + t) * P:(2 * (r % 2) + t + 1) * P],
                                          src[:, r, t * P:t * P + n], ident)
                mm.then_inc(aT, 1)

            def att_values(b):
                kind, h0, q = BATCH[b]
                kv = h0 // 4
                pe.wait_ge(aC, 8 + b + 1)
                opens = kind in (0, 3)
                if opens:
                    pe.wait_ge(aF, 8 + sum(x < b for x in CLOSED))
                for r in range(4):
                    o = pw[:, 4, r * P:(r + 1) * P]
                    ts = range(q + 1 if kind else 1)
                    for t in ts:
                        if kind == 0:
                            l, x = vcn[0:15, kv, :], pT2[0:15, b % 2, 2 * r, :]
                        elif kind == 3:
                            l, x = vn3[:, t, h0 + r, :], pT3[:, b % 2, 2 * r + t, :]
                        else:
                            l, x = vn2[:, t, 2 * (kind - 1) + kv, :], pT2[:, b % 2, 2 * r + t, :]
                        mm = pe.matmul(o, l, x, start=opens and r == 0 and t == 0,
                                       stop=kind >= 2 and t == q and r == 3, skip_group_check=True)
                mm.then_inc(aO, 1)

            def attention(b0, b1):
                att_logits(b0)
                for b in range(b0, b1):
                    if b + 1 < b1:
                        att_logits(b + 1)
                    if b > b0:
                        att_values(b - 1)
                    att_turn(b)
                att_values(b1 - 1)

            attention(0, NSA_B)
            loop4("ng", 2)
            branch("b", 8)
            loop4("fx", 6)
            transposes([fx[:, 16 + n, :] for n in range(8)], 8)
            for n in range(8):
                head_sum(7 + n)
            attention(NSA_B, len(BATCH))
            loop4("fg", 2)
            branch("c", 9)
            pe.wait_ge(acts_ok, 10)
            loop4("w2", 4, lambda k: (m2_hi[:, k, :], m2_lo[:, k, :]))
            pe.wait_ge(p_ok, 1)
            for c in range(2):
                halves(At(C0["ple"] + c), At(E0["ple"] + 4 * c), lambda k: (p_hi[:, k, :], p_lo[:, k, :]), 2, ms=2)
            pe.wait_ge(h_ok, 1)
            rms(5, sqF)
            loop4("pg", 4)

        @block.scalar
        def _(act):
            def split_hi(c):
                if not c.terms and c.base >= NRUN:
                    return
                act.wait_ge(raw_in[c.slot(4)], c.round(4, 16, 16))
                for h in range(2):
                    if c.terms or c.base >= 2:
                        act.wait_ge(used, c.times(2, h - 3))
                    act.activation(whi[:, c.slot(2), 8 * h:8 * h + 8, :], raw[:, c.slot(4), 8 * h:8 * h + 8, :],
                                   ACT.Copy).then_inc(hi_done, 1)

            def take(c, e, out, func=ACT.Copy, n=S, rows=P, **kw):
                act.wait_ge(used, c.times(2, 2))
                act.activation(out, accp[0:rows, e.slot(2), 0:n], func, **kw).then_inc(evac, 1)

            def root(n, o, v):
                act.wait_ge(rv, n)
                act.activation(o, v, ACT.Sqrt).then_inc(rs, 1)

            act.wait_ge(cst_in, 16)
            act.activation(cact[:, :], C("c", 0, 16), ACT.Silu).then_inc(cact_ok, 1)
            act.wait_ge(x_in, 16)
            act.activation(sqT[:, :, :], xT[:, :, :], ACT.Square).then_inc(rq, 1)
            for n in range(2):
                act.activation(nudge[:, n:n + 1], C("c", n, 1), ACT.Copy).then_inc(silu_d, 1)
            act.activation(nudge[:, 2:3], C("c"), ACT.Copy).then_inc(s0_ev, 1)
            root(1, rstd[:, :], sqT[:, 0, :])
            split_hi(At(0))

            def qkv_part(i):
                for j in range(4):
                    c = at(j, i, 4)
                    split_hi(c + 1)
                    take(c, c, qkv[:, one(i * 4 + j), :])

            qkv_part(0)
            with act.Fori(1, 9) as i:
                qkv_part(i)
            act.dma_start(oneh[:, :, :], onehot).then_inc(oneh_in, 16)
            split_hi(At(37))
            act.wait_ge(mod_used, 64)
            take(At(36), At(36), dtr[:, :], ACT.Identity, rows=64, bias=C("dtb")[0:64, :])
            act.wait_ge(spx, 1)
            act.activation(dts[:, 2, :], dts[:, 1, :], ACT.Exp, scale=-1.0).then_inc(spe, 1)
            act.activation(aneg[0:64, :], C("alog")[0:64, :], ACT.Exp).then_inc(spe, 1)
            act.wait_ge(brow_mm, 1)
            for g in range(3):
                ins = act.activation(brow[:, g, :], pw[0:4, g, :], ACT.Copy)
            ins.then_inc(brow_ev, 1)
            act.wait_ge(brow_ev, 1)
            act.dma_start(br_d, brow[:, :, :].rearrange("j g n -> j (g n)")).then_inc(brow_st, 16)
            for n in range(6):
                act.wait_ge(tp_mm, n + 1)
                act.activation(vnat[:, :, 2 * n:2 * n + 2, :].rearrange("p t m d -> p m t d"),
                               pw[:, 4 + n % 2, :].rearrange("p (m t d) -> p m t d", m=2, t=2),
                               ACT.Copy).then_inc(tp_ev, 1)

            def bias(u):
                j, q = UNITS[u]
                nk = P * (q + 1)
                src = bass.AP(tensor=bw_d.tensor, offset=bw_d.offset + j * P * 1536 + 255 - P * q,
                              ap=[[1535, P], [512, 3], [1, nk]])
                act.dma_start(biasT[:, u % 2, :, 0:nk], src).then_inc(bias_in[u % 2], 16)

            act.wait_ge(brow_st, 16)
            for j in range(4):
                act.dma_start(bw_d[j], br_d[j:j + 1, :].to_broadcast([P, 1536])).then_inc(brow_st, 16)
            act.wait_ge(brow_st, 80)
            bias(0)
            for u in range(8):
                if u + 1 < 8:
                    if u:
                        act.wait_ge(aA, u)
                    bias(u + 1)
                j, q = UNITS[u]
                act.wait_ge(aA, u + 1)
                act.activation(lgt[:, u % 2, 0:3, 0:P * (q + 1)], lgt[:, u % 2, 0:3, 0:P * (q + 1)], ACT.Exp,
                               bias=nmx[:, u % 2, 0:1], accum_out=sums[:, u % 2, 0:1]).then_inc(aX, 1)
                act.wait_ge(aT, u + 1)
                if u >= 2:
                    act.wait_ge(aO, u - 1)
                flat = pw[:, 2:4, :].rearrange("p b n -> p (b n)")
                act.activation(pT[:, u % 2, 0:6, :].rearrange("p (g t) n -> p g t n", t=2)[:, :, 0:q + 1, :],
                               flat[:, 0:768].rearrange("p (g t n) -> p g t n", g=3, t=2)[:, :, 0:q + 1, :],
                               ACT.Copy).then_inc(aC, 1)
            act.wait_ge(ac_ok, 1)
            act.activation(dts[:, 2, 0:P], dts[:, 2, 0:P], ACT.Exp).then_inc(dt_ex, 1)
            act.dma_start(ac_d.rearrange("g (r n) -> (g r) n", r=8), dts[:, 1, :]).then_inc(ac_st, 16)
            act.wait_ge(ac_st, 16)

            def group(i, h, gg):
                g = at(4 * h + gg, i, 2)
                ph = f"ssm{h}"
                act.wait_ge(y_ev, g.times(4, 1))
                act.dma_start(acb[:, :, :, :].rearrange("p r t n -> p (r t n)"),
                              ac_d[one(g.times(1)), :].to_broadcast([P, 2048])).then_inc(acb_in, 16)
                for j in range(10):
                    c, e = at(C0[ph] + 10 * gg + j, i, 20), at(E0[ph] + 10 * gg + j, i, 20)
                    split_hi(c + 1)
                    if 1 <= j <= 6:
                        act.wait_ge(conv_d, g.times(6, 2 + j))
                        o = bct[:, gg, j - 1, :] if j <= 2 else xs[:, gg, j - 3, :]
                        act.activation(o, cv[:, (j - 1) % 2, :], ACT.Silu).then_inc(silu_d, 1)
                    if j == 4:
                        act.wait_ge(dec_in, g.times(1, 1))
                        act.activation(dec[:, :, :, :], dec[:, :, :, :], ACT.Exp).then_inc(dec_ex, 1)
                        act.activation(acb[:, :, 1, :], acb[:, :, 1, :], ACT.Exp).then_inc(dec_ex, 1)
                    if j == 9:
                        act.wait_ge(s0_mm, g.times(1, 1))
                        act.activation(st0[:, :], pw[:, 2, :], ACT.Copy).then_inc(s0_ev, 1)
                    if j < 6:
                        act.wait_ge(conv_d, g.times(6, 1 + j))
                        take(c, e, ub[:, j % 2, 3:259])
                    else:
                        if j == 6:
                            act.wait_ge(grp, g.times(1, 1))
                        take(c, e, sz[:, j - 6, :], ACT.Silu)
                for t in range(4):
                    act.wait_ge(y_ev, g.times(4, t + 2))
                    if t:
                        act.wait_ge(ssq_mm, g.times(4, t))
                    act.activation(sq[:, :], sz[:, t, :], ACT.Square).then_inc(sq_ok, 1)
                act.wait_ge(ssq_v, g.times(1, 1))
                act.activation(rstd[:, :], cv[:, 0, :], ACT.Sqrt).then_inc(ssq_r, 1)

            def to_tm(ph, j, i, stride, base, c, e, buf, **kw):
                idx = at(POST0[ph] + base, i, stride)
                act.wait_ge(post, idx.times(1, 1))
                take(c, e, buf[:, idx.slot(4), :], **kw)

            for h in range(2):
                with act.Fori(0, 2) as i:
                    group(i, h, 0)
                    group(i, h, 1)
                ph = f"sp{h}"
                with act.Fori(0, 4) as i:
                    for j in range(4):
                        c, e = at(C0[ph] + j, i, 4), at(E0[ph] + j, i, 4)
                        split_hi(c + 1)
                        if h == 0:
                            take(c, e, accS[:, one(i * 4 + j), :])
                        else:
                            to_tm(ph, j, i, 4, j, c, e, tm)
            for c in range(4):
                split_hi(At(C0["ap"] + c + 1))
                for h in range(2):
                    act.wait_ge(used, 2 * (C0["ap"] + c) + h + 1)
                    act.activation(accA[:, 4 * c + 2 * h:4 * c + 2 * h + 2, :],
                                   accp[:, (E0["ap"] + 2 * c + h) % 2, :].rearrange("p (m n) -> p m n", m=2),
                                   ACT.Copy).then_inc(evac, 1)

            def temps(ph, n, buf, func_of, last=False):
                def four(i):
                    for j in range(4):
                        c, e = at(C0[ph] + j, i, 4), at(E0[ph] + j, i, 4)
                        split_hi(c + 1)
                        to_tm(ph, j, i, 4, j, c, e, buf, func=func_of(j))
                with act.Fori(0, n - last) as i:
                    four(i)
                if last:
                    four(n - 1)

            temps("gs", 4, tm, lambda j: ACT.Sigmoid)
            temps("ga", 4, tm, lambda j: ACT.Sigmoid)
            act.wait_ge(acts_ok, 2)
            act.dma_start(x1[:, :, :], xt).then_inc(x_in, 16)
            temps("wo", 4, tm, lambda j: ACT.Copy)
            act.wait_ge(post, 4 + POST0["fi"])
            act.dma_start(x1_d, x1[:, :, :].rearrange("p k n -> p (k n)")).then_inc(x1_st, 16)
            act.activation(sq1[:, :, :], x1[:, :, :], ACT.Square).then_inc(rq, 1)
            root(2, rstd[:, :], sq1[:, 0, :])
            act.wait_ge(acts_ok, 3)
            temps("fi", FF_T // 2, tf, lambda j: ACT.Copy if j % 2 else ACT.Silu)
            act.wait_ge(acts_ok, 4)
            act.wait_ge(used, 2 * C0["fo"])
            act.wait_ge(x1_st, 16)
            act.dma_start(x1r[:, :, :].rearrange("p k n -> p (k n)"), x1_d).then_inc(x1_in, 16)
            with act.Fori(0, 8) as i:
                for m in range(2):
                    for q in range(4):
                        c = at(C0["fo"] + 4 * m + q, i, 8)
                        split_hi(c + 1)
                    e = at(E0["fo"] + m, i, 2)
                    idx = at(POST0["fo"] + m, i, 2)
                    act.wait_ge(post, idx.times(1, 3))
                    take(c, e, tf[:, idx.slot(2), :])


            act.wait_ge(post, 4 + POST0["lx"])
            act.activation(sqF[:, :, :], x1r[:, :, :], ACT.Square).then_inc(rq, 1)
            root(3, rstd[:, :], sqF[:, 0, :])
            act.wait_ge(acts_ok, 5)
            act.activation(sqF[:, :, :], x2T[:, :, :], ACT.Square).then_inc(rq, 1)
            root(4, rstd[:, :], sqF[:, 0, :])
            act.wait_ge(lam_x, 1)
            act.activation(lcon[:, 2, :], lcon[:, 1, :], ACT.Exp, scale=-1.0).then_inc(spe, 1)

            def biased(ph, n, dst, func, lead=True, ring=4):
                with act.Fori(0, n) as i:
                    for j in range(4):
                        c, e = at(C0[ph] + j, i, 4), at(E0[ph] + j, i, 4)
                        split_hi(c + 1)
                        idx = at(POST0[ph] + j, i, 4) if ph in POST0 else None
                        if idx is not None:
                            act.wait_ge(post, idx.times(1, 5 - ring))
                        take(c, e, dst(i, j, idx.slot(4) if idx is not None else 0), func, bias=Cd("b2", i * 4 + (B2[ph] + j)))

            def branch(ph):
                with act.Fori(0, 2) as i:
                    for j in range(4):
                        c = at(C0["wb" + ph] + j, i, 4)
                        split_hi(c + 1)
                        for h in range(2):
                            e = at(E0["wb" + ph] + 2 * j + h, i, 8)
                            act.wait_ge(used, c.times(2, h + 1))
                            act.activation(proj[:, one(i * 8 + (2 * j + h)), :], accp[:, e.slot(2):e.slot(2) + 1, 0:S], ACT.Copy).then_inc(evac, 1)
                biased("mg" + ph, 4, lambda i, j, s: tm2[:, s, :], ACT.Sigmoid)

            act.wait_ge(pad_ok, 1)
            biased("lx", 2, lambda i, j, s: ub2[:, j % 2, 3:259], ACT.Identity, ring=2)
            for i in range(2):
                if i:
                    act.wait_ge(lru_mm, i)
                act.dma_start(wabs[:, :, :, :], wab[:, 4 * i:4 * i + 4]).then_inc(wab_in, 16)
                act.wait_ge(lru_mm, i + 1)
                if i:
                    act.wait_ge(lru_y, i)
                for t in range(4):
                    act.activation(lr[:, t, :], pw[:, t, 0:S], ACT.Sigmoid, bias=C("ba", 4 * i + t))
                    ins = act.activation(li[:, t, :], pw[:, t, S:2 * S], ACT.Sigmoid, bias=C("bx", 4 * i + t))
                ins.then_inc(lru_g, 1)
                for j in range(4):
                    c, e = At(C0["lg"] + 4 * i + j), At(E0["lg"] + 4 * i + j)
                    split_hi(c + 1)
                    if j == 1:
                        act.wait_ge(lru_l, i + 1)
                        act.activation(lt[:, :, :], lr[:, :, :], ACT.Tanh)
                        act.activation(la[:, :, :], lr[:, :, :], ACT.Exp, scale=-1.0).then_inc(lru_e, 1)
                    if j == 3:
                        act.wait_ge(lru_w, i + 1)
                        act.activation(lw[:, :, :], lw[:, :, :], ACT.Sqrt).then_inc(lru_q, 1)
                    take(c, e, gl[:, j, :], ACT.Silu, bias=C("b2", B2["lg"] + 4 * i + j))
            act.wait_ge(acts_ok, 7)
            branch("a")
            c, e = At(C0["bf"]), At(E0["bf"])
            split_hi(c + 1)
            take(c, e, zf[:, :], ACT.Identity, bias=C("b2", B2["bf"]))
            act.wait_ge(spx, 2)
            act.activation(sft[32:40, 1, :], sft[32:40, 0, :], ACT.Exp, scale=-1.0).then_inc(spe, 1)
            act.wait_ge(evac, E0["bf"] + 1)
            act.activation(zf[0:24, :], zf[0:24, :], ACT.Sigmoid).then_inc(zf_ok, 1)
            act.wait_ge(gn_ok, 1)
            biased("nq", 5, lambda i, j, s: nk[:, one(i * 4 + j), :], ACT.Identity)
            act.dma_start(cw2s[:, :, :, :], cw2).then_inc(cw2_in, 16)

            def head_squares(n, src):
                if n >= 2:
                    act.wait_ge(hm, n - 1)
                act.activation(hq_[:, n % 2, :], src, ACT.Square).then_inc(hq, 1)

            def head_root(n, o, v):
                act.wait_ge(hv, n + 1)
                if n:
                    act.wait_ge(hn_ok, n)
                act.activation(o, v, ACT.Sqrt).then_inc(hr, 1)

            NSA_N = [0, 2, 4, 6, 12, 16]
            two = lambda t, n: t[:, n:n + 2, :].rearrange("p k n -> p (k n)")
            for j in range(8):
                x, m = j // 4, j // 2 % 2
                split_hi(At(C0["cmp"] + j + 1))
                if j < 6:
                    head_squares(j, two(nk, NSA_N[j]))
                if 1 <= j < 7:
                    head_root(j - 1, hr_[:, :], he_[:, :])
                if j % 2:
                    take(At(C0["cmp"] + j), At(E0["cmp"] + j // 2), hc[:, x, m, :], ACT.Silu, n=30)

            def copy_out(n, dst):
                act.wait_ge(tp_mm, n + 1)
                act.activation(dst.rearrange("p t m d -> p m t d"),
                               pw[:, 2 + n % 2, :].rearrange("p (m t d) -> p m t d", m=2, t=2), ACT.Copy).then_inc(tp_ev, 1)

            act.wait_ge(kc_mm, 1)
            act.activation(kcT[:, :], pw[:, 0, 0:30], ACT.Copy)
            act.activation(kcs[:, 0, :], pw[:, 0, 0:30], ACT.Square).then_inc(hq, 1)
            act.activation(vcn[:, :, :].rearrange("p a n -> p (a n)"), pw[0:15, 1, 0:256], ACT.Copy).then_inc(kc_ev, 1)
            for n in range(2):
                copy_out(6 + n, vn2[:, :, 2 * n:2 * n + 2, :])
            head_root(6, kcs[:, 1, :], kcs[:, 2, :])

            def attention(b0, b1):
                for b in range(b0, b1):
                    kind, h0, q = BATCH[b]
                    n = P * (q + 1) if kind else 15
                    l = (lg3 if kind == 3 else lg2)[:, b % 2]
                    act.wait_ge(aA, 8 + b + 1)
                    for r in range(4):
                        kw = {"accum_out": sums[:, b % 2, r:r + 1]} if kind else {}
                        ins = act.activation(l[:, r, 0:n], l[:, r, 0:n], ACT.Exp, bias=nmx[:, b % 2, r:r + 1], **kw)
                    ins.then_inc(aX, 1)
                    act.wait_ge(aT, 8 + b + 1)
                    if b - b0 >= 2:
                        act.wait_ge(aO, 8 + b - 1)
                    pt = (pT3 if kind == 3 else pT2)[:, b % 2].rearrange("p (r t) n -> p r t n", t=2)
                    rows, k = (P, q + 1) if kind else (15, 1)
                    act.activation(pt[0:rows, :, 0:k, :],
                                   pw[0:rows, 2:4, :].rearrange("p b (r t n) -> p (b r) t n", r=2, t=2)[:, :, 0:k, :],
                                   ACT.Copy).then_inc(aC, 1)

            attention(0, NSA_B)
            biased("ng", 2, lambda i, j, s: tm2[:, s, :], ACT.Silu)
            act.wait_ge(acts_ok, 8)
            branch("b")
            act.wait_ge(post, 4 + POST0["fg"])
            biased("fx", 6, lambda i, j, s: fx[:, one(i * 4 + j), :], ACT.Identity)
            for n in range(8):
                head_squares(7 + n, two(fx, 2 * n))
                if n < 4:
                    copy_out(8 + n, vn3[:, :, 2 * n:2 * n + 2, :])
                if n:
                    head_root(6 + n, hr_[:, :], he_[:, :])
            head_root(14, hr_[:, :], he_[:, :])
            attention(NSA_B, len(BATCH))
            biased("fg", 2, lambda i, j, s: tm2[:, s, :], ACT.Silu)
            act.wait_ge(acts_ok, 9)
            branch("c")
            act.wait_ge(acts_ok, 10)
            act.dma_start(p_in[:, :, :], pt).then_inc(p_land, 16)
            temps("w2", 4, tm2, lambda j: ACT.Copy)
            for c in range(2):
                split_hi(At(C0["ple"] + c + 1))
                for h in range(2):
                    act.wait_ge(used, 2 * (C0["ple"] + c) + h + 1)
                    for r in range(2):
                        e = E0["ple"] + 4 * c + 2 * h + r
                        m = 8 * c + 4 * h + 2 * r
                        act.activation(eT[:, m:m + 2, :], accp[:, e % 2, :].rearrange("p (m n) -> p m n", m=2), ACT.Copy).then_inc(evac, 1)
            act.wait_ge(evac, E0["pg"])
            act.activation(sqF[:, :, :], eT[:, :, :], ACT.Square).then_inc(rq, 1)
            root(5, rstd[:, :], sqF[:, 0, :])
            temps("pg", 4, tm2, lambda j: ACT.Sigmoid, last=True)

        @block.vector
        def _(dve):
            def split_lo(c):
                if not c.terms and c.base >= NRUN:
                    return
                dve.wait_ge(hi_done, c.times(2, 2))
                dve.tensor_tensor(wlo[:, c.slot(2), 8:16, :], raw[:, c.slot(4), 8:16, :],
                                  whi[:, c.slot(2), 8:16, :].bitcast(F32), ALU.subtract).then_inc(lo_b, 1)

            def pair(hi, lo, src):
                dve.tensor_copy(hi, src)
                dve.drain()
                return dve.tensor_tensor(lo, src, hi.bitcast(F32), ALU.subtract)

            def rms_root(n, ss, v, width, r=None, sems=None):
                r = rstd[:, :] if r is None else r
                sm, sv, sr, tmp, rec = sems
                dve.wait_ge(sm[0], sm[1])
                dve.tensor_scalar(v, ss, 1.0 / width, EPS, ALU.mult, ALU.add)
                dve.drain()
                dve.reciprocal(rec, v).then_inc(sv, 1)
                dve.wait_ge(sr[0], sr[1])
                dve.tensor_tensor(tmp, r, r, ALU.mult)
                dve.drain()
                dve.tensor_tensor(tmp, tmp, v, ALU.mult)
                dve.drain()
                dve.tensor_scalar(tmp, tmp, -0.5, 1.5, ALU.mult, ALU.add)
                dve.drain()
                dve.tensor_tensor(r, r, tmp, ALU.mult)
                dve.drain()

            def mod_piece(b, j):
                idx = b * 2 + (j // 2)
                dve.wait_ge(mod_in[j % 2], idx * 16 + 16)
                for k in range(4):
                    a = 4 * j + k
                    if a == 0:
                        ins = dve.tensor_scalar(macc[:, :], mraw[:, 0, 0, :], cact[:, 0:1], None, ALU.mult)
                    else:
                        ins = dve.scalar_tensor_tensor(macc[:, :], mraw[:, j % 2, k, :], cact[:, a:a + 1],
                                                       macc[:, :], ALU.mult, ALU.add)
                    if k < 3:
                        dve.drain()
                ins.then_inc(mod_used, 1)
                if j < 3:
                    dve.drain()
                else:
                    dve.drain().then_inc(macc_ok, 1)

            def mod_finish(b):
                dve.wait_ge(mod_mm, b + 1)
                dve.tensor_tensor(modT[:, wide(b, 4)], pw[:, 5, 0:4],
                                  cst[:, bass.ds(b * 4 + CO["bmod"], 4)] if not isinstance(b, int) else C("bmod", 4 * b, 4),
                                  ALU.add).then_inc(mod_ok, 1)

            def softplus(x, t, o, n, x_ok=None):
                ax, e, s, s2 = t
                dve.scalar_tensor_tensor(ax, x, -1.0, x, ALU.mult, ALU.max).then_inc(x_ok or spx, 1)
                dve.wait_ge(spe, n)
                dve.tensor_scalar(s, e, 2.0, None, ALU.add)
                dve.drain()
                dve.reciprocal(s, s)
                dve.drain()
                dve.tensor_tensor(s, s, e, ALU.mult)
                dve.drain()
                dve.tensor_tensor(s2, s, s, ALU.mult)
                dve.drain()
                dve.tensor_scalar(e, s2, 1.0 / 15, None, ALU.mult)
                for d in (13, 11, 9, 7, 5, 3):
                    dve.drain()
                    dve.scalar_tensor_tensor(e, e, 1.0 / d, s2, ALU.add, ALU.mult)
                dve.drain()
                dve.scalar_tensor_tensor(e, e, 1.0, s, ALU.add, ALU.mult)
                dve.tensor_scalar(ax, x, 0.0, None, ALU.max)
                dve.drain()
                dve.scalar_tensor_tensor(o, e, 2.0, ax, ALU.mult, ALU.add)
                dve.drain()

            dve.memset(ones[:, :], 1.0).then_inc(ones_ok, 1)
            for s_, n in ((post, 4), (cb_ev, 1), (xt_ev, 2), (y_ev, 1), (grp, 1)):
                for _ in range(n):
                    dve.memset(nudge[:, 4:5], 0.0).then_inc(s_, 1)
                    dve.drain()
            dve.wait_ge(cact_ok, 1)
            rms_root(1, pw[:, 4, 0:S], sqT[:, 1, :], D, sems=((rm, 1), rv, (rs, 1), sqT[:, 2, :], sqT[:, 0, :]))
            dve.tensor_tensor(xT[:, :, :], xT[:, :, :], rstd[:, :].rearrange("p (a n) -> p a n", a=1).to_broadcast([P, DT, S]), ALU.mult)
            for j in range(4):
                mod_piece(0, j)
            with dve.Fori(1, NMOD1) as b:
                mod_finish(b - 1)
                for j in range(4):
                    mod_piece(b, j)
            mod_finish(NMOD1 - 1)
            split_lo(At(0))
            dve.drain()

            def modulate(src, gain, norm, sh, sc, tmp):
                dve.scalar_tensor_tensor(gain, modT[:, sc:sc + 16], 1.0, norm, ALU.add, ALU.mult)
                dve.drain()
                for k in range(DT):
                    dve.tensor_scalar(tmp[:, k, :], src[:, k, :], gain[:, k:k + 1], modT[:, sh + k:sh + k + 1],
                                      ALU.mult, ALU.add)
                dve.drain()
                pair(act_hi[:, :, :], act_lo[:, :, :], tmp[:, :, :]).then_inc(acts_ok, 1)

            modulate(xT, gain1[:, :], C("n1", 0, 16), 0, 16, xT)

            def qkv_part(i, ride):
                for j in range(4):
                    split_lo(at(j + 1, i, 4))
                    if ride:
                        if j == 0:
                            mod_finish(i + (NMOD1 - 1)) if not (isinstance(i, int) and i == 0) else None
                        mod_piece(i + NMOD1, j)

            qkv_part(0, True)
            with dve.Fori(1, 8) as i:
                qkv_part(i, True)
            qkv_part(8, False)
            mod_finish(15)
            split_lo(At(37))
            dve.wait_ge(evac, 37)
            dve.wait_ge(mod_ok, 16)
            softplus(dtr[:, :], [dts[:, k, :] for k in (1, 2, 3, 4)], dts[:, 0, :], 2)
            dve.tensor_scalar(aneg[0:64, :], aneg[0:64, :], -1.0, None, ALU.mult)
            dve.drain()
            dve.tensor_scalar(dts[:, 3, :], dts[:, 0, :], aneg[0:64, 0:1], None, ALU.mult)
            dve.memset(dts[:, 4, :], 1.0)
            dve.drain()
            for t in range(2):
                dve.tensor_tensor_scan(dts[:, 1, t * P:(t + 1) * P], dts[:, 4, 0:P], dts[:, 3, t * P:(t + 1) * P],
                                       0.0, ALU.mult, ALU.add)
            dve.drain()
            dve.tensor_scalar(dts[:, 2, 0:P], dts[:, 1, 0:P], dts[:, 1, P - 1:P], -1.0, ALU.subtract, ALU.mult).then_inc(ac_ok, 1)

            def biased(u):
                j, q = UNITS[u]
                nk = P * (q + 1)
                dve.wait_ge(aL, u + 1)
                dve.wait_ge(bias_in[u % 2], 16 * (u // 2 + 1))
                if u >= 2:
                    dve.wait_ge(aT, u - 1)
                else:
                    dve.wait_ge(brow_ev, 1)
                flat = pw[:, 0:2, :].rearrange("p b n -> p (b n)")[:, 0:768].rearrange("p (g n) -> p g n", g=3)[:, :, 0:nk]
                l = lgt[:, u % 2, 0:3, 0:nk]
                dve.scalar_tensor_tensor(l, flat, ATT_SCALE, biasT[:, u % 2, :, 0:nk], ALU.mult, ALU.add)
                dve.drain()
                dve.tensor_reduce(mx[:, u % 2, 0:1], l, AX.XY, ALU.max)
                dve.drain()
                dve.tensor_scalar(nmx[:, u % 2, 0:1], mx[:, u % 2, 0:1], -1.0, None, ALU.mult).then_inc(aA, 1)

            def moved(u):
                j, q = UNITS[u]
                dve.wait_ge(aO, u + 1)
                dve.tensor_copy(ovec[:, u % 2, :], pw[:, 4, 0:P]).then_inc(aF, 1)
                dve.drain()
                pair(att_hi[:, j, q * P:(q + 1) * P], att_lo[:, j, q * P:(q + 1) * P], ovec[:, u % 2, :])

            biased(0)
            for u in range(8):
                if u + 1 < 8:
                    biased(u + 1)
                j, q = UNITS[u]
                l = lgt[:, u % 2, 0:3, 0:P * (q + 1)]
                dve.wait_ge(aX, u + 1)
                dve.reciprocal(rsum[:, u % 2, 0:1], sums[:, u % 2, 0:1])
                dve.drain()
                dve.tensor_scalar(l, l, rsum[:, u % 2, 0:1], None, ALU.mult).then_inc(aB, 1)
                if u:
                    moved(u - 1)
            moved(7)
            dve.wait_ge(dt_mm, 1)
            dve.tensor_copy(dtn[:, :, :].rearrange("p t h -> p (t h)"), pw[:, 0, 0:128])
            dve.tensor_copy(acn[:, :, :].rearrange("p t h -> p (t h)"), pw[:, 0, 128:256])
            dve.wait_ge(ac_st, 16)
            dve.tensor_copy(decn[:, :], pw[:, 0, 256:320]).then_inc(dt_ev, 1)
            for n in range(2):
                dve.memset(ub[:, n, 0:3], 0.0).then_inc(conv_d, 1)
            dve.drain()

            def group(i, h, gg):
                g = at(4 * h + gg, i, 2)
                ph = f"ssm{h}"
                bc, x = bct[:, gg], xs[:, gg]
                gv = g.times(1)

                def convolve(j):
                    dve.wait_ge(evac, at(E0[ph] + 10 * gg + j, i, 20).times(1, 1))
                    dve.wait_ge(silu_d, g.times(6, j + 1))
                    tile = g.times(1, 32 + 8 * j) if j < 2 else g.times(4, j - 2)
                    u, o = ub[:, j % 2, :], cv[:, j % 2, :]
                    dve.tensor_scalar(o, u[:, 0:S], Cd("cw", tile * 4), Cd("cb", tile), ALU.mult, ALU.add)
                    for k in range(1, 4):
                        dve.drain()
                        ins = dve.scalar_tensor_tensor(o, u[:, k:k + S], Cd("cw", tile * 4 + k), o, ALU.mult, ALU.add)
                    ins.then_inc(conv_d, 1)

                def stepped(t):
                    dve.wait_ge(xt_mm, g.times(4, t + 1))
                    dve.tensor_tensor(xdt[:, :, t * P:(t + 1) * P].rearrange("p c (r n) -> p c r n", r=2),
                                      pw[:, 5 if t % 2 else 1, 0:S].rearrange("p (c r n) -> p c r n", c=2, r=2),
                                      dtn[:, :, span(gv * 8 + 2 * t, 2)].rearrange("p c (r a) -> p c r a", a=1).to_broadcast([P, 2, 2, 64]), ALU.mult).then_inc(xt_ev, 1)

                for j in range(10):
                    split_lo(at(C0[ph] + 10 * gg + j + 1, i, 20))
                    if j < 6:
                        convolve(j)
                    if j == 2:
                        dve.wait_ge(acb_in, g.times(16, 16))
                        for r in range(8):
                            for t in range(2):
                                ins = dve.tensor_scalar(dec[:, r, t, :], acb[:, r, t, :],
                                                        acn[:, t, one(gv * 8 + r)],
                                                        0.0, ALU.subtract, ALU.min)
                        ins.then_inc(dec_in, 1)
                    if j == 3:
                        dve.wait_ge(cb_mm, g.times(1, 1))
                        dve.tensor_tensor(cbm[:, :, :], pw[:, 0, 0:S].rearrange("p (t n) -> p t n", t=2),
                                          C("tri01", 0, 128).rearrange("p (a n) -> p a n", a=1).to_broadcast([P, 2, P]), ALU.mult)
                        dve.tensor_copy(bnat[:, :], pw[:, 0, 256:384]).then_inc(cb_ev, 1)
                        dve.drain()
                    if j == 4:
                        dve.wait_ge(dec_ex, g.times(2, 1))
                        dve.tensor_tensor(dec[:, :, :, :].rearrange("p r t n -> p r (t n)"), dec[:, :, :, :].rearrange("p r t n -> p r (t n)"),
                                          cbm[:, :, :].rearrange("p t n -> p (t n)").rearrange("p (a n) -> p a n", a=1).to_broadcast([P, 8, S]),
                                          ALU.mult).then_inc(m_ok, 1)
                    if j == 5:
                        dve.wait_ge(dec_ex, g.times(2, 2))
                        dve.tensor_tensor(acb[:, :, 1, :], acb[:, :, 1, :],
                                          bc[:, 1, P:S].rearrange("p (a n) -> p a n", a=1).to_broadcast([P, 8, P]),
                                          ALU.mult).then_inc(ce_ok, 1)
                    if 5 <= j < 9:
                        stepped(j - 5)
                    if j == 8:
                        dve.drain()
                        dve.tensor_tensor(xdd[:, :].rearrange("p (r n) -> p r n", r=8),
                                          xdt[:, 0, :].rearrange("p (r n) -> p r n", r=8),
                                          decn[:, wide(gv, 8)].rearrange("p (r a) -> p r a", a=1).to_broadcast([P, 8, 64]),
                                          ALU.mult).then_inc(xdd_ok, 1)
                dve.wait_ge(evac, at(E0[ph] + 10 * gg + 9, i, 20).times(1, 1))
                for t in range(4):
                    dve.wait_ge(y_mm, g.times(4, t + 1))
                    dve.scalar_tensor_tensor(x[:, t, :], x[:, t, :], Cd("dsk", g.times(4, t)),
                                             pw[:, YB[t], 0:S], ALU.mult, ALU.add)
                    dve.drain()
                    dve.tensor_tensor(sz[:, t, :], sz[:, t, :], x[:, t, :], ALU.mult).then_inc(y_ev, 1)
                rms_root(None, pw[:, 5, 0:S], cv[:, 1, :], 512,
                         sems=((ssq_mm, g.times(4, 4)), ssq_v, (ssq_r, g.times(1, 1)), xdd[:, 0:S], cv[:, 0, :]))
                for t in range(4):
                    dve.scalar_tensor_tensor(sz[:, t, :], sz[:, t, :], Cd("ssmn", g.times(4, t)), rstd[:, :],
                                             ALU.mult, ALU.mult)
                dve.drain()
                k = wide(i * 2 + gg, 4)
                dve.tensor_copy(y_hi[:, k, :], sz[:, :, :])
                dve.drain()
                dve.tensor_tensor(y_lo[:, k, :], sz[:, :, :], y_hi[:, k, :].bitcast(F32), ALU.subtract).then_inc(grp, 1)

            def posts(ph, n, f, last=False):
                def four(i):
                    for j in range(4):
                        split_lo(at(C0[ph] + j + 1, i, 4))
                        dve.wait_ge(evac, at(E0[ph] + j, i, 4).times(1, 1))
                        f(i, j, at(POST0[ph] + j, i, 4).slot(4))
                with dve.Fori(0, n - last) as i:
                    four(i)
                if last:
                    four(n - 1)

            for h in range(2):
                with dve.Fori(0, 2) as i:
                    group(i, h, 0)
                    group(i, h, 1)
                if h == 0:
                    with dve.Fori(0, 4) as i:
                        for j in range(4):
                            split_lo(at(C0["sp0"] + j + 1, i, 4))
                else:
                    def add_s(i, j, s):
                        m = one(i * 4 + j)
                        dve.tensor_tensor(accS[:, m, :], accS[:, m, :], tm[:, s:s + 1, :], ALU.add).then_inc(post, 1)
                    posts("sp1", 4, add_s)
            dve.drain()
            for c in range(4):
                split_lo(At(C0["ap"] + c + 1))

            def gate_s(i, j, s):
                mod_gate(i, j, 16)
                m = one(i * 4 + j)
                dve.tensor_tensor(accS[:, m, :], accS[:, m, :], tm[:, s:s + 1, :], ALU.mult).then_inc(post, 1)

            def mod_gate(i, j, b0):
                if j == 0 and b0 == 16:
                    pass
                mod_piece(i + b0, j)
                if j == 3:
                    mod_finish(i + b0)

            posts("gs", 4, gate_s)

            def gate_a(i, j, s):
                mod_gate(i, j, 20)
                m = one(i * 4 + j)
                dve.tensor_tensor(t2[:, j % 2, :].rearrange("p (a n) -> p a n", a=1), accA[:, m, :], tm[:, s:s + 1, :], ALU.mult).then_inc(post, 1)
                dve.drain()
                dve.tensor_tensor(t2[:, j % 2, :].rearrange("p (a n) -> p a n", a=1), t2[:, j % 2, :].rearrange("p (a n) -> p a n", a=1), accS[:, m, :], ALU.add)
                dve.drain()
                pair(mg_hi[:, m, :], mg_lo[:, m, :], t2[:, j % 2, :].rearrange("p (a n) -> p a n", a=1))

            posts("ga", 4, gate_a)
            dve.drain().then_inc(acts_ok, 1)
            dve.wait_ge(x_in, 32)

            def add_x(i, j, s):
                m = one(i * 4 + j)
                dve.scalar_tensor_tensor(x1[:, m, :], tm[:, s:s + 1, :], modT[:, one(i * 4 + (32 + j))], x1[:, m, :],
                                         ALU.mult, ALU.add).then_inc(post, 1)

            posts("wo", 4, add_x)
            rms_root(2, pw[:, 4, 0:S], sq1[:, 1, :], D, sems=((rm, 2), rv, (rs, 2), sq1[:, 2, :], sq1[:, 0, :]))
            dve.wait_ge(x1_st, 16)
            dve.tensor_tensor(x1[:, :, :], x1[:, :, :], rstd[:, :].rearrange("p (a n) -> p a n", a=1).to_broadcast([P, DT, S]), ALU.mult)
            dve.drain()
            modulate(x1, gain2[:, :], C("n2", 0, 16), 48, 64, x1)

            def hidden(i, j, s):
                if j % 2:
                    f = one(i * 2 + j // 2)
                    o = hf[:, (j // 2):(j // 2) + 1, :]
                    dve.tensor_tensor(o, tf[:, s - 1:s, :], tf[:, s:s + 1, :], ALU.mult).then_inc(post, 1)
                    dve.drain()
                    dve.tensor_copy(hid_hi[:, f, :], o).then_inc(post, 1)
                    dve.drain()
                    dve.tensor_tensor(hid_lo[:, f, :], o, hid_hi[:, f, :].bitcast(F32), ALU.subtract)

            posts("fi", FF_T // 2, hidden)
            dve.drain().then_inc(acts_ok, 1)
            dve.wait_ge(x1_in, 16)
            with dve.Fori(0, 8) as i:
                for m in range(2):
                    for q in range(4):
                        c = at(C0["fo"] + 4 * m + q, i, 8)
                        split_lo(c + 1)
                    dve.wait_ge(evac, at(E0["fo"] + m, i, 2).times(1, 1))
                    k = one(i * 2 + m)
                    dve.scalar_tensor_tensor(x1r[:, k, :], tf[:, (POST0["fo"] + m) % 2:(POST0["fo"] + m) % 2 + 1, :],
                                             modT[:, one(i * 2 + (80 + m))], x1r[:, k, :], ALU.mult, ALU.add).then_inc(post, 1)
            dve.drain()
            bc16 = rstd[:, :].rearrange("p (a n) -> p a n", a=1).to_broadcast([P, DT, S])
            rms_root(3, pw[:, 4, 0:S], sqF[:, 1, :], D, sems=((rm, 3), rv, (rs, 3), sqF[:, 2, :], sqF[:, 0, :]))
            for k in range(DT):
                dve.scalar_tensor_tensor(x2T[:, k, :], x1r[:, k, :], C("fin", k), rstd[:, :], ALU.mult, ALU.mult)
            dve.drain().then_inc(acts_ok, 1)
            rms_root(4, pw[:, 4, 0:S], sqF[:, 1, :], D, sems=((rm, 4), rv, (rs, 4), sqF[:, 2, :], sqF[:, 0, :]))
            for k in range(DT):
                dve.scalar_tensor_tensor(sqF[:, k, :], x2T[:, k, :], C("ln2", k), rstd[:, :], ALU.mult, ALU.mult)
            dve.drain()
            pair(act_hi[:, :, :], act_lo[:, :, :], sqF[:, :, :])
            dve.drain().then_inc(acts_ok, 1)
            dve.tensor_scalar(lcon[:, 0, :], C("lam", 0, 8), -1.0, None, ALU.mult)
            dve.drain()
            softplus(lcon[:, 0, :], [lcon[:, k, :] for k in (1, 2, 3, 4)], lcon[:, 5, :], 3, lam_x)
            dve.tensor_scalar(lcon[:, 5, :], lcon[:, 5, :], 8.0, None, ALU.mult)
            for n in range(2):
                ins = dve.memset(ub2[:, n, 0:3], 0.0)
            dve.drain().then_inc(pad_ok, 1)

            def conv2(i, j, s):
                t = i * 4 + j
                u, o = ub2[:, j % 2:j % 2 + 1, :], uc[:, one(t), :]
                dve.tensor_scalar(o, u[:, :, 0:S], Cd("cw2", t * 4), Cd("cb2", t), ALU.mult, ALU.add)
                for k in range(1, 4):
                    dve.drain()
                    ins = dve.scalar_tensor_tensor(o, u[:, :, k:k + S], Cd("cw2", t * 4 + k), o, ALU.mult, ALU.add)
                ins.then_inc(post, 1)

            posts("lx", 2, conv2)
            dve.drain().then_inc(uc_ok, 1)
            for i in range(2):
                dve.wait_ge(lru_g, i + 1)
                for t in range(4):
                    dve.tensor_scalar(lr[:, t, :], lr[:, t, :], lcon[:, 5, 4 * i + t:4 * i + t + 1], None, ALU.mult)
                dve.drain().then_inc(lru_l, 1)
                for j in range(4):
                    split_lo(At(C0["lg"] + 4 * i + j + 1))
                    if j == 1:
                        dve.wait_ge(lru_e, i + 1)
                        dve.tensor_scalar(lw[:, :, :], lt[:, :, :], 1.0, None, ALU.add)
                        dve.drain()
                        dve.reciprocal(lw[:, :, :], lw[:, :, :])
                        dve.drain()
                        dve.tensor_tensor(li[:, :, :], li[:, :, :], uc[:, 4 * i:4 * i + 4, :], ALU.mult)
                        dve.scalar_tensor_tensor(lw[:, :, :], lt[:, :, :], 2.0, lw[:, :, :], ALU.mult, ALU.mult).then_inc(lru_w, 1)
                    if j == 3:
                        dve.wait_ge(lru_q, i + 1)
                        dve.tensor_tensor(lw[:, :, :], lw[:, :, :], li[:, :, :], ALU.mult)
                        dve.drain()
                        for t in range(4):
                            dve.tensor_tensor_scan(lt[:, t, :], la[:, t, :], lw[:, t, :], 0.0, ALU.mult, ALU.add)
                        dve.drain()
                dve.wait_ge(evac, E0["lg"] + 4 * i + 4)
                dve.tensor_tensor(gl[:, :, :], gl[:, :, :], lt[:, :, :], ALU.mult)
                dve.drain()
                pair(yb_hi[:, 4 * i:4 * i + 4, :], yb_lo[:, 4 * i:4 * i + 4, :], gl[:, :, :]).then_inc(lru_y, 1)
            dve.drain().then_inc(acts_ok, 1)

            def quiet(ph, n):
                with dve.Fori(0, n) as i:
                    for j in range(4):
                        split_lo(at(C0[ph] + j + 1, i, 4))

            def branch(ph):
                quiet("wb" + ph, 2)

                def merge(i, j, s):
                    m = one(i * 4 + j)
                    o = accM[:, m, :] if ph == "a" else t3[:, j % 2:j % 2 + 1, :]
                    dve.tensor_tensor(o, proj[:, m, :], tm2[:, s:s + 1, :], ALU.mult).then_inc(post, 1)
                    if ph != "a":
                        dve.drain()
                        dve.tensor_tensor(o if ph == "c" else accM[:, m, :], o, accM[:, m, :], ALU.add)
                    if ph == "c":
                        dve.drain()
                        pair(m2_hi[:, m, :], m2_lo[:, m, :], o)

                posts("mg" + ph, 4, merge)

            branch("a")
            split_lo(At(C0["bf"] + 1))
            dve.wait_ge(evac, E0["bf"] + 1)
            f = slice(32, 40)
            dve.tensor_scalar(zf[f, :], zf[f, :], -1.0, None, ALU.mult)
            dve.drain()
            softplus(zf[f, :], [sft[f, k, :] for k in (0, 1, 2, 3)], sft[f, 4, :], 4)
            dve.tensor_scalar(sft[f, 4, :], sft[f, 4, :], -1.0, None, ALU.mult)
            dve.memset(sft[f, 0, :], 1.0)
            dve.drain()
            dve.tensor_tensor_scan(zf[f, :], sft[f, 0, :], sft[f, 4, :], 0.0, ALU.mult, ALU.add)
            dve.tensor_scalar(nudge[:, :], cst[:, CO["ident"] + 32:CO["ident"] + 40], -1.0, None, ALU.mult)
            dve.drain().then_inc(zf_ok, 1)
            dve.wait_ge(gn_mm, 1)
            dve.tensor_copy(gn[:, :, :], pw[:, 5, 0:S].rearrange("p (t n) -> p t n", t=2)[:, :, 0:24])
            dve.tensor_copy(cn[:, :, :], pw[:, 5, 0:S].rearrange("p (t n) -> p t n", t=2)[:, :, 32:40])
            dve.tensor_scalar(C("gnq"), C("gnq"), ATT_SCALE, None, ALU.mult)
            dve.tensor_scalar(C("gfq"), C("gfq"), ATT_SCALE, None, ALU.mult)
            dve.drain().then_inc(gn_ok, 1)
            quiet("nq", 5)
            dve.wait_ge(evac, E0["nq"] + 20)
            for x in range(2):
                for v in range(2):
                    src = nk[:, 8 + 2 * x + v, :].rearrange("p (c t) -> p t c", t=16)
                    for r in range(2):
                        dve.tensor_tensor(kp[:, x, 16 * r:16 * r + 16, 15 * v:15 * v + 15], src[:, :, r:r + 15],
                                          C("pos", 32 * x + 16 * r, 16).rearrange("p (t a) -> p t a", a=1).to_broadcast([P, 16, 15]),
                                          ALU.add)
            dve.drain()
            kall = lambda t: t[:, :, :, :].rearrange("p x t c -> p (x t c)")
            pair(kall(kp_hi), kall(kp_lo), kall(kp))
            dve.drain().then_inc(kp_ok, 1)

            def head_norm(n, tiles, gain):
                rms_root(None, pw[:, 5, 0:512], hv_[:, :], P, hr_[:, :],
                         sems=((hm, n + 1), hv, (hr, n + 1), ht_[:, :], he_[:, :]))
                ins = dve.scalar_tensor_tensor(tiles, tiles, gain, hr_[:, :], ALU.mult, ALU.mult)
                dve.drain().then_inc(hn_ok, 1)

            NSA_N = [0, 2, 4, 6, 12, 16]
            two = lambda t, n: t[:, n:n + 2, :].rearrange("p k n -> p (k n)")
            for j in range(8):
                split_lo(At(C0["cmp"] + j + 1))
                if 1 <= j < 7:
                    head_norm(j - 1, two(nk, NSA_N[j - 1]), C("gnq") if j - 1 < 4 else C("gnk"))
            dve.wait_ge(kc_ev, 1)
            rms_root(None, pw[:, 5, 0:30], kcs[:, 3, :], P, kcs[:, 1, :], sems=((hm, 7), hv, (hr, 7), kcs[:, 4, :], kcs[:, 2, :]))
            dve.scalar_tensor_tensor(kcT[:, :], kcT[:, :], C("gnk"), kcs[:, 1, :], ALU.mult, ALU.mult)
            dve.drain().then_inc(hn_ok, 1)

            def att_bias(b):
                kind, h0, q = BATCH[b]
                n = P * (q + 1) if kind else 15
                dve.wait_ge(aL, 8 + b + 1)
                if b % 100 and b not in (NSA_B, NSA_B + 1) and b >= 2:
                    dve.wait_ge(aT, 8 + b - 1)
                l = (lg3 if kind == 3 else lg2)[:, b % 2, :, 0:n]
                flat = pw[:, 0:2, :].rearrange("p b (r n) -> p (b r) n", r=2)[:, :, 0:n]
                mask = (C("tri", 0, 256) if q else C("tri", 128, 128)) if kind else C("cmask", 15 * q, 15)
                if kind == 3:
                    for r in range(4):
                        dve.scalar_tensor_tensor(l[:, r, :], flat[:, r, :], cn[:, q, h0 + r:h0 + r + 1], mask, ALU.add, ALU.add)
                else:
                    dve.tensor_tensor(l, flat, mask.rearrange("p (a n) -> p a n", a=1).to_broadcast([P, 4, n]), ALU.add)
                dve.drain()
                dve.tensor_reduce(mx[:, b % 2, :], l, AX.X, ALU.max)
                dve.drain()
                dve.tensor_scalar(nmx[:, b % 2, :], mx[:, b % 2, :], -1.0, None, ALU.mult).then_inc(aA, 1)

            def att_scale(b):
                kind, h0, q = BATCH[b]
                n = P * (q + 1) if kind else 15
                l = (lg3 if kind == 3 else lg2)[:, b % 2, :, 0:n]
                s_, r_ = sums[:, b % 2, :], rsum[:, b % 2, :]
                dve.wait_ge(aX, 8 + b + 1)
                if kind == 0:
                    dve.tensor_tensor(l, l, C("cmask", 30 + 15 * q, 15).rearrange("p (a n) -> p a n", a=1).to_broadcast([P, 4, 15]), ALU.mult)
                    dve.drain()
                    dve.tensor_reduce(s_, l, AX.X, ALU.add)
                    dve.drain()
                dve.tensor_scalar(s_, s_, 1e-30, None, ALU.max)
                dve.drain()
                dve.reciprocal(r_, s_)
                dve.drain()
                if kind < 3:
                    dve.tensor_tensor(r_, r_, gn[:, q, 3 * h0 + kind:3 * h0 + kind + 10:3], ALU.mult)
                    dve.drain()
                for r in range(4):
                    ins = dve.tensor_scalar(l[:, r, :], l[:, r, :], r_[:, r:r + 1], None, ALU.mult)
                ins.then_inc(aB, 1)

            def att_moved(b):
                kind, h0, q = BATCH[b]
                if kind < 2:
                    return
                dve.wait_ge(aO, 8 + b + 1)
                dve.tensor_copy((fx if kind == 3 else nk)[:, h0:h0 + 4, q * P:(q + 1) * P],
                                pw[:, 4, :].rearrange("p (r n) -> p r n", r=4)).then_inc(aF, 1)

            def attention(b0, b1):
                att_bias(b0)
                for b in range(b0, b1):
                    if b + 1 < b1:
                        att_bias(b + 1)
                    att_scale(b)
                    if b > b0:
                        att_moved(b - 1)
                att_moved(b1 - 1)
                dve.drain()

            def gated(src):
                def f(i, j, s):
                    m = one(i * 4 + j)
                    o = t3[:, j % 2:j % 2 + 1, :]
                    dve.tensor_tensor(o, src[:, m, :], tm2[:, s:s + 1, :], ALU.mult).then_inc(post, 1)
                    dve.drain()
                    pair(yb_hi[:, m, :], yb_lo[:, m, :], o)
                return f

            attention(0, NSA_B)
            posts("ng", 2, gated(nk))
            dve.drain().then_inc(acts_ok, 1)
            branch("b")
            quiet("fx", 6)
            for n in range(8):
                head_norm(7 + n, two(fx, 2 * n), C("gfq") if n < 4 else C("gfk"))
            attention(NSA_B, len(BATCH))
            posts("fg", 2, gated(fx))
            dve.drain().then_inc(acts_ok, 1)
            branch("c")
            dve.drain().then_inc(acts_ok, 1)

            def add_x2(i, j, s):
                m = one(i * 4 + j)
                dve.tensor_tensor(x2T[:, m, :], x2T[:, m, :], tm2[:, s:s + 1, :], ALU.add).then_inc(post, 1)
                dve.drain()
                pair(act_hi[:, m, :], act_lo[:, m, :], x2T[:, m, :])

            dve.wait_ge(p_land, 16)
            pair(p_hi[:, :, :], p_lo[:, :, :], p_in[:, :, :]).then_inc(p_ok, 1)
            posts("w2", 4, add_x2)
            dve.drain().then_inc(h_ok, 1)
            for c in range(2):
                split_lo(At(C0["ple"] + c + 1))
            rms_root(5, pw[:, 4, 0:S], sqF[:, 1, :], D, sems=((rm, 5), rv, (rs, 5), sqF[:, 2, :], sqF[:, 0, :]))
            for k in range(DT):
                dve.scalar_tensor_tensor(eT[:, k, :], eT[:, k, :], C("pleg", k), rstd[:, :], ALU.mult, ALU.mult)
            dve.drain()

            def finish(i, j, s):
                m = one(i * 4 + j)
                o = t3[:, j % 2:j % 2 + 1, :]
                dve.tensor_tensor(o, eT[:, m, :], tm2[:, s:s + 1, :], ALU.mult).then_inc(post, 1)
                dve.drain()
                dve.tensor_tensor(x2T[:, m, :], x2T[:, m, :], o, ALU.add)

            posts("pg", 4, finish, last=True)
            dve.drain().then_inc(out_ok, 1)


def tiles(w, kt=16):
    k, m = w.shape
    return w.reshape(k // P // kt, kt, P, m // P, P).transpose(3, 0, 2, 1, 4)


def padded(w, cols):
    out = np.zeros((w.shape[0], cols), w.dtype)
    out[:, :w.shape[1]] = w
    return out


def per_tile(v):
    return v.reshape(-1, P).T


def feature_major(x):
    return np.ascontiguousarray(x.T.reshape(-1, P, x.shape[0]).transpose(1, 0, 2))


def distance_buckets():
    out = np.zeros((33, 3, 512), np.float32)
    for g, (window, dil) in enumerate(((128, 1), (512, 4), (2048, 16))):
        for i in range(512):
            d = 255 - i
            if d < 0 or d % dil or d > window:
                out[32, g, i] = 1
                continue
            n = np.float32(max(d, 1))
            large = 16 + int(np.float32(np.log(n / np.float32(16))) / np.float32(np.log(2048 / 16)) * np.float32(16))
            out[d if d < 16 else min(large, 31), g, i] = 1
    return out


def pack(a):
    f = lambda n: np.asarray(a[n])
    w_in = f("w_in")[0]
    chunks = [tiles(w_in[:, 0:4608])]
    chunks.append(tiles(padded(w_in[:, 14848:14912], P)))
    tz, tx = tiles(w_in[:, 4608:8704]), tiles(w_in[:, 8704:14848])
    sp = f("w_ssm_proj")[0]
    for h in range(2):
        for g in range(4 * h, 4 * h + 4):
            chunks += [tx[32 + g:33 + g], tx[40 + g:41 + g], tx[4 * g:4 * g + 4], tz[4 * g:4 * g + 4]]
        chunks.append(tiles(sp[2048 * h:2048 * h + 2048]))
    ap = f("w_attn_proj")[0].reshape(4, P, 4, 4, P)
    chunks.append(ap.transpose(2, 1, 3, 0, 4).reshape(4, 1, P, 16, P))
    chunks.append(tiles(w_in[:, 16960:19008]))
    chunks.append(tiles(w_in[:, 14912:16960]))
    chunks.append(tiles(f("w_out")[0]))
    ff = tiles(f("w_ffn_in")[0])
    chunks.append(np.stack([ff[0:FF_T], ff[FF_T:]], 1).reshape(2 * FF_T, 1, P, 16, P))
    w2 = f("w_in_2")[0]
    b2 = f("b_in_2")[0]
    o2, at2 = {}, 0
    for name, n in (("lx", 1024), ("lg", 1024), ("q", 1024), ("kv", 1536), ("bg", 24), ("ng", 1024),
                    ("fx", 3072), ("ff", 8), ("fg", 1024), ("mg", 6144)):
        o2[name] = slice(at2, at2 + n)
        at2 += n
    mg = [slice(o2["mg"].start + 2048 * b, o2["mg"].start + 2048 * b + 2048) for b in range(3)]

    def gates(v):
        out = np.zeros(v.shape[:-1] + (P,), v.dtype)
        out[..., 0:24] = v[..., o2["bg"]]
        out[..., 32:40] = v[..., o2["ff"]]
        return out

    wb = f("w_branch_2")[0]

    def branch(b):
        return wb[b].reshape(8, P, 8, 2, P).transpose(2, 1, 3, 0, 4).reshape(8, P, 16, P)

    cmp1 = f("cmp_w1_2")[0]
    chunks += [tiles(w2[:, o2["lx"]]), tiles(w2[:, o2["lg"]]), branch(0), tiles(w2[:, mg[0]]),
               tiles(gates(w2)), tiles(w2[:, o2["q"]]), tiles(w2[:, o2["kv"]]), tiles(cmp1[0]), tiles(cmp1[1]),
               tiles(w2[:, o2["ng"]]), branch(1), tiles(w2[:, mg[1]]),
               tiles(w2[:, o2["fx"]]), tiles(w2[:, o2["fg"]]), branch(2), tiles(w2[:, mg[2]]),
               tiles(f("w_out_2")[0]),
               f("w_ple_2")[0].reshape(2, P, 2, 8, P).transpose(2, 1, 3, 0, 4).reshape(2, P, 16, P),
               tiles(f("w_ple_gate_2")[0])]
    w16 = np.concatenate([c.reshape(-1, P, 16, P) for c in chunks])
    w11 = np.ascontiguousarray(tiles(f("w_ffn_out")[0], KFO).reshape(NFO, P, KFO, P))
    wm = np.ascontiguousarray(f("w_mod")[0].reshape(4, 4, P, 24, 512).transpose(3, 0, 2, 1, 4))
    cst = np.zeros((P, NCST), np.float32)

    def put(name, v):
        v = np.asarray(v)
        cst[:v.shape[0], CO[name]:CO[name] + v.shape[1]] = v

    put("c", per_tile(f("c")[0]))
    put("bmod", per_tile(f("b_mod")[0]))
    put("n1", per_tile(f("norm1_w")[0]))
    put("n2", per_tile(f("norm2_w")[0]))
    put("fin", per_tile(f("final_norm_w")))
    put("cw", f("conv_w")[0].reshape(4, 48, P).transpose(2, 1, 0).reshape(P, 192))
    put("cb", per_tile(f("conv_b")[0]))
    put("dtb", f("dt_bias")[0][:, None])
    put("alog", f("a_log")[0][:, None])
    put("dsk", per_tile(np.repeat(f("d_skip")[0], 64)))
    put("ssmn", per_tile(f("ssm_norm_w")[0]))
    put("rel", np.concatenate([f("rel_bias"), np.full((1, 12), NEG, np.float32)]))
    put("ident", np.eye(P))
    order = [b2[o2["lx"]], b2[o2["lg"]], b2[mg[0]], gates(b2), b2[o2["q"]], b2[o2["kv"]], b2[o2["ng"]],
             b2[mg[1]], b2[o2["fx"]], b2[o2["fg"]], b2[mg[2]]]
    put("b2", per_tile(np.concatenate(order)))
    put("cw2", f("conv_w_2")[0].reshape(4, 8, P).transpose(2, 1, 0).reshape(P, 32))
    put("cb2", per_tile(f("conv_b_2")[0]))
    put("ba", per_tile(f("lru_ba_2")[0]))
    put("bx", per_tile(f("lru_bx_2")[0]))
    put("lam", per_tile(f("lru_lambda_2")[0]))
    put("pos", f("cmp_pos_2")[0].transpose(2, 0, 1).reshape(P, 64))
    for name, src in (("gnq", "nsa_q_gain_2"), ("gnk", "nsa_k_gain_2"), ("gfq", "fox_q_gain_2"), ("gfk", "fox_k_gain_2")):
        put(name, f(src)[0][:, None])
    put("ln2", per_tile(f("ln_gain_2")[0]))
    put("pleg", per_tile(f("ple_gain_2")[0]))
    i = np.arange(P)
    tri = np.zeros((P, 256), np.float32)
    tri[:, 128:] = np.where(i[None, :] <= i[:, None], 0, NEG)
    put("tri", tri)
    seen = (np.arange(15) * 16 + 31)[None, None, :] <= i[:, None, None] + P * np.arange(2)[None, :, None]
    put("cmask", np.concatenate([np.where(seen, 0, NEG).reshape(P, 30), seen.reshape(P, 30)], 1).astype(np.float32))
    wab = np.zeros((P, 8, 2, P), np.float32)
    for n, name in enumerate(("lru_wa_2", "lru_wx_2")):
        v = f(name)[0].reshape(8, 2, 64, 64)
        for r in range(2):
            wab[64 * r:64 * r + 64, :, n, 64 * r:64 * r + 64] = v[:, r].transpose(1, 0, 2)
    cw2 = np.ascontiguousarray(f("cmp_w2_2")[0].reshape(2, 2, P, P).transpose(2, 0, 1, 3))
    put("tri01", (i[None, :] >= i[:, None]).astype(np.float32))
    return {"w16": w16, "w11": w11, "wm": wm, "cst": cst, "onehot": distance_buckets(),
            "xt": feature_major(f("x")[0]), "pt": feature_major(f("p_2")[0, 0]), "wab": wab, "cw2": cw2}


_NAMES = ["w16", "w11", "wm", "cst", "onehot", "xt", "pt", "wab", "cw2"]


def kernel(**inputs):
    import numpy as _np
    import concourse.bacc as _bacc
    from concourse import mybir as _mybir
    from concourse.bass_utils import run_bass_kernel_spmd as _run

    arrays = {k: _np.ascontiguousarray(v) for k, v in pack(inputs).items()}
    nc = _bacc.Bacc("TRN2", target_bir_lowering=False, num_devices=1)
    args = [nc.dram_tensor(k, arrays[k].shape, _mybir.dt.float32, kind="ExternalInput").ap() for k in _NAMES]
    args.append(nc.dram_tensor("out_dram", (P, DT * S), _mybir.dt.float32, kind="ExternalOutput").ap())
    first_and_second_block(nc, *args)
    r = _run(nc, [arrays], core_ids=[0])
    got = r.results[0]["out_dram"]
    return got.reshape(P, DT, S).transpose(2, 1, 0).reshape(1, S, D)
```

```python
from contextlib import ExitStack

import numpy as np
import concourse.bass as bass
from concourse import mybir

F32 = mybir.dt.float32
F32R = mybir.dt.float32r
ALU = mybir.AluOpType
ACT = mybir.ActivationFunctionType
AX = mybir.AxisListType

P = 128
S = 256
D = 2048
DT = D // P
EPS = 1e-6
NEG = -1e30
ATT_SCALE = float(128) ** -0.5
FF_T = 5632 // P
SG = 8
LRU_T = 8

PHASES = [
    ("qkv", 36, 36), ("dt", 1, 1),
    ("ssm0", 40, 40), ("sp0", 16, 16), ("ssm1", 40, 40), ("sp1", 16, 16),
    ("ap", 4, 8), ("gs", 16, 16), ("ga", 16, 16), ("wo", 16, 16),
    ("fi", 88, 88), ("fo", 64, 16),
    ("lx", 8, 8), ("lg", 8, 8), ("wba", 8, 16), ("mga", 16, 16),
    ("bf", 1, 1), ("nq", 20, 20), ("cmp", 8, 2), ("ng", 8, 8), ("wbb", 8, 16), ("mgb", 16, 16),
    ("fx", 24, 24), ("fg", 8, 8), ("wbc", 8, 16), ("mgc", 16, 16),
    ("w2", 16, 16), ("ple", 2, 8), ("pg", 16, 16),
]
C0, E0 = {}, {}
_c = _e = 0
for _n, _k, _r in PHASES:
    C0[_n], E0[_n] = _c, _e
    _c, _e = _c + _k, _e + _r
CHUNKS = _c
KFO = 11
NFO = 64

CST = [
    ("c", 16), ("bmod", 96), ("n1", 16), ("n2", 16), ("fin", 16), ("cw", 48 * 4), ("cb", 48),
    ("dtb", 1), ("alog", 1), ("dsk", 32), ("ssmn", 32), ("rel", 12),
    ("b2", 125), ("cw2", 32), ("cb2", 8), ("ba", 8), ("bx", 8), ("lam", 8), ("pos", 64),
    ("gnq", 1), ("gnk", 1), ("gfq", 1), ("gfk", 1), ("ln2", 16), ("pleg", 16),
    ("ident", 128), ("tri", 256), ("tri01", 128), ("cmask", 60),
]
CO = {}
_o = 0
for _n, _k in CST:
    CO[_n] = _o
    _o += _k
NCST = _o


class At:

    def __init__(self, base, *terms):
        self.base, self.terms = base, terms

    def __add__(self, n):
        return At(self.base + n, *self.terms)

    def slot(self, n):
        return self.base % n

    def times(self, k, add=0):
        v = self.base * k + add
        for reg, stride in self.terms:
            v = reg * (stride * k) + v
        return v

    def round(self, n, k, add=0):
        v = (self.base // n) * k + add
        for reg, stride in self.terms:
            v = reg * (stride // n * k) + v
        return v


def at(base, i, stride):
    return At(base + i * stride) if isinstance(i, int) else At(base, (i, stride))


def one(i):
    return slice(i, i + 1) if isinstance(i, int) else bass.ds(i, 1)


def span(i, n):
    return slice(i, i + n) if isinstance(i, int) else bass.ds(i, n)


def wide(i, n):
    return slice(i * n, i * n + n) if isinstance(i, int) else bass.ds(i * n, n)


def first_and_second_block(nc, w16, w11, wm, cst_d, onehot, xt, pt, wab, cw2, out):
    ctx = ExitStack()
    with ctx:
        BASE = 16512
        CSTB = BASE + 98304
        W = CSTB + 9216

        def sb(name, shape, offset, dt=F32):
            return nc.alloc_sbuf_tensor_at(name, shape, dt, offset=offset)

        def sem(name):
            return ctx.enter_context(nc.semaphore(name))

        raw = sb("raw", [P, 4, 16, P], BASE)
        whi = sb("whi", [P, 2, 16, P], BASE + 32768, F32R)
        wlo = sb("wlo", [P, 2, 16, P], BASE + 49152, F32R)
        act_hi = sb("act_hi", [P, DT, S], BASE + 65536, F32R)
        act_lo = sb("act_lo", [P, DT, S], BASE + 81920, F32R)
        cst = sb("cst", [P, NCST], CSTB)
        ones = sb("ones", [P, P], CSTB + 5376)
        modT = sb("modT", [P, 96], CSTB + 5888)
        dtn = sb("dtn", [P, 2, 64], CSTB + 6272)
        acn = sb("acn", [P, 2, 64], CSTB + 6784)
        decn = sb("decn", [P, 64], CSTB + 7296)
        gain1 = sb("gain1", [P, DT], CSTB + 7552)
        gain2 = sb("gain2", [P, DT], CSTB + 7616)
        mx = sb("mx", [P, 2, 4], CSTB + 7680)
        nmx = sb("nmx", [P, 2, 4], CSTB + 7712)
        sums = sb("sums", [P, 2, 4], CSTB + 7744)
        rsum = sb("rsum", [P, 2, 4], CSTB + 7776)
        cact = sb("cact", [P, 16], CSTB + 7808)
        aneg = sb("aneg", [P, 1], CSTB + 7872)
        nudge = sb("nudge", [P, 8], CSTB + 7904)
        spl = sb("spl", [P, 8], CSTB + 7936)
        rstd = sb("rstd", [P, S], CSTB + 8192)

        def C(name, a=0, n=1):
            return cst[:, CO[name] + a:CO[name] + a + n]

        def Cd(name, a):
            return cst[:, CO[name] + a:CO[name] + a + 1] if isinstance(a, int) else cst[:, bass.ds(a + CO[name], 1)]

        ident = C("ident", 0, 128)

        xT = sb("xT", [P, DT, S], W)
        sqT = sb("sqT", [P, DT, S], W + 16384)
        mraw_a = sb("mraw_a", [P, 4, 4, 512], W + 36864)
        mraw_b = sb("mraw_b", [P, 4, 4, 512], W + 57344)
        macc = sb("macc", [P, 512], W + 98304)
        macp = sb("macp", [P, 512], W + 100352)
        macc1 = sb("macc1", [P, 512], W + 69632)
        macp1 = sb("macp1", [P, 512], W + 71680)
        qkv = sb("qkv", [P, 36, S], W)
        vnat = sb("vnat", [P, 2, 12, P], W + 36864)
        att_hi = sb("att_hi", [P, 4, S], W + 49152, F32R)
        att_lo = sb("att_lo", [P, 4, S], W + 53248, F32R)
        dtr = sb("dtr", [64, S], W + 57344)
        dts = sb("dts", [64, 6, S], W + 58368)
        biasT = sb("biasT", [P, 2, 3, S], W + 75776)
        lgt = sb("lgt", [P, 2, 4, S], W + 81920)
        pT = sb("pT", [P, 2, 8, P], W + 90112)
        ovec = sb("ovec", [P, 2, P], W + 64512)
        brow = sb("brow", [4, 3, 512], W + 98304)
        oneh = sb("oneh", [33, 3, 512], W + 81920)
        y_hi = sb("y_hi", [P, 16, S], W, F32R)
        y_lo = sb("y_lo", [P, 16, S], W + 16384, F32R)
        accS = sb("accS", [P, DT, S], W + 32768)
        Z = W + 57344
        ub = sb("ub", [P, 2, 259], Z)
        cv = sb("cv", [P, 2, S], Z + 2080)
        bct = sb("bct", [P, 2, 2, S], Z + 4128)
        xs = sb("xs", [P, 2, 4, S], Z + 8224)
        sz = sb("sz", [P, 4, S], Z + 16416)
        acb = sb("acb", [P, 8, 2, P], Z + 20512)
        dec = sb("dec", [P, 8, 2, P], Z + 28704)
        xdt = sb("xdt", [P, 2, 512], Z + 36896)
        xdd = sb("xdd", [P, 512], Z + 40992)
        st0 = sb("st0", [P, 512], Z + 43040)
        cbm = sb("cbm", [P, 2, P], Z + 45088)
        bnat = sb("bnat", [P, P], Z + 46112)
        sq = sb("sq", [P, S], Z + 46624)
        accA = sb("accA", [P, DT, S], W + 16384)
        mg_hi = sb("mg_hi", [P, DT, S], W, F32R)
        mg_lo = sb("mg_lo", [P, DT, S], W + 75776, F32R)
        tm = sb("tm", [P, 4, S], W + 92160)
        t2 = sb("t2", [P, 2, S], W + 96256)
        x1 = sb("x1", [P, DT, S], W + 32768)
        xq = sb("xq", [P, DT, S], W)
        sq1 = sb("sq1", [P, DT, S], W + 16384)
        hid_hi = sb("hid_hi", [P, FF_T, S], W, F32R)
        hid_lo = sb("hid_lo", [P, FF_T, S], W + 45056, F32R)
        tf = sb("tf", [P, 4, S], W + 90112)
        hf = sb("hf", [P, 2, S], W + 94208)
        x1r = sb("x1r", [P, DT, S], BASE + 65536)

        x2T = sb("x2T", [P, DT, S], W)
        accM = sb("accM", [P, DT, S], W + 16384)
        sqF = sb("sqF", [P, DT, S], W + 49152)
        yb_hi = sb("yb_hi", [P, 8, S], W + 32768, F32R)
        yb_lo = sb("yb_lo", [P, 8, S], W + 40960, F32R)
        gate = sb("gate", [P, 8, S], W + 40960)
        R2 = W + 49152
        proj = sb("proj", [P, DT, S], R2)
        tm2 = sb("tm2", [P, 4, S], W + 98304)
        t3 = sb("t3", [P, 2, S], W + 102400)
        uc = sb("uc", [P, 8, S], R2)
        gl = sb("gl", [P, 4, S], R2 + 8192)
        lr, li, lt, la, lw = (sb(n, [P, 4, S], R2 + 12288 + 4096 * k) for k, n in enumerate(("lr", "li", "lt", "la", "lw")))
        wabs = sb("wabs", [P, 4, 2, P], R2 + 32768)
        ub2 = sb("ub2", [P, 2, 259], R2 + 36864)
        lcon = sb("lcon", [P, 6, 8], R2 + 38976)
        zf = sb("zf", [P, S], CSTB + 6272)
        gn = sb("gn", [P, 2, 24], CSTB + 7296)
        cn = sb("cn", [P, 2, 8], CSTB + 7488)
        sft = sb("sft", [P, 5, S], W + 32768)
        nk = sb("nk", [P, 20, S], R2)
        kp = sb("kp", [P, 2, 32, 30], R2 + 20480)
        kp_hi = sb("kp_hi", [P, 2, 32, 30], R2 + 28160, F32R)
        kp_lo = sb("kp_lo", [P, 2, 32, 30], R2 + 35840, F32R)
        cw2s = sb("cw2s", [P, 2, 2, P], R2 + 43520)
        hc = sb("hc", [P, 2, 2, 30], R2 + 45568)
        hct = sb("hct", [30, 2, 256], R2 + 20480)
        vcn = sb("vcn", [15, 2, P], R2 + 46080)
        kcT = sb("kcT", [P, 30], R2 + 47104)
        kcs = sb("kcs", [P, 5, 30], R2 + 47232)
        hq_ = sb("hsq", [P, 2, 512], W + 32768)
        hr_, hv_, ht_, he_ = (sb(n, [P, 512], W + 36864 + 2048 * k) for k, n in enumerate(("hroot", "hval", "htmp", "hrec")))
        lg2 = sb("lg2", [P, 2, 4, S], R2 + 20480)
        pT2 = sb("pT2", [P, 2, 8, P], R2 + 28672)
        vn2 = sb("vn2", [P, 2, 4, P], R2 + 36864)
        fx = sb("fx", [P, 24, S], R2)
        vn3 = sb("vn3", [P, 2, 8, P], R2 + 24576)
        lg3 = sb("lg3", [P, 2, 4, S], R2 + 32768)
        pT3 = sb("pT3", [P, 2, 8, P], R2 + 40960)
        m2_hi = sb("m2_hi", [P, DT, S], W + 65536, F32R)
        m2_lo = sb("m2_lo", [P, DT, S], W + 81920, F32R)
        eT = sb("eT", [P, DT, S], W + 16384)
        p_in = sb("p_in", [P, 2, S], W + 32768)
        p_hi = sb("p_hi", [P, 2, S], W + 34816, F32R)
        p_lo = sb("p_lo", [P, 2, S], W + 36864, F32R)

        accp = ctx.enter_context(nc.psum_tensor("accp", [P, 2, 512], F32))
        pw = ctx.enter_context(nc.psum_tensor("pw", [P, 6, 512], F32))

        x1_d = nc.dram_tensor("x1_d", [P, DT * S], F32, kind="Internal").ap()
        ac_d = nc.dram_tensor("ac_d", [SG, 8 * S], F32, kind="Internal").ap()
        br_d = nc.dram_tensor("br_d", [4, 3 * 512], F32, kind="Internal").ap()
        bw_d = nc.dram_tensor("bw_d", [4, P, 3 * 512], F32, kind="Internal").ap()

        raw_in = [sem(f"raw_in{i}") for i in range(4)]
        hi_done = sem("hi_done")
        lo_a = sem("lo_a")
        lo_b = sem("lo_b")
        used = sem("used")
        evac = sem("evac")
        post = sem("post")
        cst_in = sem("cst_in")
        x_in = sem("x_in")
        ones_ok = sem("ones_ok")
        mod_in = [sem(f"mod_in{j}") for j in range(4)]
        mod_used = sem("mod_used")
        modp_used = sem("modp_used")
        quarter = sem("quarter")
        quarter_hi = sem("quarter_hi")
        quarter_lo = sem("quarter_lo")
        cact_ok = sem("cact_ok")
        macc_ok = sem("macc_ok")
        mod_mm = sem("mod_mm")
        mod_ok = sem("mod_ok")
        rq, rm, rv, rs = sem("rms_squares"), sem("rms_sum"), sem("rms_recip"), sem("rms_root")
        acts_ok = sem("acts_ok")
        spx, spe = sem("sp_abs"), sem("sp_exp")
        tp_mm, tp_ev = sem("tp_mm"), sem("tp_ev")
        aL, aA, aX, aB, aT, aC, aO, aF = (sem("att_" + n) for n in (
            "logits", "biased", "exp", "scaled", "turned", "copied", "out", "moved"))
        brow_mm, brow_ev, brow_st = sem("brow_mm"), sem("brow_ev"), sem("brow_st")
        oneh_in = sem("oneh_in")
        bias_in = [sem("bias_in0"), sem("bias_in1")]
        ac_ok, ac_st, acb_in = sem("ac_ok"), sem("ac_st"), sem("acb_in")
        dt_mm, dt_ev, dt_ex = sem("dt_mm"), sem("dt_ev"), sem("dt_ex")
        conv_d, silu_d = sem("conv_done"), sem("silu_done")
        dec_in, dec_ex = sem("dec_ready"), sem("dec_exp")
        cb_mm, cb_ev = sem("cb_mm"), sem("cb_ev")
        m_ok, ce_ok = sem("m_ok"), sem("ce_ok")
        xt_mm, xt_ev = sem("xt_mm"), sem("xt_ev")
        xdd_ok, s0_mm, s0_ev = sem("xdd_ok"), sem("s0_mm"), sem("s0_ev")
        y_mm, y_ev, sq_ok = sem("y_mm"), sem("y_ev"), sem("sq_ok")
        ssq_mm, ssq_v, ssq_r, grp = sem("ssq_mm"), sem("ssq_v"), sem("ssq_r"), sem("grp_done")
        x1_st, x1_in = sem("x1_st"), sem("x1_in")
        pad_ok = sem("pad_ok")
        out_ok, out_st = sem("out_ok"), sem("out_st")

        uc_ok, wab_in, lru_mm, lru_g, lru_l, lru_e, lru_w, lru_q, lru_y = (sem("lru_" + n) for n in (
            "conv", "weights", "mm", "gates", "logs", "exps", "squares", "roots", "y"))
        lam_x = sem("lam")
        yb_ok = sem("yb_ok")
        zf_ok, gn_mm, gn_ok = sem("zf_ok"), sem("gn_mm"), sem("gn_ok")
        kp_ok, cw2_in, kc_mm, kc_ev = sem("kp_ok"), sem("cw2_in"), sem("kc_mm"), sem("kc_ev")
        hq, hm, hv, hr = sem("head_squares"), sem("head_sum"), sem("head_recip"), sem("head_root")
        hn_ok = sem("head_normed")
        hct_mm, hct_ev = sem("hidden_turned"), sem("hidden_moved")
        p_ok, p_land, h_ok = sem("p_ok"), sem("p_land"), sem("h_ok")
        POST0, _p = {}, 0
        for name, n in (("sp1", 16), ("gs", 16), ("ga", 16), ("wo", 16), ("fi", 88), ("fo", 16),
                        ("lx", 8), ("mga", 16), ("mgb", 16), ("mgc", 16), ("w2", 16), ("pg", 16)):
            POST0[name] = _p
            _p += n
        NMOD1 = 8
        YB = (3, 4, 0, 1)
        B2, _b = {}, 0
        for name, n in (("lx", 8), ("lg", 8), ("mga", 16), ("bf", 1), ("nq", 20), ("ng", 8), ("mgb", 16),
                        ("fx", 24), ("fg", 8), ("mgc", 16)):
            B2[name] = _b
            _b += n
        NSA_N = [0, 2, 4, 6, 12, 16]
        BATCH = [(kind, 4 * g, q) for g in range(2) for q in (1, 0) for kind in range(3)]
        BATCH += [(3, 4 * g, q) for g in range(2) for q in (1, 0)]
        NSA_B = 12
        RIDES = {b: [b + 1] for b in range(1, 7)} | {NSA_B + b: [2 * b, 2 * b + 1] for b in range(4)}
        CLOSED = [n for n, b in enumerate(BATCH) if b[0] >= 2]
        UNITS = [(j, q) for j in range(4) for q in (1, 0)]

        block = ctx.enter_context(nc.Block())

        @block.sync
        def _(sp):
            sp.dma_start(cst[:, :], cst_d).then_inc(cst_in, 16)
            sp.dma_start(xT[:, :, :], xt).then_inc(x_in, 16)

            def piece(b, j, ring=4):
                if ring == 4 and not (isinstance(b, int) and b == 0):
                    sp.wait_ge(modp_used if j == 3 else mod_used, b if j == 3 else b * 3 + (j - 2))
                elif ring == 2 and j == 1:
                    sp.wait_ge(modp_used, b)
                elif ring == 2:
                    sp.wait_ge(mod_used, b * 3 + (0, 0, 1, 2)[j])
                buf = mraw_a if early else mraw_b
                sp.dma_start(buf[:, j % ring], wm[one(b), j].rearrange("a p k n -> p (a k) n")).then_inc(mod_in[j], 16)

            def load(c, src, k=16, free=True):
                if free:
                    sp.wait_ge(lo_a, c.times(1, -3))
                    sp.wait_ge(lo_b, c.times(1, -3))
                sp.dma_start(raw[:, c.slot(4), 0:k, :], src.rearrange("a p k n -> p (a k) n")).then_inc(raw_in[c.slot(4)], 16)

            early = True
            for j in range(4):
                piece(0, j)
            with sp.Fori(1, NMOD1 - 1) as b:
                for j in range(4):
                    piece(b, j)
            load(At(0), w16[0:1], free=False)
            for j in range(4):
                piece(NMOD1 - 1, j)
            for j in range(1, 4):
                load(At(j), w16[j:j + 1], free=False)

            def riding(n, c0, b0, js, ring=4):
                with sp.Fori(0, n) as i:
                    for j in range(8):
                        load(at(c0 + j, i, 8), w16[one(i * 8 + (c0 + j))])
                        if j in js:
                            piece(i + b0, js.index(j), ring)

            def plain(a, b, arr=None, off=0, k=16):
                arr = w16 if arr is None else arr
                n = (b - a) // 4
                if n > 0:
                    with sp.Fori(0, n) as i:
                        for j in range(4):
                            load(at(a + j, i, 4), arr[one(i * 4 + (a + j - off))], k)
                for c in range(a + 4 * n, b):
                    load(At(c), arr[c - off:c - off + 1], k)

            riding(4, 4, 8, (0, 1, 2, 3))
            plain(36, C0["sp0"] + 4)
            early = False
            for h in range(2):
                sp.wait_ge(grp, 4 * h + 5)
                riding(2, C0[f"sp{h}"] + 4, 12 + 2 * h, (0, 1, 2, 3))
                plain(C0[f"sp{h}"] + 20, C0["sp1"] + 4 if h == 0 else C0["gs"])
            for n, ph in enumerate(("gs", "ga", "wo", "fi")):
                riding(2, C0[ph], 16 + 2 * n, (0, 2, 4, 6), 2)
            plain(C0["fi"] + 16, C0["fo"])
            plain(C0["fo"], C0["fo"] + NFO, w11, C0["fo"], KFO)
            plain(C0["lx"], CHUNKS, w16, NFO)
            sp.wait_ge(out_ok, 1)
            sp.dma_start(out, x2T[:, :, :].rearrange("p k n -> p (k n)")).then_inc(out_st, 16)
            sp.wait_ge(out_st, 16)

        NRUN = CHUNKS

        @block.gpsimd
        def _(pool):
            def lo(c):
                pool.wait_ge(hi_done, c.times(2, 1))
                nc.gpsimd.tensor_tensor(wlo[:, c.slot(2), 0:8, :], raw[:, c.slot(4), 0:8, :],
                                        whi[:, c.slot(2), 0:8, :].bitcast(F32), ALU.subtract).then_inc(lo_a, 1)

            def run(a, b):
                n = (b - a) // 4
                if n > 0:
                    with pool.Fori(0, n) as i:
                        for j in range(4):
                            lo(at(a + j, i, 4))
                for c in range(a + 4 * n, b):
                    lo(At(c))

            def mod_scale(b, buf, slot=3):
                pool.wait_ge(mod_in[3], b * 16 + 16)
                nc.gpsimd.tensor_tensor(buf[:, slot, :, :], buf[:, slot, :, :],
                                        cact[:, 12:16].rearrange("p (k a) -> p k a", a=1).to_broadcast([P, 4, 512]), ALU.mult)
                pool.drain()

            def mod_add(b, buf, slot=3, acc=None, ahead=0):
                nc.gpsimd.tensor_tensor(buf[:, slot, 0:2, :], buf[:, slot, 0:2, :], buf[:, slot, 2:4, :], ALU.add)
                pool.drain()
                if not isinstance(b, int) or b > ahead:
                    pool.wait_ge(mod_mm, b - ahead)
                nc.gpsimd.tensor_tensor((acc or macp)[:, :], buf[:, slot, 0, :], buf[:, slot, 1, :], ALU.add).then_inc(modp_used, 1)

            def lo_quarter(n, src):
                pool.wait_ge(quarter_hi, n + 1)
                t = slice(4 * (n % 4), 4 * (n % 4) + 4)
                nc.gpsimd.tensor_tensor(act_lo[:, t, :], src[:, t, :], act_hi[:, t, :].bitcast(F32), ALU.subtract).then_inc(quarter_lo, 1)

            pool.wait_ge(cact_ok, 1)
            for b in range(NMOD1):
                mod_scale(b, mraw_a)
                mod_add(b, mraw_a, 3, (macp, macp1)[b % 2], 1)
                if b == 7:
                    lo(At(0))
                if b >= 5:
                    lo_quarter(b - 5, xT)
            lo_quarter(3, xT)

            def riding(n, c0, b0, j0, buf, slot=3):
                with pool.Fori(0, n) as i:
                    for j in range(8):
                        lo(at(c0 + 1 + j, i, 8))
                        if j == j0:
                            mod_scale(i + b0, buf, slot)
                        if j == j0 + 2:
                            mod_add(i + b0, buf, slot)

            riding(4, 0, 8, 3, mraw_a)
            run(33, C0["sp0"] + 1)
            for h in range(2):
                pool.wait_ge(grp, 4 * h + 5)
                riding(2, C0[f"sp{h}"], 12 + 2 * h, 5, mraw_b)
                run(C0[f"sp{h}"] + 17, C0["sp1"] + 1 if h == 0 else C0["gs"] + 1)
            for n, ph in enumerate(("gs", "ga", "wo", "fi")):
                if ph == "fi":
                    for m in range(4, 8):
                        lo_quarter(m, x1)
                riding(2, C0[ph], 16 + 2 * n, 4, mraw_b, 1)
            run(C0["fi"] + 17, CHUNKS)

        @block.tensor
        def _(pe):
            def chunk(c, e, rhs, nk=16, start=True, stop=True, n=S):
                if start and (e.terms or e.base >= 2):
                    pe.wait_ge(evac, e.times(1, -1))
                acc = accp[:, e.slot(2), 0:n]
                for h in range(2):
                    pe.wait_ge(lo_b if h else lo_a, c.times(1, 1))
                    for k in range(8 * h, min(nk, 8 * h + 8)):
                        xh, xl = rhs(k)
                        wh, wl = whi[:, c.slot(2), k, :], wlo[:, c.slot(2), k, :]
                        first = start and k == 0
                        last = stop and k == nk - 1
                        pe.matmul(acc, wh, xh, start=first, stop=False)
                        pe.matmul(acc, wh, xl, start=False, stop=False)
                        mm = pe.matmul(acc, wl, xh, start=False, stop=last)
                    mm.then_inc(used, 1)

            def acts(k):
                return act_hi[:, k, :], act_lo[:, k, :]

            def mod_block(b, mc=None, mp=None):
                pe.wait_ge(macc_ok, b + 1)
                pe.wait_ge(modp_used, b + 1)
                mc, mp = mc or macc, mp or macp
                if not (isinstance(b, int) and b == 0):
                    pe.wait_ge(mod_ok, b)
                for j in range(4):
                    pe.matmul(pw[:, 5, j:j + 1], mc[:, j * P:(j + 1) * P], ones[:, 0:1], start=True, stop=False)
                    mm = pe.matmul(pw[:, 5, j:j + 1], mp[:, j * P:(j + 1) * P], ones[:, 0:1], start=False, stop=True)
                mm.then_inc(mod_mm, 1)

            def first_chunk(c, e, n):
                def rhs(k):
                    if k % 4 == 0:
                        pe.wait_ge(quarter_lo, 4 * n + k // 4 + 1)
                    return acts(k)
                chunk(c, e, rhs)

            def rms(n, src):
                pe.wait_ge(rq, n)
                for k in range(DT):
                    mm = pe.matmul(pw[:, 4, 0:S], ones[:, :], src[:, k, :], start=k == 0, stop=k == DT - 1)
                mm.then_inc(rm, 1)

            pe.wait_ge(ones_ok, 1)
            rms(1, sqT)
            for b in range(NMOD1):
                mod_block(b, (macc, macc1)[b % 2], (macp, macp1)[b % 2])
            first_chunk(At(0), At(0), 0)

            def qkv_part(i):
                for j in range(8):
                    if not (isinstance(i, int) and j == 0):
                        chunk(at(j, i, 8), at(j, i, 8), acts)
                    if j == 7:
                        mod_block(i + 8)

            qkv_part(0)
            with pe.Fori(1, 4) as i:
                qkv_part(i)
            for c in range(32, 37):
                chunk(At(c), At(c), acts)

            pe.wait_ge(oneh_in, 16)
            pe.wait_ge(mod_ok, 12)
            for g in range(3):
                mm = pe.matmul(pw[0:4, g, :], C("rel", 4 * g, 4)[0:33, :], oneh[0:33, g, :], start=True, stop=True)
            mm.then_inc(brow_mm, 1)
            pe.wait_ge(evac, 36)
            for n in range(6):
                if n >= 2:
                    pe.wait_ge(tp_ev, n - 1)
                for m in range(2):
                    for t in range(2):
                        mm = pe.transpose(pw[:, 4 + n % 2, (2 * m + t) * P:(2 * m + t + 1) * P],
                                          qkv[:, 24 + 2 * n + m, t * P:(t + 1) * P], ident)
                mm.then_inc(tp_mm, 1)

            def logits(u):
                j, q = UNITS[u]
                nk = P * (q + 1)
                if u == 0:
                    pe.wait_ge(brow_ev, 1)
                else:
                    pe.wait_ge(aA, u)
                flat = pw[:, 0:2, :].rearrange("p b n -> p (b n)")
                for g in range(3):
                    mm = pe.matmul(flat[:, g * S:g * S + nk], qkv[:, 4 * g + j, q * P:(q + 1) * P],
                                   qkv[:, 12 + 4 * g + j, 0:nk], start=True, stop=True)
                mm.then_inc(aL, 1)

            def turn(u):
                j, q = UNITS[u]
                pe.wait_ge(aB, u + 1)
                if u:
                    pe.wait_ge(aC, u)
                flat = pw[:, 2:4, :].rearrange("p b n -> p (b n)")
                for g in range(3):
                    for t in range(q + 1):
                        mm = pe.transpose(flat[:, (2 * g + t) * P:(2 * g + t + 1) * P],
                                          lgt[:, u % 2, g, t * P:(t + 1) * P], ident)
                mm.then_inc(aT, 1)

            def values(u):
                j, q = UNITS[u]
                pe.wait_ge(aC, u + 1)
                if u:
                    pe.wait_ge(aF, u)
                else:
                    pe.wait_ge(tp_ev, 6)
                n = 0
                for g in range(3):
                    for t in range(q + 1):
                        n += 1
                        mm = pe.matmul(pw[:, 4, 0:P], vnat[:, t, 4 * g + j, :], pT[:, u % 2, 2 * g + t, :],
                                       start=n == 1, stop=n == 3 * (q + 1))
                mm.then_inc(aO, 1)

            logits(0)
            for u in range(8):
                if u + 1 < 8:
                    logits(u + 1)
                if u:
                    values(u - 1)
                turn(u)
            values(7)
            pe.wait_ge(dt_ex, 1)
            pe.wait_ge(aA, 8)
            for t in range(2):
                pe.transpose(pw[:, 0, 64 * t:64 * t + 64], dts[:, 0, t * P:(t + 1) * P], ident[0:64, 0:64])
                pe.transpose(pw[:, 0, 128 + 64 * t:192 + 64 * t], dts[:, 1, t * P:(t + 1) * P], ident[0:64, 0:64])
            pe.transpose(pw[:, 0, 256:320], dts[:, 2, 0:P], ident[0:64, 0:64]).then_inc(dt_mm, 1)

            def group(i, h, gg):
                g = at(4 * h + gg, i, 2)
                ph = f"ssm{h}"
                bc, x = bct[:, gg], xs[:, gg]
                for j in range(10):
                    chunk(at(C0[ph] + 10 * gg + j, i, 20), at(E0[ph] + 10 * gg + j, i, 20), acts)
                    if j == 2:
                        pe.wait_ge(silu_d, g.times(6, 2 + 2))
                        pe.wait_ge(cb_ev, g.times(1, 1))
                        pe.wait_ge(y_ev, g.times(4, 1))
                        for t in range(2):
                            pe.matmul(pw[:, 0, t * P:(t + 1) * P], bc[:, 0, t * P:(t + 1) * P],
                                      bc[:, 1, t * P:(t + 1) * P], start=True, stop=True)
                        pe.transpose(pw[:, 0, 256:384], bc[:, 0, 0:P], ident).then_inc(cb_mm, 1)
                    if 4 <= j < 8:
                        t = j - 4
                        pe.wait_ge(silu_d, g.times(6, 2 + 3 + t))
                        pe.wait_ge(xt_ev, g.times(4, t + 1))
                        for q in range(2):
                            mm = pe.transpose(pw[:, 5 if t % 2 else 1, q * P:(q + 1) * P],
                                              x[:, t, q * P:(q + 1) * P], ident)
                        mm.then_inc(xt_mm, 1)
                    if j == 8:
                        pe.wait_ge(xdd_ok, g.times(1, 1))
                        pe.wait_ge(s0_ev, g.times(1, 1))
                        pe.matmul(pw[:, 2, :], bnat[:, :], xdd[:, :], start=True, stop=True).then_inc(s0_mm, 1)
                pe.wait_ge(m_ok, g.times(1, 1))
                pe.wait_ge(ce_ok, g.times(1, 1))
                pe.wait_ge(s0_ev, g.times(1, 2))
                pe.wait_ge(y_ev, g.times(4, 1))
                for t in range(4):
                    for r in range(2):
                        hh = 2 * t + r
                        o = pw[64 * r:64 * r + 64, YB[t], 0:S]
                        hc = slice(hh * 64, hh * 64 + 64)
                        pe.matmul(o[:, 0:P], xdt[:, 0, hc], dec[:, hh, 0, :], start=True, stop=True)
                        pe.matmul(o[:, P:S], xdt[:, 1, hc], dec[:, hh, 1, :], start=True, stop=False)
                        mm = pe.matmul(o[:, P:S], st0[:, hc], acb[:, hh, 1, :], start=False, stop=True)
                    mm.then_inc(y_mm, 1)
                for t in range(4):
                    pe.wait_ge(sq_ok, g.times(4, t + 1))
                    pe.matmul(pw[:, 5, 0:S], ones[:, :], sq[:, :], start=t == 0, stop=t == 3).then_inc(ssq_mm, 1)

            def eight(ph, b0, rhs):
                with pe.Fori(0, 2) as i:
                    for j in range(8):
                        chunk(at(C0[ph] + j, i, 8), at(E0[ph] + j, i, 8), rhs)
                        if j == 7:
                            mod_block(i + b0)

            def ys(k):
                return y_hi[:, k, :], y_lo[:, k, :]

            for h in range(2):
                with pe.Fori(0, 2) as i:
                    group(i, h, 0)
                    group(i, h, 1)
                pe.wait_ge(grp, 4 * h + 5)

                eight(f"sp{h}", 12 + 2 * h, ys)
                pe.wait_ge(mod_ok, 14 + 2 * h)

            for c in range(4):
                for h in range(2):
                    e = E0["ap"] + 2 * c + h
                    pe.wait_ge(evac, e - 1)
                    pe.wait_ge(lo_b if h else lo_a, C0["ap"] + c + 1)
                    for m in range(2):
                        for k in range(4):
                            kk, s2 = 8 * h + 4 * m + k, (C0["ap"] + c) % 2
                            acc = accp[:, e % 2, m * S:(m + 1) * S]
                            pe.matmul(acc, whi[:, s2, kk, :], att_hi[:, k, :], start=k == 0, stop=False)
                            pe.matmul(acc, whi[:, s2, kk, :], att_lo[:, k, :], start=False, stop=False)
                            mm = pe.matmul(acc, wlo[:, s2, kk, :], att_hi[:, k, :], start=False, stop=k == 3)
                    mm.then_inc(used, 1)
            eight("gs", 16, acts)
            eight("ga", 18, acts)
            pe.wait_ge(acts_ok, 2)
            eight("wo", 20, lambda k: (mg_hi[:, k, :], mg_lo[:, k, :]))
            rms(2, sq1)
            first_chunk(At(C0["fi"]), At(E0["fi"]), 1)
            for j in range(1, 8):
                chunk(At(C0["fi"] + j), At(E0["fi"] + j), acts)
            mod_block(22)
            for j in range(8, 16):
                chunk(At(C0["fi"] + j), At(E0["fi"] + j), acts)
            mod_block(23)
            with pe.Fori(4, FF_T // 2) as i:
                for j in range(4):
                    chunk(at(C0["fi"] + j, i, 4), at(E0["fi"] + j, i, 4), acts)
            pe.wait_ge(acts_ok, 4)
            with pe.Fori(0, 8) as i:
                for m in range(2):
                    for q in range(4):
                        chunk(at(C0["fo"] + 4 * m + q, i, 8), at(E0["fo"] + m, i, 2),
                              lambda k, q=q: (hid_hi[:, KFO * q + k, :], hid_lo[:, KFO * q + k, :]),
                              nk=KFO, start=q == 0, stop=q == 3)


            rms(3, sqF)
            rms(4, sqF)
            pe.wait_ge(acts_ok, 6)

            def loop4(ph, n, rhs=acts):
                with pe.Fori(0, n) as i:
                    for j in range(4):
                        chunk(at(C0[ph] + j, i, 4), at(E0[ph] + j, i, 4), rhs)

            def halves(c, e, rhs, kts, ms=1):
                for h in range(2):
                    pe.wait_ge(lo_b if h else lo_a, c.times(1, 1))
                    n = 8 // kts // ms
                    for r in range(n):
                        eh = e + (h * n + r)
                        pe.wait_ge(evac, eh.times(1, -1))
                        for m in range(ms):
                            for k in range(kts):
                                kk = 8 * h + (r * ms + m) * kts + k
                                xh, xl = rhs(k)
                                acc = accp[:, eh.slot(2), m * S:(m + 1) * S]
                                pe.matmul(acc, whi[:, c.slot(2), kk, :], xh, start=k == 0, stop=False)
                                pe.matmul(acc, whi[:, c.slot(2), kk, :], xl, start=False, stop=False)
                                mm = pe.matmul(acc, wlo[:, c.slot(2), kk, :], xh, start=False, stop=k == kts - 1)
                    mm.then_inc(used, 1)

            def branch(ph, n):
                if n == 7:
                    pe.wait_ge(acts_ok, n)

                def half(i):
                    for j in range(4):
                        def rhs(k):
                            if n > 7 and isinstance(i, int) and j == 0 and k % 4 == 0:
                                pe.wait_ge(yb_ok, 2 * (n - 8) + k // 4 + 1)
                            return yb_hi[:, k, :], yb_lo[:, k, :]
                        halves(at(C0["wb" + ph] + j, i, 4), at(E0["wb" + ph] + 2 * j, i, 8), rhs, 8)

                half(0)
                with pe.Fori(1, 2) as i:
                    half(i)
                loop4("mg" + ph, 4)

            loop4("lx", 2)
            for i in range(2):
                pe.wait_ge(uc_ok, 1)
                pe.wait_ge(wab_in, 16 * (i + 1))
                if i:
                    pe.wait_ge(lru_g, i)
                for t in range(4):
                    for w in range(2):
                        mm = pe.matmul(pw[:, t, w * S:(w + 1) * S], wabs[:, t, w, :], uc[:, 4 * i + t, :], start=True, stop=True)
                mm.then_inc(lru_mm, 1)
                for j in range(4):
                    chunk(At(C0["lg"] + 4 * i + j), At(E0["lg"] + 4 * i + j), acts)
            branch("a", 7)
            chunk(At(C0["bf"]), At(E0["bf"]), acts)
            def head_sum(n, cols=512):
                pe.wait_ge(hq, n + 1)
                if n:
                    pe.wait_ge(hv, n)
                else:
                    pe.wait_ge(gn_ok, 1)
                src = hq_[:, n % 2, :] if cols == 512 else kcs[:, 0, :]
                pe.matmul(pw[:, 5, 0:cols], ones[:, :], src, start=True, stop=True).then_inc(hm, 1)

            def transposes(srcs, n0):
                for n in range(len(srcs) // 2):
                    if n0 + n >= 2:
                        pe.wait_ge(tp_ev, n0 + n - 1)
                    for m in range(2):
                        for t in range(2):
                            mm = pe.transpose(pw[:, 2 + (n0 + n) % 2, (2 * m + t) * P:(2 * m + t + 1) * P],
                                              srcs[2 * n + m][:, t * P:(t + 1) * P], ident)
                    mm.then_inc(tp_mm, 1)

            for c in range(20):
                chunk(At(C0["nq"] + c), At(E0["nq"] + c), acts)
                if c == 1:
                    pe.wait_ge(zf_ok, 2)
                    for t in range(2):
                        mm = pe.transpose(pw[:, 5, t * P:(t + 1) * P], zf[:, t * P:(t + 1) * P], ident)
                    mm.then_inc(gn_mm, 1)
                if c - 2 in NSA_N:
                    head_sum(NSA_N.index(c - 2))
            pe.wait_ge(kp_ok, 1)
            for j in range(8):
                x, c, e = j // 4, C0["cmp"] + j, E0["cmp"] + j // 4
                acc = accp[0:30, e % 2, 0:256]
                for h in range(2):
                    pe.wait_ge(lo_b if h else lo_a, c + 1)
                    if j % 4 == 0 and h == 0:
                        pe.wait_ge(evac, e - 1)
                    for k in range(4 * h, 4 * h + 4):
                        kk = 8 * (j % 4) + k
                        wh, wl = (w[:, c % 2, 2 * k:2 * k + 2, :].rearrange("p a n -> p (a n)") for w in (whi, wlo))
                        pe.matmul(acc, kp_hi[:, x, kk, :], wh, start=kk == 0, stop=False)
                        pe.matmul(acc, kp_lo[:, x, kk, :], wh, start=False, stop=False)
                        mm = pe.matmul(acc, kp_hi[:, x, kk, :], wl, start=False, stop=kk == 31)
                    mm.then_inc(used, 1)
            pe.wait_ge(evac, E0["cmp"] + 2)
            for n in range(4):
                mm = pe.transpose(pw[:, 4, 30 * n:30 * n + 30], hct[0:30, n // 2, n % 2 * P:n % 2 * P + P], ident[0:30, 0:30])
            mm.then_inc(hct_mm, 1)
            chunk(At(C0["ng"]), At(E0["ng"]), acts)
            pe.wait_ge(cw2_in, 16)
            pe.wait_ge(hct_ev, 1)
            for m in range(2):
                pe.matmul(pw[:, 0, 0:30], cw2s[:, 0, m, :], hc[:, 0, m, :], start=m == 0, stop=m == 1)
            for x in range(2):
                for m in range(2):
                    mm = pe.matmul(pw[0:15, 1, x * P:(x + 1) * P], hc[:, 1, m, 15 * x:15 * x + 15], cw2s[:, 1, m, :], start=m == 0, stop=m == 1)
            mm.then_inc(kc_mm, 1)
            transposes([nk[:, n, :] for n in (14, 15, 18, 19)], 6)
            chunk(At(C0["ng"] + 1), At(E0["ng"] + 1), acts)
            head_sum(6, 30)

            def att_logits(b):
                kind, h0, q = BATCH[b]
                n = P * (q + 1) if kind else 15
                if b in (0, NSA_B):
                    pe.wait_ge(hn_ok, 7 if b == 0 else 15)
                    pe.wait_ge(tp_ev, 8 if b == 0 else 12)
                if b:
                    pe.wait_ge(aA, 8 + b)
                for r in range(4):
                    h = h0 + r
                    kv = h0 // 4
                    o = pw[:, r // 2, (r % 2) * S:(r % 2) * S + n]
                    qq = (fx if kind == 3 else nk)[:, h, q * P:(q + 1) * P]
                    kk = (kcT[:, 15 * kv:15 * kv + 15], nk[:, 12 + kv, 0:n], nk[:, 16 + kv, 0:n], fx[:, 8 + h, 0:n])[kind]
                    mm = pe.matmul(o, qq, kk, start=True, stop=kind != 3)
                    if kind == 3:
                        mm = pe.matmul(o, nudge[:, h:h + 1].to_broadcast([P, P]), zf[:, 0:n], start=False, stop=True)
                mm.then_inc(aL, 1)

            def att_turn(b):
                kind, h0, q = BATCH[b]
                pe.wait_ge(aB, 8 + b + 1)
                pe.wait_ge(aC, 8 + b)
                src = (lg3 if kind == 3 else lg2)[:, b % 2]
                for r in range(4):
                    for t in range(q + 1 if kind else 1):
                        rows, n = (P, P) if kind else (15, 15)
                        mm = pe.transpose(pw[0:rows, 2 + r // 2, (2 * (r % 2) + t) * P:(2 * (r % 2) + t + 1) * P],
                                          src[:, r, t * P:t * P + n], ident)
                mm.then_inc(aT, 1)

            def att_values(b):
                kind, h0, q = BATCH[b]
                kv = h0 // 4
                pe.wait_ge(aC, 8 + b + 1)
                opens = kind in (0, 3)
                if opens:
                    pe.wait_ge(aF, 8 + sum(x < b for x in CLOSED))
                for r in range(4):
                    o = pw[:, 4, r * P:(r + 1) * P]
                    ts = range(q + 1 if kind else 1)
                    for t in ts:
                        if kind == 0:
                            l, x = vcn[0:15, kv, :], pT2[0:15, b % 2, 2 * r, :]
                        elif kind == 3:
                            l, x = vn3[:, t, h0 + r, :], pT3[:, b % 2, 2 * r + t, :]
                        else:
                            l, x = vn2[:, t, 2 * (kind - 1) + kv, :], pT2[:, b % 2, 2 * r + t, :]
                        mm = pe.matmul(o, l, x, start=opens and r == 0 and t == 0,
                                       stop=kind >= 2 and t == q and r == 3, skip_group_check=True)
                mm.then_inc(aO, 1)

            def attention(b0, b1, ph):
                att_logits(b0)
                for b in range(b0, b1):
                    if b + 1 < b1:
                        att_logits(b + 1)
                    rides = RIDES.get(b, [])
                    for c in rides[1:]:
                        chunk(At(C0[ph] + c - 1), At(E0[ph] + c - 1), acts)
                    if b > b0:
                        att_values(b - 1)
                    for c in rides[-1:]:
                        chunk(At(C0[ph] + c), At(E0[ph] + c), acts)
                    att_turn(b)
                att_values(b1 - 1)

            attention(0, NSA_B, "ng")
            branch("b", 8)
            for c in range(25):
                if c < 24:
                    chunk(At(C0["fx"] + c), At(E0["fx"] + c), acts)
                if 2 <= c < 18 and c % 2 == 0:
                    head_sum(6 + c // 2)
                if c >= 18 and c % 2 == 0:
                    pe.wait_ge(evac, E0["fx"] + c)
                    transposes([fx[:, c - 2, :], fx[:, c - 1, :]], c // 2 - 1)
            attention(NSA_B, len(BATCH), "fg")
            branch("c", 9)
            pe.wait_ge(acts_ok, 10)
            loop4("w2", 4, lambda k: (m2_hi[:, k, :], m2_lo[:, k, :]))
            pe.wait_ge(p_ok, 1)
            for c in range(2):
                halves(At(C0["ple"] + c), At(E0["ple"] + 4 * c), lambda k: (p_hi[:, k, :], p_lo[:, k, :]), 2, ms=2)
            pe.wait_ge(h_ok, 1)
            rms(5, sqF)
            loop4("pg", 4)

        @block.scalar
        def _(act):
            def split_hi(c):
                if not c.terms and c.base >= NRUN:
                    return
                act.wait_ge(raw_in[c.slot(4)], c.round(4, 16, 16))
                for h in range(2):
                    if c.terms or c.base >= 2:
                        act.wait_ge(used, c.times(2, h - 3))
                    act.activation(whi[:, c.slot(2), 8 * h:8 * h + 8, :], raw[:, c.slot(4), 8 * h:8 * h + 8, :],
                                   ACT.Copy).then_inc(hi_done, 1)

            def take(c, e, out, func=ACT.Copy, n=S, rows=P, **kw):
                act.wait_ge(used, c.times(2, 2))
                act.activation(out, accp[0:rows, e.slot(2), 0:n], func, **kw).then_inc(evac, 1)

            def root(n, o, v):
                act.wait_ge(rv, n)
                act.activation(o, v, ACT.Sqrt).then_inc(rs, 1)

            act.wait_ge(cst_in, 16)
            act.activation(cact[:, :], C("c", 0, 16), ACT.Silu).then_inc(cact_ok, 1)
            act.wait_ge(x_in, 16)
            act.activation(sqT[:, :, :], xT[:, :, :], ACT.Square).then_inc(rq, 1)
            for n in range(2):
                act.activation(nudge[:, n:n + 1], C("c", n, 1), ACT.Copy).then_inc(silu_d, 1)
            act.activation(nudge[:, 2:3], C("c"), ACT.Copy).then_inc(s0_ev, 1)
            root(1, rstd[:, :], sqT[:, 0, :])

            def hi_quarter(n, src):
                act.wait_ge(quarter, n + 1)
                t = slice(4 * (n % 4), 4 * (n % 4) + 4)
                act.activation(act_hi[:, t, :], src[:, t, :], ACT.Copy).then_inc(quarter_hi, 1)

            hi_quarter(0, xT)
            hi_quarter(1, xT)
            split_hi(At(0))
            hi_quarter(2, xT)
            hi_quarter(3, xT)

            def qkv_part(i):
                for j in range(4):
                    c = at(j, i, 4)
                    split_hi(c + 1)
                    take(c, c, qkv[:, one(i * 4 + j), :])

            qkv_part(0)
            with act.Fori(1, 9) as i:
                qkv_part(i)
            act.wait_ge(mod_ok, 12)
            act.dma_start(oneh[:, :, :], onehot).then_inc(oneh_in, 16)
            split_hi(At(37))
            act.wait_ge(mod_ok, 12)
            take(At(36), At(36), dtr[:, :], ACT.Identity, rows=64, bias=C("dtb")[0:64, :])
            act.wait_ge(spx, 1)
            act.activation(dts[:, 2, :], dts[:, 1, :], ACT.Exp, scale=-1.0).then_inc(spe, 1)
            act.activation(aneg[0:64, :], C("alog")[0:64, :], ACT.Exp).then_inc(spe, 1)
            act.wait_ge(brow_mm, 1)
            for g in range(3):
                ins = act.activation(brow[:, g, :], pw[0:4, g, :], ACT.Copy)
            ins.then_inc(brow_ev, 1)
            act.wait_ge(brow_ev, 1)
            act.dma_start(br_d, brow[:, :, :].rearrange("j g n -> j (g n)")).then_inc(brow_st, 16)
            for n in range(6):
                act.wait_ge(tp_mm, n + 1)
                act.activation(vnat[:, :, 2 * n:2 * n + 2, :].rearrange("p t m d -> p m t d"),
                               pw[:, 4 + n % 2, :].rearrange("p (m t d) -> p m t d", m=2, t=2),
                               ACT.Copy).then_inc(tp_ev, 1)

            def bias(u):
                j, q = UNITS[u]
                nk = P * (q + 1)
                src = bass.AP(tensor=bw_d.tensor, offset=bw_d.offset + j * P * 1536 + 255 - P * q,
                              ap=[[1535, P], [512, 3], [1, nk]])
                act.dma_start(biasT[:, u % 2, :, 0:nk], src).then_inc(bias_in[u % 2], 16)

            act.wait_ge(brow_st, 16)
            for j in range(4):
                act.dma_start(bw_d[j], br_d[j:j + 1, :].to_broadcast([P, 1536])).then_inc(brow_st, 16)
            act.wait_ge(brow_st, 80)
            bias(0)
            for u in range(8):
                if u + 1 < 8:
                    if u:
                        act.wait_ge(aA, u)
                    bias(u + 1)
                j, q = UNITS[u]
                act.wait_ge(aA, u + 1)
                act.activation(lgt[:, u % 2, 0:3, 0:P * (q + 1)], lgt[:, u % 2, 0:3, 0:P * (q + 1)], ACT.Exp,
                               bias=nmx[:, u % 2, 0:1], accum_out=sums[:, u % 2, 0:1]).then_inc(aX, 1)
                act.wait_ge(aT, u + 1)
                if u >= 2:
                    act.wait_ge(aO, u - 1)
                flat = pw[:, 2:4, :].rearrange("p b n -> p (b n)")
                act.activation(pT[:, u % 2, 0:6, :].rearrange("p (g t) n -> p g t n", t=2)[:, :, 0:q + 1, :],
                               flat[:, 0:768].rearrange("p (g t n) -> p g t n", g=3, t=2)[:, :, 0:q + 1, :],
                               ACT.Copy).then_inc(aC, 1)
            act.wait_ge(ac_ok, 1)
            act.activation(dts[:, 2, 0:P], dts[:, 2, 0:P], ACT.Exp).then_inc(dt_ex, 1)
            act.dma_start(ac_d.rearrange("g (r n) -> (g r) n", r=8), dts[:, 1, :]).then_inc(ac_st, 16)
            act.wait_ge(ac_st, 16)

            def group(i, h, gg):
                g = at(4 * h + gg, i, 2)
                ph = f"ssm{h}"
                act.wait_ge(y_ev, g.times(4, 1))
                act.dma_start(acb[:, :, :, :].rearrange("p r t n -> p (r t n)"),
                              ac_d[one(g.times(1)), :].to_broadcast([P, 2048])).then_inc(acb_in, 16)
                for j in range(10):
                    c, e = at(C0[ph] + 10 * gg + j, i, 20), at(E0[ph] + 10 * gg + j, i, 20)
                    split_hi(c + 1)
                    if 1 <= j <= 6:
                        act.wait_ge(conv_d, g.times(6, 2 + j))
                        o = bct[:, gg, j - 1, :] if j <= 2 else xs[:, gg, j - 3, :]
                        act.activation(o, cv[:, (j - 1) % 2, :], ACT.Silu).then_inc(silu_d, 1)
                    if j == 4:
                        act.wait_ge(dec_in, g.times(1, 1))
                        act.activation(dec[:, :, :, :], dec[:, :, :, :], ACT.Exp).then_inc(dec_ex, 1)
                        act.activation(acb[:, :, 1, :], acb[:, :, 1, :], ACT.Exp).then_inc(dec_ex, 1)
                    if j == 9:
                        act.wait_ge(s0_mm, g.times(1, 1))
                        act.activation(st0[:, :], pw[:, 2, :], ACT.Copy).then_inc(s0_ev, 1)
                    if j < 6:
                        act.wait_ge(conv_d, g.times(6, 1 + j))
                        take(c, e, ub[:, j % 2, 3:259])
                    else:
                        if j == 6:
                            act.wait_ge(grp, g.times(1, 1))
                        take(c, e, sz[:, j - 6, :], ACT.Silu)
                for t in range(4):
                    act.wait_ge(y_ev, g.times(4, t + 2))
                    if t:
                        act.wait_ge(ssq_mm, g.times(4, t))
                    act.activation(sq[:, :], sz[:, t, :], ACT.Square).then_inc(sq_ok, 1)
                act.wait_ge(ssq_v, g.times(1, 1))
                act.activation(rstd[:, :], cv[:, 0, :], ACT.Sqrt).then_inc(ssq_r, 1)

            def to_tm(ph, j, i, stride, base, c, e, buf, **kw):
                idx = at(POST0[ph] + base, i, stride)
                act.wait_ge(post, idx.times(1, 1))
                take(c, e, buf[:, idx.slot(4), :], **kw)

            for h in range(2):
                if h:
                    act.wait_ge(mod_ok, 14)
                with act.Fori(0, 2) as i:
                    group(i, h, 0)
                    group(i, h, 1)
                ph = f"sp{h}"
                with act.Fori(0, 4) as i:
                    for j in range(4):
                        c, e = at(C0[ph] + j, i, 4), at(E0[ph] + j, i, 4)
                        split_hi(c + 1)
                        if h == 0:
                            take(c, e, accS[:, one(i * 4 + j), :])
                        else:
                            to_tm(ph, j, i, 4, j, c, e, tm)
            for c in range(4):
                split_hi(At(C0["ap"] + c + 1))
                for h in range(2):
                    act.wait_ge(used, 2 * (C0["ap"] + c) + h + 1)
                    act.activation(accA[:, 4 * c + 2 * h:4 * c + 2 * h + 2, :],
                                   accp[:, (E0["ap"] + 2 * c + h) % 2, :].rearrange("p (m n) -> p m n", m=2),
                                   ACT.Copy).then_inc(evac, 1)

            def temps(ph, n, buf, func_of, last=False):
                def four(i):
                    for j in range(4):
                        c, e = at(C0[ph] + j, i, 4), at(E0[ph] + j, i, 4)
                        split_hi(c + 1)
                        to_tm(ph, j, i, 4, j, c, e, buf, func=func_of(j))
                with act.Fori(0, n - last) as i:
                    four(i)
                if last:
                    four(n - 1)

            temps("gs", 4, tm, lambda j: ACT.Sigmoid)
            temps("ga", 4, tm, lambda j: ACT.Sigmoid)
            act.wait_ge(acts_ok, 2)
            act.dma_start(x1[:, :, :], xt).then_inc(x_in, 16)
            temps("wo", 4, tm, lambda j: ACT.Copy)
            act.wait_ge(post, 4 + POST0["fi"])
            act.dma_start(x1_d, x1[:, :, :].rearrange("p k n -> p (k n)")).then_inc(x1_st, 16)
            act.activation(sq1[:, :, :], x1[:, :, :], ACT.Square).then_inc(rq, 1)
            root(2, rstd[:, :], sq1[:, 0, :])
            for n in range(4, 8):
                hi_quarter(n, x1)
            act.wait_ge(acts_ok, 3)
            temps("fi", FF_T // 2, tf, lambda j: ACT.Copy if j % 2 else ACT.Silu)
            act.wait_ge(acts_ok, 4)
            act.wait_ge(used, 2 * C0["fo"])
            act.wait_ge(x1_st, 16)
            act.dma_start(x1r[:, :, :].rearrange("p k n -> p (k n)"), x1_d).then_inc(x1_in, 16)
            with act.Fori(0, 8) as i:
                for m in range(2):
                    for q in range(4):
                        c = at(C0["fo"] + 4 * m + q, i, 8)
                        split_hi(c + 1)
                    e = at(E0["fo"] + m, i, 2)
                    idx = at(POST0["fo"] + m, i, 2)
                    act.wait_ge(post, idx.times(1, 3))
                    take(c, e, tf[:, idx.slot(2), :])


            act.wait_ge(post, 4 + POST0["lx"])
            act.activation(sqF[:, :, :], x1r[:, :, :], ACT.Square).then_inc(rq, 1)
            root(3, rstd[:, :], sqF[:, 0, :])
            act.wait_ge(acts_ok, 5)
            act.activation(sqF[:, :, :], x2T[:, :, :], ACT.Square).then_inc(rq, 1)
            root(4, rstd[:, :], sqF[:, 0, :])
            act.wait_ge(lam_x, 1)
            act.activation(lcon[:, 2, :], lcon[:, 1, :], ACT.Exp, scale=-1.0).then_inc(spe, 1)

            def biased(ph, n, dst, func, lead=True, ring=4):
                with act.Fori(0, n) as i:
                    for j in range(4):
                        c, e = at(C0[ph] + j, i, 4), at(E0[ph] + j, i, 4)
                        split_hi(c + 1)
                        idx = at(POST0[ph] + j, i, 4) if ph in POST0 else None
                        if idx is not None:
                            act.wait_ge(post, idx.times(1, 5 - ring))
                        take(c, e, dst(i, j, idx.slot(4) if idx is not None else 0), func, bias=Cd("b2", i * 4 + (B2[ph] + j)))

            def branch(ph):
                with act.Fori(0, 2) as i:
                    for j in range(4):
                        c = at(C0["wb" + ph] + j, i, 4)
                        split_hi(c + 1)
                        for h in range(2):
                            e = at(E0["wb" + ph] + 2 * j + h, i, 8)
                            act.wait_ge(used, c.times(2, h + 1))
                            act.activation(proj[:, one(i * 8 + (2 * j + h)), :], accp[:, e.slot(2):e.slot(2) + 1, 0:S], ACT.Copy).then_inc(evac, 1)
                biased("mg" + ph, 4, lambda i, j, s: tm2[:, s, :], ACT.Sigmoid)

            act.wait_ge(pad_ok, 1)
            biased("lx", 2, lambda i, j, s: ub2[:, j % 2, 3:259], ACT.Identity, ring=2)
            for i in range(2):
                if i:
                    act.wait_ge(lru_mm, i)
                act.dma_start(wabs[:, :, :, :], wab[:, 4 * i:4 * i + 4]).then_inc(wab_in, 16)
                act.wait_ge(lru_mm, i + 1)
                if i:
                    act.wait_ge(lru_y, i)
                for t in range(4):
                    act.activation(lr[:, t, :], pw[:, t, 0:S], ACT.Sigmoid, bias=C("ba", 4 * i + t))
                    ins = act.activation(li[:, t, :], pw[:, t, S:2 * S], ACT.Sigmoid, bias=C("bx", 4 * i + t))
                ins.then_inc(lru_g, 1)
                for j in range(4):
                    c, e = At(C0["lg"] + 4 * i + j), At(E0["lg"] + 4 * i + j)
                    split_hi(c + 1)
                    if j == 1:
                        act.wait_ge(lru_l, i + 1)
                        act.activation(lt[:, :, :], lr[:, :, :], ACT.Tanh)
                        act.activation(la[:, :, :], lr[:, :, :], ACT.Exp, scale=-1.0).then_inc(lru_e, 1)
                    if j == 3:
                        act.wait_ge(lru_w, i + 1)
                        act.activation(lw[:, :, :], lw[:, :, :], ACT.Sqrt).then_inc(lru_q, 1)
                    take(c, e, gl[:, j, :], ACT.Silu, bias=C("b2", B2["lg"] + 4 * i + j))
            act.wait_ge(acts_ok, 7)
            branch("a")
            c, e = At(C0["bf"]), At(E0["bf"])
            split_hi(c + 1)
            take(c, e, zf[:, :], ACT.Identity, bias=C("b2", B2["bf"]))
            split_hi(c + 2)
            act.wait_ge(spx, 2)
            act.activation(sft[32:40, 1, :], sft[32:40, 0, :], ACT.Exp, scale=-1.0).then_inc(spe, 1)
            act.wait_ge(evac, E0["bf"] + 1)
            act.activation(zf[0:24, :], zf[0:24, :], ACT.Sigmoid).then_inc(zf_ok, 1)

            def head_squares(n, src):
                if n >= 2:
                    act.wait_ge(hm, n - 1)
                act.activation(hq_[:, n % 2, :], src, ACT.Square).then_inc(hq, 1)

            def head_root(n, o, v):
                act.wait_ge(hv, n + 1)
                if n:
                    act.wait_ge(hn_ok, n)
                act.activation(o, v, ACT.Sqrt).then_inc(hr, 1)

            two = lambda t, n: t[:, n:n + 2, :].rearrange("p k n -> p (k n)")
            for c in range(20):
                if c:
                    split_hi(At(C0["nq"] + c + 1))
                if c - 3 in NSA_N:
                    head_root(NSA_N.index(c - 3), hr_[:, :], he_[:, :])
                if c - 2 in NSA_N:
                    if c == 2:
                        act.wait_ge(gn_ok, 1)
                    act.wait_ge(evac, E0["nq"] + c)
                    head_squares(NSA_N.index(c - 2), two(nk, c - 2))
                take(At(C0["nq"] + c), At(E0["nq"] + c), nk[:, c, :], ACT.Identity, bias=C("b2", B2["nq"] + c))
            act.dma_start(cw2s[:, :, :, :], cw2).then_inc(cw2_in, 16)
            for j in range(8):
                split_hi(At(C0["cmp"] + j + 1))
                if j % 4 == 3:
                    c, e = C0["cmp"] + j, E0["cmp"] + j // 4
                    take(At(c), At(e), hct[0:30, j // 4, :], ACT.Silu, n=256, rows=30)

            def gate_of(ph, c):
                split_hi(At(C0[ph] + c + 1))
                take(At(C0[ph] + c), At(E0[ph] + c), gate[:, c, :], ACT.Silu, bias=C("b2", B2[ph] + c))

            act.wait_ge(hct_mm, 1)
            act.activation(hc[:, :, :, :].rearrange("p x m n -> p (x m n)"), pw[:, 4, 0:120], ACT.Copy).then_inc(hct_ev, 1)
            gate_of("ng", 0)

            def copy_out(n, dst):
                act.wait_ge(tp_mm, n + 1)
                act.activation(dst.rearrange("p t m d -> p m t d"),
                               pw[:, 2 + n % 2, :].rearrange("p (m t d) -> p m t d", m=2, t=2), ACT.Copy).then_inc(tp_ev, 1)

            act.wait_ge(kc_mm, 1)
            act.activation(kcT[:, :], pw[:, 0, 0:30], ACT.Copy)
            act.activation(kcs[:, 0, :], pw[:, 0, 0:30], ACT.Square).then_inc(hq, 1)
            act.activation(vcn[:, :, :].rearrange("p a n -> p (a n)"), pw[0:15, 1, 0:256], ACT.Copy).then_inc(kc_ev, 1)
            for n in range(2):
                copy_out(6 + n, vn2[:, :, 2 * n:2 * n + 2, :])
            gate_of("ng", 1)
            head_root(6, kcs[:, 1, :], kcs[:, 2, :])

            def attention(b0, b1, ph):
                for b in range(b0, b1):
                    kind, h0, q = BATCH[b]
                    n = P * (q + 1) if kind else 15
                    l = (lg3 if kind == 3 else lg2)[:, b % 2]
                    act.wait_ge(aA, 8 + b + 1)
                    for r in range(4):
                        kw = {"accum_out": sums[:, b % 2, r:r + 1]} if kind else {}
                        ins = act.activation(l[:, r, 0:n], l[:, r, 0:n], ACT.Exp, bias=nmx[:, b % 2, r:r + 1], **kw)
                    ins.then_inc(aX, 1)
                    for c in RIDES.get(b, []):
                        gate_of(ph, c)
                    act.wait_ge(aT, 8 + b + 1)
                    if b - b0 >= 2:
                        act.wait_ge(aO, 8 + b - 1)
                    pt = (pT3 if kind == 3 else pT2)[:, b % 2].rearrange("p (r t) n -> p r t n", t=2)
                    rows, k = (P, q + 1) if kind else (15, 1)
                    act.activation(pt[0:rows, :, 0:k, :],
                                   pw[0:rows, 2:4, :].rearrange("p b (r t n) -> p (b r) t n", r=2, t=2)[:, :, 0:k, :],
                                   ACT.Copy).then_inc(aC, 1)

            attention(0, NSA_B, "ng")
            act.wait_ge(acts_ok, 8)
            branch("b")
            act.wait_ge(post, 4 + POST0["mgc"])
            for c in range(25):
                if c < 24:
                    split_hi(At(C0["fx"] + c + 1))
                if 3 <= c < 19 and c % 2:
                    head_root(7 + (c - 3) // 2, hr_[:, :], he_[:, :])
                if 2 <= c < 18 and c % 2 == 0:
                    act.wait_ge(evac, E0["fx"] + c)
                    head_squares(6 + c // 2, two(fx, c - 2))
                if c >= 19 and c % 2:
                    copy_out(8 + (c - 19) // 2, vn3[:, :, c - 19:c - 17, :])
                if c < 24:
                    take(At(C0["fx"] + c), At(E0["fx"] + c), fx[:, c, :], ACT.Identity, bias=C("b2", B2["fx"] + c))
            copy_out(11, vn3[:, :, 6:8, :])
            attention(NSA_B, len(BATCH), "fg")
            act.wait_ge(acts_ok, 9)
            branch("c")
            act.wait_ge(acts_ok, 10)
            act.dma_start(p_in[:, :, :], pt).then_inc(p_land, 16)
            temps("w2", 4, tm2, lambda j: ACT.Copy)
            for c in range(2):
                split_hi(At(C0["ple"] + c + 1))
                for h in range(2):
                    act.wait_ge(used, 2 * (C0["ple"] + c) + h + 1)
                    for r in range(2):
                        e = E0["ple"] + 4 * c + 2 * h + r
                        m = 8 * c + 4 * h + 2 * r
                        act.activation(eT[:, m:m + 2, :], accp[:, e % 2, :].rearrange("p (m n) -> p m n", m=2), ACT.Copy).then_inc(evac, 1)
            act.wait_ge(evac, E0["pg"])
            act.activation(sqF[:, :, :], eT[:, :, :], ACT.Square).then_inc(rq, 1)
            root(5, rstd[:, :], sqF[:, 0, :])
            temps("pg", 4, tm2, lambda j: ACT.Sigmoid, last=True)

        @block.vector
        def _(dve):
            def split_lo(c):
                if not c.terms and c.base >= NRUN:
                    return
                dve.wait_ge(hi_done, c.times(2, 2))
                dve.tensor_tensor(wlo[:, c.slot(2), 8:16, :], raw[:, c.slot(4), 8:16, :],
                                  whi[:, c.slot(2), 8:16, :].bitcast(F32), ALU.subtract).then_inc(lo_b, 1)

            def pair(hi, lo, src):
                dve.tensor_copy(hi, src)
                dve.drain()
                return dve.tensor_tensor(lo, src, hi.bitcast(F32), ALU.subtract)

            def rms_root(n, ss, v, width, r=None, sems=None):
                r = rstd[:, :] if r is None else r
                sm, sv, sr, tmp, rec = sems
                dve.wait_ge(sm[0], sm[1])
                dve.tensor_scalar(v, ss, 1.0 / width, EPS, ALU.mult, ALU.add)
                dve.drain()
                dve.reciprocal(rec, v).then_inc(sv, 1)
                dve.wait_ge(sr[0], sr[1])
                dve.tensor_tensor(tmp, r, r, ALU.mult)
                dve.drain()
                dve.tensor_tensor(tmp, tmp, v, ALU.mult)
                dve.drain()
                dve.tensor_scalar(tmp, tmp, -0.5, 1.5, ALU.mult, ALU.add)
                dve.drain()
                dve.tensor_tensor(r, r, tmp, ALU.mult)
                dve.drain()

            def mod_piece(b, j, buf, ring=4, acc=None):
                acc = acc or macc
                dve.wait_ge(mod_in[j], b * 16 + 16)
                for k in range(4):
                    a = 4 * j + k
                    if a == 0:
                        ins = dve.tensor_scalar(acc[:, :], buf[:, 0, 0, :], cact[:, 0:1], None, ALU.mult)
                    else:
                        ins = dve.scalar_tensor_tensor(acc[:, :], buf[:, j % ring, k, :], cact[:, a:a + 1],
                                                       acc[:, :], ALU.mult, ALU.add)
                    if k < 3:
                        dve.drain()
                ins.then_inc(mod_used, 1)
                if j < 2:
                    dve.drain()
                else:
                    dve.drain().then_inc(macc_ok, 1)

            def mod_finish(b):
                dve.wait_ge(mod_mm, b + 1)
                dve.tensor_tensor(modT[:, wide(b, 4)], pw[:, 5, 0:4],
                                  cst[:, bass.ds(b * 4 + CO["bmod"], 4)] if not isinstance(b, int) else C("bmod", 4 * b, 4),
                                  ALU.add).then_inc(mod_ok, 1)

            def softplus(x, t, o, n, x_ok=None):
                ax, e, s, s2 = t
                dve.scalar_tensor_tensor(ax, x, -1.0, x, ALU.mult, ALU.max).then_inc(x_ok or spx, 1)
                dve.wait_ge(spe, n)
                dve.tensor_scalar(s, e, 2.0, None, ALU.add)
                dve.drain()
                dve.reciprocal(s, s)
                dve.drain()
                dve.tensor_tensor(s, s, e, ALU.mult)
                dve.drain()
                dve.tensor_tensor(s2, s, s, ALU.mult)
                dve.drain()
                dve.tensor_scalar(e, s2, 1.0 / 15, None, ALU.mult)
                for d in (13, 11, 9, 7, 5, 3):
                    dve.drain()
                    dve.scalar_tensor_tensor(e, e, 1.0 / d, s2, ALU.add, ALU.mult)
                dve.drain()
                dve.scalar_tensor_tensor(e, e, 1.0, s, ALU.add, ALU.mult)
                dve.tensor_scalar(ax, x, 0.0, None, ALU.max)
                dve.drain()
                dve.scalar_tensor_tensor(o, e, 2.0, ax, ALU.mult, ALU.add)
                dve.drain()

            dve.memset(ones[:, :], 1.0).then_inc(ones_ok, 1)
            for s_, n in ((post, 4), (cb_ev, 1), (xt_ev, 2), (y_ev, 1), (grp, 1)):
                for _ in range(n):
                    dve.memset(nudge[:, 4:5], 0.0).then_inc(s_, 1)
                    dve.drain()
            dve.wait_ge(cact_ok, 1)
            rms_root(1, pw[:, 4, 0:S], sqT[:, 1, :], D, sems=((rm, 1), rv, (rs, 1), sqT[:, 2, :], sqT[:, 0, :]))
            dve.tensor_tensor(xT[:, :, :], xT[:, :, :], rstd[:, :].rearrange("p (a n) -> p a n", a=1).to_broadcast([P, DT, S]), ALU.mult)

            def modulate(m, src, gain, norm, sh, sc):
                t = slice(4 * m, 4 * m + 4)
                dve.drain()
                dve.scalar_tensor_tensor(gain[:, t], modT[:, sc + 4 * m:sc + 4 * m + 4], 1.0, norm[:, t], ALU.add, ALU.mult)
                dve.drain()
                for k in range(4 * m, 4 * m + 4):
                    ins = dve.tensor_scalar(src[:, k, :], src[:, k, :], gain[:, k:k + 1], modT[:, sh + k:sh + k + 1],
                                            ALU.mult, ALU.add)
                ins.then_inc(quarter, 1)

            for b in range(NMOD1):
                for j in range(3):
                    mod_piece(b, j, mraw_a, 4, (macc, macc1)[b % 2])
                    if j == 1 and b:
                        mod_finish(b - 1)
                        if b > 4:
                            modulate(b - 5, xT, gain1, C("n1", 0, 16), 0, 16)
            split_lo(At(0))
            mod_finish(NMOD1 - 1)
            modulate(3, xT, gain1, C("n1", 0, 16), 0, 16)
            dve.drain().then_inc(acts_ok, 1)

            with dve.Fori(0, 4) as i:
                for j in range(8):
                    split_lo(at(j + 1, i, 8))
                    if j in (0, 2, 4):
                        mod_piece(i + 8, j // 2, mraw_a)
                    if j == 7:
                        mod_finish(i + 8)
            for c in range(33, 37):
                split_lo(At(c))
            split_lo(At(37))
            dve.wait_ge(evac, 37)
            softplus(dtr[:, :], [dts[:, k, :] for k in (1, 2, 3, 4)], dts[:, 0, :], 2)
            dve.tensor_scalar(aneg[0:64, :], aneg[0:64, :], -1.0, None, ALU.mult)
            dve.drain()
            dve.tensor_scalar(dts[:, 3, :], dts[:, 0, :], aneg[0:64, 0:1], None, ALU.mult)
            dve.memset(dts[:, 4, :], 1.0)
            dve.drain()
            for t in range(2):
                dve.tensor_tensor_scan(dts[:, 1, t * P:(t + 1) * P], dts[:, 4, 0:P], dts[:, 3, t * P:(t + 1) * P],
                                       0.0, ALU.mult, ALU.add)
            dve.drain()
            dve.tensor_scalar(dts[:, 2, 0:P], dts[:, 1, 0:P], dts[:, 1, P - 1:P], -1.0, ALU.subtract, ALU.mult).then_inc(ac_ok, 1)

            def biased(u):
                j, q = UNITS[u]
                nk = P * (q + 1)
                dve.wait_ge(aL, u + 1)
                dve.wait_ge(bias_in[u % 2], 16 * (u // 2 + 1))
                if u >= 2:
                    dve.wait_ge(aT, u - 1)
                else:
                    dve.wait_ge(brow_ev, 1)
                flat = pw[:, 0:2, :].rearrange("p b n -> p (b n)")[:, 0:768].rearrange("p (g n) -> p g n", g=3)[:, :, 0:nk]
                l = lgt[:, u % 2, 0:3, 0:nk]
                dve.scalar_tensor_tensor(l, flat, ATT_SCALE, biasT[:, u % 2, :, 0:nk], ALU.mult, ALU.add)
                dve.drain()
                dve.tensor_reduce(mx[:, u % 2, 0:1], l, AX.XY, ALU.max)
                dve.drain()
                dve.tensor_scalar(nmx[:, u % 2, 0:1], mx[:, u % 2, 0:1], -1.0, None, ALU.mult).then_inc(aA, 1)

            def moved(u):
                j, q = UNITS[u]
                dve.wait_ge(aO, u + 1)
                dve.tensor_copy(ovec[:, u % 2, :], pw[:, 4, 0:P]).then_inc(aF, 1)
                dve.drain()
                pair(att_hi[:, j, q * P:(q + 1) * P], att_lo[:, j, q * P:(q + 1) * P], ovec[:, u % 2, :])

            biased(0)
            for u in range(8):
                if u + 1 < 8:
                    biased(u + 1)
                j, q = UNITS[u]
                l = lgt[:, u % 2, 0:3, 0:P * (q + 1)]
                dve.wait_ge(aX, u + 1)
                dve.reciprocal(rsum[:, u % 2, 0:1], sums[:, u % 2, 0:1])
                dve.drain()
                dve.tensor_scalar(l, l, rsum[:, u % 2, 0:1], None, ALU.mult).then_inc(aB, 1)
                if u:
                    moved(u - 1)
            moved(7)
            dve.wait_ge(dt_mm, 1)
            dve.tensor_copy(dtn[:, :, :].rearrange("p t h -> p (t h)"), pw[:, 0, 0:128])
            dve.tensor_copy(acn[:, :, :].rearrange("p t h -> p (t h)"), pw[:, 0, 128:256])
            dve.wait_ge(ac_st, 16)
            dve.tensor_copy(decn[:, :], pw[:, 0, 256:320]).then_inc(dt_ev, 1)
            for n in range(2):
                dve.memset(ub[:, n, 0:3], 0.0).then_inc(conv_d, 1)
            dve.drain()

            def group(i, h, gg):
                g = at(4 * h + gg, i, 2)
                ph = f"ssm{h}"
                bc, x = bct[:, gg], xs[:, gg]
                gv = g.times(1)

                def convolve(j):
                    dve.wait_ge(evac, at(E0[ph] + 10 * gg + j, i, 20).times(1, 1))
                    dve.wait_ge(silu_d, g.times(6, j + 1))
                    tile = g.times(1, 32 + 8 * j) if j < 2 else g.times(4, j - 2)
                    u, o = ub[:, j % 2, :], cv[:, j % 2, :]
                    dve.tensor_scalar(o, u[:, 0:S], Cd("cw", tile * 4), Cd("cb", tile), ALU.mult, ALU.add)
                    for k in range(1, 4):
                        dve.drain()
                        ins = dve.scalar_tensor_tensor(o, u[:, k:k + S], Cd("cw", tile * 4 + k), o, ALU.mult, ALU.add)
                    ins.then_inc(conv_d, 1)

                def stepped(t):
                    dve.wait_ge(xt_mm, g.times(4, t + 1))
                    dve.tensor_tensor(xdt[:, :, t * P:(t + 1) * P].rearrange("p c (r n) -> p c r n", r=2),
                                      pw[:, 5 if t % 2 else 1, 0:S].rearrange("p (c r n) -> p c r n", c=2, r=2),
                                      dtn[:, :, span(gv * 8 + 2 * t, 2)].rearrange("p c (r a) -> p c r a", a=1).to_broadcast([P, 2, 2, 64]), ALU.mult).then_inc(xt_ev, 1)

                for j in range(10):
                    split_lo(at(C0[ph] + 10 * gg + j + 1, i, 20))
                    if j < 6:
                        convolve(j)
                    if j == 2:
                        dve.wait_ge(acb_in, g.times(16, 16))
                        for r in range(8):
                            for t in range(2):
                                ins = dve.tensor_scalar(dec[:, r, t, :], acb[:, r, t, :],
                                                        acn[:, t, one(gv * 8 + r)],
                                                        0.0, ALU.subtract, ALU.min)
                        ins.then_inc(dec_in, 1)
                    if j == 3:
                        dve.wait_ge(cb_mm, g.times(1, 1))
                        dve.tensor_tensor(cbm[:, :, :], pw[:, 0, 0:S].rearrange("p (t n) -> p t n", t=2),
                                          C("tri01", 0, 128).rearrange("p (a n) -> p a n", a=1).to_broadcast([P, 2, P]), ALU.mult)
                        dve.tensor_copy(bnat[:, :], pw[:, 0, 256:384]).then_inc(cb_ev, 1)
                        dve.drain()
                    if j == 4:
                        dve.wait_ge(dec_ex, g.times(2, 1))
                        dve.tensor_tensor(dec[:, :, :, :].rearrange("p r t n -> p r (t n)"), dec[:, :, :, :].rearrange("p r t n -> p r (t n)"),
                                          cbm[:, :, :].rearrange("p t n -> p (t n)").rearrange("p (a n) -> p a n", a=1).to_broadcast([P, 8, S]),
                                          ALU.mult).then_inc(m_ok, 1)
                    if j == 5:
                        dve.wait_ge(dec_ex, g.times(2, 2))
                        dve.tensor_tensor(acb[:, :, 1, :], acb[:, :, 1, :],
                                          bc[:, 1, P:S].rearrange("p (a n) -> p a n", a=1).to_broadcast([P, 8, P]),
                                          ALU.mult).then_inc(ce_ok, 1)
                    if 5 <= j < 9:
                        stepped(j - 5)
                    if j == 8:
                        dve.drain()
                        dve.tensor_tensor(xdd[:, :].rearrange("p (r n) -> p r n", r=8),
                                          xdt[:, 0, :].rearrange("p (r n) -> p r n", r=8),
                                          decn[:, wide(gv, 8)].rearrange("p (r a) -> p r a", a=1).to_broadcast([P, 8, 64]),
                                          ALU.mult).then_inc(xdd_ok, 1)
                dve.wait_ge(evac, at(E0[ph] + 10 * gg + 9, i, 20).times(1, 1))
                for t in range(4):
                    dve.wait_ge(y_mm, g.times(4, t + 1))
                    dve.scalar_tensor_tensor(x[:, t, :], x[:, t, :], Cd("dsk", g.times(4, t)),
                                             pw[:, YB[t], 0:S], ALU.mult, ALU.add)
                    dve.drain()
                    dve.tensor_tensor(sz[:, t, :], sz[:, t, :], x[:, t, :], ALU.mult).then_inc(y_ev, 1)
                rms_root(None, pw[:, 5, 0:S], cv[:, 1, :], 512,
                         sems=((ssq_mm, g.times(4, 4)), ssq_v, (ssq_r, g.times(1, 1)), xdd[:, 0:S], cv[:, 0, :]))
                for t in range(4):
                    dve.scalar_tensor_tensor(sz[:, t, :], sz[:, t, :], Cd("ssmn", g.times(4, t)), rstd[:, :],
                                             ALU.mult, ALU.mult)
                dve.drain()
                k = wide(i * 2 + gg, 4)
                dve.tensor_copy(y_hi[:, k, :], sz[:, :, :])
                dve.drain()
                dve.tensor_tensor(y_lo[:, k, :], sz[:, :, :], y_hi[:, k, :].bitcast(F32), ALU.subtract).then_inc(grp, 1)

            def posts8(ph, b0, f, ring=2):
                with dve.Fori(0, 2) as i:
                    for j in range(8):
                        split_lo(at(C0[ph] + j + 1, i, 8))
                        if j - (ring - 2) in (0, 2, 4):
                            mod_piece(i + b0, (j - (ring - 2)) // 2, mraw_b, ring)
                        if f is not None:
                            dve.wait_ge(evac, at(E0[ph] + j, i, 8).times(1, 1))
                            f(i * 2, j, at(POST0[ph] + j, i, 8).slot(4))
                        if j == 7:
                            mod_finish(i + b0)

            def posts(ph, n, f, last=False, first=0):
                def four(i):
                    for j in range(4):
                        split_lo(at(C0[ph] + j + 1, i, 4))
                        dve.wait_ge(evac, at(E0[ph] + j, i, 4).times(1, 1))
                        f(i, j, at(POST0[ph] + j, i, 4).slot(4))
                with dve.Fori(first, n - last) as i:
                    four(i)
                if last:
                    four(n - 1)

            for h in range(2):
                with dve.Fori(0, 2) as i:
                    group(i, h, 0)
                    group(i, h, 1)

                def add_s(i, j, s):
                    m = one(i * 4 + j)
                    dve.tensor_tensor(accS[:, m, :], accS[:, m, :], tm[:, s:s + 1, :], ALU.add).then_inc(post, 1)

                posts8(f"sp{h}", 12 + 2 * h, add_s if h else None, 4)
                if h == 0:
                    for n in range(2):
                        dve.memset(ub[:, n, 0:3], 0.0)
                    dve.drain()
            dve.drain()
            for c in range(4):
                split_lo(At(C0["ap"] + c + 1))

            def gate_s(i, j, s):
                m = one(i * 4 + j)
                dve.tensor_tensor(accS[:, m, :], accS[:, m, :], tm[:, s:s + 1, :], ALU.mult).then_inc(post, 1)

            posts8("gs", 16, gate_s)

            def gate_a(i, j, s):
                m = one(i * 4 + j)
                dve.tensor_tensor(t2[:, j % 2, :].rearrange("p (a n) -> p a n", a=1), accA[:, m, :], tm[:, s:s + 1, :], ALU.mult).then_inc(post, 1)
                dve.drain()
                dve.tensor_tensor(t2[:, j % 2, :].rearrange("p (a n) -> p a n", a=1), t2[:, j % 2, :].rearrange("p (a n) -> p a n", a=1), accS[:, m, :], ALU.add)
                dve.drain()
                pair(mg_hi[:, m, :], mg_lo[:, m, :], t2[:, j % 2, :].rearrange("p (a n) -> p a n", a=1))

            posts8("ga", 18, gate_a)
            dve.drain().then_inc(acts_ok, 1)
            dve.wait_ge(x_in, 32)

            def add_x(i, j, s):
                m = one(i * 4 + j)
                dve.scalar_tensor_tensor(x1[:, m, :], tm[:, s:s + 1, :], modT[:, one(i * 4 + (32 + j))], x1[:, m, :],
                                         ALU.mult, ALU.add).then_inc(post, 1)

            posts8("wo", 20, add_x)
            rms_root(2, pw[:, 4, 0:S], sq1[:, 1, :], D, sems=((rm, 2), rv, (rs, 2), sq1[:, 2, :], sq1[:, 0, :]))
            dve.wait_ge(x1_st, 16)
            dve.tensor_tensor(x1[:, :, :], x1[:, :, :], rstd[:, :].rearrange("p (a n) -> p a n", a=1).to_broadcast([P, DT, S]), ALU.mult)
            dve.drain()
            for m in range(4):
                modulate(m, x1, gain2, C("n2", 0, 16), 48, 64)
            dve.wait_ge(quarter_lo, 8)
            dve.drain().then_inc(acts_ok, 1)

            def hidden(i, j, s):
                if j % 2:
                    f = one(i * 2 + j // 2)
                    o = hf[:, j // 2 % 2:j // 2 % 2 + 1, :]
                    dve.tensor_tensor(o, tf[:, s - 1:s, :], tf[:, s:s + 1, :], ALU.mult).then_inc(post, 1)
                    dve.drain()
                    dve.tensor_copy(hid_hi[:, f, :], o).then_inc(post, 1)
                    dve.drain()
                    dve.tensor_tensor(hid_lo[:, f, :], o, hid_hi[:, f, :].bitcast(F32), ALU.subtract)

            posts8("fi", 22, hidden)
            posts("fi", FF_T // 2, hidden, first=4)
            dve.drain().then_inc(acts_ok, 1)
            dve.wait_ge(x1_in, 16)
            with dve.Fori(0, 8) as i:
                for m in range(2):
                    for q in range(4):
                        c = at(C0["fo"] + 4 * m + q, i, 8)
                        split_lo(c + 1)
                    dve.wait_ge(evac, at(E0["fo"] + m, i, 2).times(1, 1))
                    k = one(i * 2 + m)
                    dve.scalar_tensor_tensor(x1r[:, k, :], tf[:, (POST0["fo"] + m) % 2:(POST0["fo"] + m) % 2 + 1, :],
                                             modT[:, one(i * 2 + (80 + m))], x1r[:, k, :], ALU.mult, ALU.add).then_inc(post, 1)
            dve.drain()
            bc16 = rstd[:, :].rearrange("p (a n) -> p a n", a=1).to_broadcast([P, DT, S])
            rms_root(3, pw[:, 4, 0:S], sqF[:, 1, :], D, sems=((rm, 3), rv, (rs, 3), sqF[:, 2, :], sqF[:, 0, :]))
            for k in range(DT):
                dve.scalar_tensor_tensor(x2T[:, k, :], x1r[:, k, :], C("fin", k), rstd[:, :], ALU.mult, ALU.mult)
            dve.drain().then_inc(acts_ok, 1)
            rms_root(4, pw[:, 4, 0:S], sqF[:, 1, :], D, sems=((rm, 4), rv, (rs, 4), sqF[:, 2, :], sqF[:, 0, :]))
            for k in range(DT):
                dve.scalar_tensor_tensor(sqF[:, k, :], x2T[:, k, :], C("ln2", k), rstd[:, :], ALU.mult, ALU.mult)
            dve.drain()
            pair(act_hi[:, :, :], act_lo[:, :, :], sqF[:, :, :])
            dve.drain().then_inc(acts_ok, 1)
            dve.tensor_scalar(lcon[:, 0, :], C("lam", 0, 8), -1.0, None, ALU.mult)
            dve.drain()
            softplus(lcon[:, 0, :], [lcon[:, k, :] for k in (1, 2, 3, 4)], lcon[:, 5, :], 3, lam_x)
            dve.tensor_scalar(lcon[:, 5, :], lcon[:, 5, :], 8.0, None, ALU.mult)
            for n in range(2):
                ins = dve.memset(ub2[:, n, 0:3], 0.0)
            dve.drain().then_inc(pad_ok, 1)

            def conv2(i, j, s):
                t = i * 4 + j
                u, o = ub2[:, j % 2:j % 2 + 1, :], uc[:, one(t), :]
                dve.tensor_scalar(o, u[:, :, 0:S], Cd("cw2", t * 4), Cd("cb2", t), ALU.mult, ALU.add)
                for k in range(1, 4):
                    dve.drain()
                    ins = dve.scalar_tensor_tensor(o, u[:, :, k:k + S], Cd("cw2", t * 4 + k), o, ALU.mult, ALU.add)
                ins.then_inc(post, 1)

            posts("lx", 2, conv2)
            dve.drain().then_inc(uc_ok, 1)
            for i in range(2):
                dve.wait_ge(lru_g, i + 1)
                for t in range(4):
                    dve.tensor_scalar(lr[:, t, :], lr[:, t, :], lcon[:, 5, 4 * i + t:4 * i + t + 1], None, ALU.mult)
                dve.drain().then_inc(lru_l, 1)
                for j in range(4):
                    split_lo(At(C0["lg"] + 4 * i + j + 1))
                    if j == 1:
                        dve.wait_ge(lru_e, i + 1)
                        dve.tensor_scalar(lw[:, :, :], lt[:, :, :], 1.0, None, ALU.add)
                        dve.drain()
                        dve.reciprocal(lw[:, :, :], lw[:, :, :])
                        dve.drain()
                        dve.tensor_tensor(li[:, :, :], li[:, :, :], uc[:, 4 * i:4 * i + 4, :], ALU.mult)
                        dve.scalar_tensor_tensor(lw[:, :, :], lt[:, :, :], 2.0, lw[:, :, :], ALU.mult, ALU.mult).then_inc(lru_w, 1)
                    if j == 3:
                        dve.wait_ge(lru_q, i + 1)
                        dve.tensor_tensor(lw[:, :, :], lw[:, :, :], li[:, :, :], ALU.mult)
                        dve.drain()
                        for t in range(4):
                            dve.tensor_tensor_scan(lt[:, t, :], la[:, t, :], lw[:, t, :], 0.0, ALU.mult, ALU.add)
                        dve.drain()
                dve.wait_ge(evac, E0["lg"] + 4 * i + 4)
                dve.tensor_tensor(gl[:, :, :], gl[:, :, :], lt[:, :, :], ALU.mult)
                dve.drain()
                pair(yb_hi[:, 4 * i:4 * i + 4, :], yb_lo[:, 4 * i:4 * i + 4, :], gl[:, :, :]).then_inc(lru_y, 1)
            dve.drain().then_inc(acts_ok, 1)

            def quiet(ph, n):
                with dve.Fori(0, n) as i:
                    for j in range(4):
                        split_lo(at(C0[ph] + j + 1, i, 4))

            def branch(ph):
                quiet("wb" + ph, 2)

                def merge(i, j, s):
                    m = one(i * 4 + j)
                    o = accM[:, m, :] if ph == "a" else t3[:, j % 2:j % 2 + 1, :]
                    dve.tensor_tensor(o, proj[:, m, :], tm2[:, s:s + 1, :], ALU.mult).then_inc(post, 1)
                    if ph != "a":
                        dve.drain()
                        dve.tensor_tensor(o if ph == "c" else accM[:, m, :], o, accM[:, m, :], ALU.add)
                    if ph == "c":
                        dve.drain()
                        pair(m2_hi[:, m, :], m2_lo[:, m, :], o)

                posts("mg" + ph, 4, merge)

            branch("a")
            split_lo(At(C0["bf"] + 1))
            split_lo(At(C0["nq"] + 1))
            dve.wait_ge(evac, E0["bf"] + 1)
            f = slice(32, 40)
            dve.tensor_scalar(zf[f, :], zf[f, :], -1.0, None, ALU.mult)
            dve.drain()
            softplus(zf[f, :], [sft[f, k, :] for k in (0, 1, 2, 3)], sft[f, 4, :], 4)
            dve.tensor_scalar(sft[f, 4, :], sft[f, 4, :], -1.0, None, ALU.mult)
            dve.memset(sft[f, 0, :], 1.0)
            dve.drain()
            dve.tensor_tensor_scan(zf[f, :], sft[f, 0, :], sft[f, 4, :], 0.0, ALU.mult, ALU.add)
            dve.tensor_scalar(nudge[:, :], cst[:, CO["ident"] + 32:CO["ident"] + 40], -1.0, None, ALU.mult)
            dve.drain().then_inc(zf_ok, 1)
            split_lo(At(C0["nq"] + 2))
            dve.wait_ge(gn_mm, 1)
            dve.tensor_copy(gn[:, :, :], pw[:, 5, 0:S].rearrange("p (t n) -> p t n", t=2)[:, :, 0:24])
            dve.tensor_copy(cn[:, :, :], pw[:, 5, 0:S].rearrange("p (t n) -> p t n", t=2)[:, :, 32:40])
            dve.tensor_scalar(C("gnq"), C("gnq"), ATT_SCALE, None, ALU.mult)
            dve.tensor_scalar(C("gfq"), C("gfq"), ATT_SCALE, None, ALU.mult)
            dve.drain().then_inc(gn_ok, 1)
            def head_norm(n, tiles, gain):
                rms_root(None, pw[:, 5, 0:512], hv_[:, :], P, hr_[:, :],
                         sems=((hm, n + 1), hv, (hr, n + 1), ht_[:, :], he_[:, :]))
                ins = dve.scalar_tensor_tensor(tiles, tiles, gain, hr_[:, :], ALU.mult, ALU.mult)
                dve.drain().then_inc(hn_ok, 1)

            def block_tokens():
                for x in range(2):
                    for v in range(2):
                        src = nk[:, 8 + 2 * x + v, :].rearrange("p (c t) -> p t c", t=16)
                        for r in range(2):
                            dve.tensor_tensor(kp[:, x, 16 * r:16 * r + 16, 15 * v:15 * v + 15], src[:, :, r:r + 15],
                                              C("pos", 32 * x + 16 * r, 16).rearrange("p (t a) -> p t a", a=1).to_broadcast([P, 16, 15]),
                                              ALU.add)
                dve.drain()

            kall = lambda t: t[:, :, :, :].rearrange("p x t c -> p (x t c)")
            two = lambda t, n: t[:, n:n + 2, :].rearrange("p k n -> p (k n)")
            for c in range(2, 20):
                split_lo(At(C0["nq"] + c + 1))
                if c - 3 in NSA_N:
                    n = NSA_N.index(c - 3)
                    head_norm(n, two(nk, c - 3), C("gnq") if n < 4 else C("gnk"))
                if c == 12:
                    dve.wait_ge(evac, E0["nq"] + 12)
                    block_tokens()
                if c == 13:
                    dve.tensor_copy(kall(kp_hi), kall(kp))
                    dve.drain()
                if c == 14:
                    dve.tensor_tensor(kall(kp_lo), kall(kp), kall(kp_hi).bitcast(F32), ALU.subtract).then_inc(kp_ok, 1)
            for j in range(8):
                split_lo(At(C0["cmp"] + j + 1))
            split_lo(At(C0["ng"] + 1))
            split_lo(At(C0["ng"] + 2))
            dve.wait_ge(kc_ev, 1)
            rms_root(None, pw[:, 5, 0:30], kcs[:, 3, :], P, kcs[:, 1, :], sems=((hm, 7), hv, (hr, 7), kcs[:, 4, :], kcs[:, 2, :]))
            dve.scalar_tensor_tensor(kcT[:, :], kcT[:, :], C("gnk"), kcs[:, 1, :], ALU.mult, ALU.mult)
            dve.drain().then_inc(hn_ok, 1)

            def att_bias(b):
                kind, h0, q = BATCH[b]
                n = P * (q + 1) if kind else 15
                dve.wait_ge(aL, 8 + b + 1)
                if b % 100 and b not in (NSA_B, NSA_B + 1) and b >= 2:
                    dve.wait_ge(aT, 8 + b - 1)
                l = (lg3 if kind == 3 else lg2)[:, b % 2, :, 0:n]
                flat = pw[:, 0:2, :].rearrange("p b (r n) -> p (b r) n", r=2)[:, :, 0:n]
                mask = (C("tri", 0, 256) if q else C("tri", 128, 128)) if kind else C("cmask", 15 * q, 15)
                if kind == 3:
                    for r in range(4):
                        dve.scalar_tensor_tensor(l[:, r, :], flat[:, r, :], cn[:, q, h0 + r:h0 + r + 1], mask, ALU.add, ALU.add)
                else:
                    dve.tensor_tensor(l, flat, mask.rearrange("p (a n) -> p a n", a=1).to_broadcast([P, 4, n]), ALU.add)
                dve.drain()
                dve.tensor_reduce(mx[:, b % 2, :], l, AX.X, ALU.max)
                dve.drain()
                dve.tensor_scalar(nmx[:, b % 2, :], mx[:, b % 2, :], -1.0, None, ALU.mult).then_inc(aA, 1)

            def att_scale(b):
                kind, h0, q = BATCH[b]
                n = P * (q + 1) if kind else 15
                l = (lg3 if kind == 3 else lg2)[:, b % 2, :, 0:n]
                s_, r_ = sums[:, b % 2, :], rsum[:, b % 2, :]
                dve.wait_ge(aX, 8 + b + 1)
                if kind == 0:
                    dve.tensor_tensor(l, l, C("cmask", 30 + 15 * q, 15).rearrange("p (a n) -> p a n", a=1).to_broadcast([P, 4, 15]), ALU.mult)
                    dve.drain()
                    dve.tensor_reduce(s_, l, AX.X, ALU.add)
                    dve.drain()
                dve.tensor_scalar(s_, s_, 1e-30, None, ALU.max)
                dve.drain()
                dve.reciprocal(r_, s_)
                dve.drain()
                if kind < 3:
                    dve.tensor_tensor(r_, r_, gn[:, q, 3 * h0 + kind:3 * h0 + kind + 10:3], ALU.mult)
                    dve.drain()
                for r in range(4):
                    ins = dve.tensor_scalar(l[:, r, :], l[:, r, :], r_[:, r:r + 1], None, ALU.mult)
                ins.then_inc(aB, 1)

            def att_moved(b):
                kind, h0, q = BATCH[b]
                if kind < 2:
                    return
                dve.wait_ge(aO, 8 + b + 1)
                dve.tensor_copy((fx if kind == 3 else nk)[:, h0:h0 + 4, q * P:(q + 1) * P],
                                pw[:, 4, :].rearrange("p (r n) -> p r n", r=4)).then_inc(aF, 1)

            def gated(ph, src, g):
                t = slice(4 * g, 4 * g + 4)
                dve.wait_ge(evac, E0[ph] + 4 * g + 4)
                dve.drain()
                dve.tensor_tensor(src[:, t, :], src[:, t, :], gate[:, t, :], ALU.mult)
                dve.drain()
                pair(yb_hi[:, t, :], yb_lo[:, t, :], src[:, t, :]).then_inc(yb_ok, 1)

            def attention(b0, b1, ph, src):
                att_bias(b0)
                for b in range(b0, b1):
                    if b + 1 < b1:
                        att_bias(b + 1)
                    att_scale(b)
                    rides = RIDES.get(b, [])
                    for c in rides[1:]:
                        split_lo(At(C0[ph] + c))
                    if b > b0:
                        att_moved(b - 1)
                    for c in rides[-1:]:
                        split_lo(At(C0[ph] + c + 1))
                    if b == (b0 + b1) // 2 + 1:
                        gated(ph, src, 0)
                att_moved(b1 - 1)
                gated(ph, src, 1)
                dve.drain().then_inc(acts_ok, 1)

            attention(0, NSA_B, "ng", nk)
            branch("b")
            for c in range(24):
                split_lo(At(C0["fx"] + c + 1))
                if 3 <= c < 19 and c % 2:
                    n = (c - 3) // 2
                    head_norm(7 + n, two(fx, 2 * n), C("gfq") if n < 4 else C("gfk"))
            attention(NSA_B, len(BATCH), "fg", fx)
            branch("c")
            dve.drain().then_inc(acts_ok, 1)

            def add_x2(i, j, s):
                m = one(i * 4 + j)
                dve.tensor_tensor(x2T[:, m, :], x2T[:, m, :], tm2[:, s:s + 1, :], ALU.add).then_inc(post, 1)
                dve.drain()
                pair(act_hi[:, m, :], act_lo[:, m, :], x2T[:, m, :])

            dve.wait_ge(p_land, 16)
            pair(p_hi[:, :, :], p_lo[:, :, :], p_in[:, :, :]).then_inc(p_ok, 1)
            posts("w2", 4, add_x2)
            dve.drain().then_inc(h_ok, 1)
            for c in range(2):
                split_lo(At(C0["ple"] + c + 1))
            rms_root(5, pw[:, 4, 0:S], sqF[:, 1, :], D, sems=((rm, 5), rv, (rs, 5), sqF[:, 2, :], sqF[:, 0, :]))
            for k in range(DT):
                dve.scalar_tensor_tensor(eT[:, k, :], eT[:, k, :], C("pleg", k), rstd[:, :], ALU.mult, ALU.mult)
            dve.drain()

            def finish(i, j, s):
                m = one(i * 4 + j)
                o = t3[:, j % 2:j % 2 + 1, :]
                dve.tensor_tensor(o, eT[:, m, :], tm2[:, s:s + 1, :], ALU.mult).then_inc(post, 1)
                dve.drain()
                dve.tensor_tensor(x2T[:, m, :], x2T[:, m, :], o, ALU.add)

            posts("pg", 4, finish, last=True)
            dve.drain().then_inc(out_ok, 1)


def tiles(w, kt=16):
    k, m = w.shape
    return w.reshape(k // P // kt, kt, P, m // P, P).transpose(3, 0, 2, 1, 4)


def padded(w, cols):
    out = np.zeros((w.shape[0], cols), w.dtype)
    out[:, :w.shape[1]] = w
    return out


def per_tile(v):
    return v.reshape(-1, P).T


def feature_major(x):
    return np.ascontiguousarray(x.T.reshape(-1, P, x.shape[0]).transpose(1, 0, 2))


def distance_buckets():
    out = np.zeros((33, 3, 512), np.float32)
    for g, (window, dil) in enumerate(((128, 1), (512, 4), (2048, 16))):
        for i in range(512):
            d = 255 - i
            if d < 0 or d % dil or d > window:
                out[32, g, i] = 1
                continue
            n = np.float32(max(d, 1))
            large = 16 + int(np.float32(np.log(n / np.float32(16))) / np.float32(np.log(2048 / 16)) * np.float32(16))
            out[d if d < 16 else min(large, 31), g, i] = 1
    return out


def pack(a):
    f = lambda n: np.asarray(a[n])
    w_in = f("w_in")[0]
    chunks = [tiles(w_in[:, 0:4608])]
    chunks.append(tiles(padded(w_in[:, 14848:14912], P)))
    tz, tx = tiles(w_in[:, 4608:8704]), tiles(w_in[:, 8704:14848])
    sp = f("w_ssm_proj")[0]
    for h in range(2):
        for g in range(4 * h, 4 * h + 4):
            chunks += [tx[32 + g:33 + g], tx[40 + g:41 + g], tx[4 * g:4 * g + 4], tz[4 * g:4 * g + 4]]
        chunks.append(tiles(sp[2048 * h:2048 * h + 2048]))
    ap = f("w_attn_proj")[0].reshape(4, P, 4, 4, P)
    chunks.append(ap.transpose(2, 1, 3, 0, 4).reshape(4, 1, P, 16, P))
    chunks.append(tiles(w_in[:, 16960:19008]))
    chunks.append(tiles(w_in[:, 14912:16960]))
    chunks.append(tiles(f("w_out")[0]))
    ff = tiles(f("w_ffn_in")[0])
    chunks.append(np.stack([ff[0:FF_T], ff[FF_T:]], 1).reshape(2 * FF_T, 1, P, 16, P))
    w2 = f("w_in_2")[0]
    b2 = f("b_in_2")[0]
    o2, at2 = {}, 0
    for name, n in (("lx", 1024), ("lg", 1024), ("q", 1024), ("kv", 1536), ("bg", 24), ("ng", 1024),
                    ("fx", 3072), ("ff", 8), ("fg", 1024), ("mg", 6144)):
        o2[name] = slice(at2, at2 + n)
        at2 += n
    mg = [slice(o2["mg"].start + 2048 * b, o2["mg"].start + 2048 * b + 2048) for b in range(3)]

    def gates(v):
        out = np.zeros(v.shape[:-1] + (P,), v.dtype)
        out[..., 0:24] = v[..., o2["bg"]]
        out[..., 32:40] = v[..., o2["ff"]]
        return out

    wb = f("w_branch_2")[0]

    def branch(b):
        return wb[b].reshape(8, P, 8, 2, P).transpose(2, 1, 3, 0, 4).reshape(8, P, 16, P)

    hidden = f("cmp_w1_2")[0].reshape(8, 8, P, 256).transpose(0, 2, 1, 3).reshape(8, 1, P, 16, P)
    chunks += [tiles(w2[:, o2["lx"]]), tiles(w2[:, o2["lg"]]), branch(0), tiles(w2[:, mg[0]]),
               tiles(gates(w2)), tiles(w2[:, o2["q"]]), tiles(w2[:, o2["kv"]]), hidden,
               tiles(w2[:, o2["ng"]]), branch(1), tiles(w2[:, mg[1]]),
               tiles(w2[:, o2["fx"]]), tiles(w2[:, o2["fg"]]), branch(2), tiles(w2[:, mg[2]]),
               tiles(f("w_out_2")[0]),
               f("w_ple_2")[0].reshape(2, P, 2, 8, P).transpose(2, 1, 3, 0, 4).reshape(2, P, 16, P),
               tiles(f("w_ple_gate_2")[0])]
    w16 = np.concatenate([c.reshape(-1, P, 16, P) for c in chunks])
    w11 = np.ascontiguousarray(tiles(f("w_ffn_out")[0], KFO).reshape(NFO, P, KFO, P))
    wm = np.ascontiguousarray(f("w_mod")[0].reshape(4, 4, P, 24, 512).transpose(3, 0, 2, 1, 4))
    cst = np.zeros((P, NCST), np.float32)

    def put(name, v):
        v = np.asarray(v)
        cst[:v.shape[0], CO[name]:CO[name] + v.shape[1]] = v

    put("c", per_tile(f("c")[0]))
    put("bmod", per_tile(f("b_mod")[0]))
    put("n1", per_tile(f("norm1_w")[0]))
    put("n2", per_tile(f("norm2_w")[0]))
    put("fin", per_tile(f("final_norm_w")))
    put("cw", f("conv_w")[0].reshape(4, 48, P).transpose(2, 1, 0).reshape(P, 192))
    put("cb", per_tile(f("conv_b")[0]))
    put("dtb", f("dt_bias")[0][:, None])
    put("alog", f("a_log")[0][:, None])
    put("dsk", per_tile(np.repeat(f("d_skip")[0], 64)))
    put("ssmn", per_tile(f("ssm_norm_w")[0]))
    put("rel", np.concatenate([f("rel_bias"), np.full((1, 12), NEG, np.float32)]))
    put("ident", np.eye(P))
    order = [b2[o2["lx"]], b2[o2["lg"]], b2[mg[0]], gates(b2), b2[o2["q"]], b2[o2["kv"]], b2[o2["ng"]],
             b2[mg[1]], b2[o2["fx"]], b2[o2["fg"]], b2[mg[2]]]
    put("b2", per_tile(np.concatenate(order)))
    put("cw2", f("conv_w_2")[0].reshape(4, 8, P).transpose(2, 1, 0).reshape(P, 32))
    put("cb2", per_tile(f("conv_b_2")[0]))
    put("ba", per_tile(f("lru_ba_2")[0]))
    put("bx", per_tile(f("lru_bx_2")[0]))
    put("lam", per_tile(f("lru_lambda_2")[0]))
    put("pos", f("cmp_pos_2")[0].transpose(2, 0, 1).reshape(P, 64))
    for name, src in (("gnq", "nsa_q_gain_2"), ("gnk", "nsa_k_gain_2"), ("gfq", "fox_q_gain_2"), ("gfk", "fox_k_gain_2")):
        put(name, f(src)[0][:, None])
    put("ln2", per_tile(f("ln_gain_2")[0]))
    put("pleg", per_tile(f("ple_gain_2")[0]))
    i = np.arange(P)
    tri = np.zeros((P, 256), np.float32)
    tri[:, 128:] = np.where(i[None, :] <= i[:, None], 0, NEG)
    put("tri", tri)
    seen = (np.arange(15) * 16 + 31)[None, None, :] <= i[:, None, None] + P * np.arange(2)[None, :, None]
    put("cmask", np.concatenate([np.where(seen, 0, NEG).reshape(P, 30), seen.reshape(P, 30)], 1).astype(np.float32))
    wab = np.zeros((P, 8, 2, P), np.float32)
    for n, name in enumerate(("lru_wa_2", "lru_wx_2")):
        v = f(name)[0].reshape(8, 2, 64, 64)
        for r in range(2):
            wab[64 * r:64 * r + 64, :, n, 64 * r:64 * r + 64] = v[:, r].transpose(1, 0, 2)
    cw2 = np.ascontiguousarray(f("cmp_w2_2")[0].reshape(2, 2, P, P).transpose(2, 0, 1, 3))
    put("tri01", (i[None, :] >= i[:, None]).astype(np.float32))
    return {"w16": w16, "w11": w11, "wm": wm, "cst": cst, "onehot": distance_buckets(),
            "xt": feature_major(f("x")[0]), "pt": feature_major(f("p_2")[0, 0]), "wab": wab, "cw2": cw2}


_NAMES = ["w16", "w11", "wm", "cst", "onehot", "xt", "pt", "wab", "cw2"]


def kernel(**inputs):
    import numpy as _np
    import concourse.bacc as _bacc
    from concourse import mybir as _mybir
    from concourse.bass_utils import run_bass_kernel_spmd as _run

    arrays = {k: _np.ascontiguousarray(v) for k, v in pack(inputs).items()}
    nc = _bacc.Bacc("TRN2", target_bir_lowering=False, num_devices=1)
    args = [nc.dram_tensor(k, arrays[k].shape, _mybir.dt.float32, kind="ExternalInput").ap() for k in _NAMES]
    args.append(nc.dram_tensor("out_dram", (P, DT * S), _mybir.dt.float32, kind="ExternalOutput").ap())
    first_and_second_block(nc, *args)
    r = _run(nc, [arrays], core_ids=[0])
    got = r.results[0]["out_dram"]
    return got.reshape(P, DT, S).transpose(2, 1, 0).reshape(1, S, D)
```

```python
from contextlib import ExitStack

import numpy as np
import concourse.bass as bass
from concourse import mybir

F32 = mybir.dt.float32
F32R = mybir.dt.float32r
ALU = mybir.AluOpType
ACT = mybir.ActivationFunctionType
AX = mybir.AxisListType

P = 128
S = 256
D = 2048
DT = D // P
EPS = 1e-6
NEG = -1e30
ATT_SCALE = float(128) ** -0.5
FF_T = 5632 // P
SG = 8
LRU_T = 8

PHASES = [
    ("qkv", 36, 36), ("dt", 1, 1), ("gs", 16, 16),
    ("ssm0", 40, 40), ("sp0", 16, 16), ("ssm1", 40, 40), ("sp1", 16, 16),
    ("ap", 4, 8), ("ga", 16, 16), ("wo", 16, 16),
    ("fi", 88, 88), ("fo", 64, 16),
    ("lx", 8, 8), ("lg", 8, 8), ("wba", 8, 16), ("mga", 16, 16),
    ("bf", 1, 1), ("nq", 20, 20), ("cmp", 8, 2), ("ng", 8, 8), ("wbb", 8, 16), ("mgb", 16, 16),
    ("fx", 24, 24), ("fg", 8, 8), ("wbc", 8, 16), ("mgc", 16, 16),
    ("w2", 16, 16), ("ple", 2, 8), ("pg", 16, 16),
]
C0, E0 = {}, {}
_c = _e = 0
for _n, _k, _r in PHASES:
    C0[_n], E0[_n] = _c, _e
    _c, _e = _c + _k, _e + _r
CHUNKS = _c
KFO = 11
NFO = 64

CST = [
    ("c", 16), ("bmod", 96), ("n1", 16), ("n2", 16), ("fin", 16), ("cw", 48 * 4), ("cb", 48),
    ("dtb", 1), ("alog", 1), ("dsk", 32), ("ssmn", 32), ("rel", 12),
    ("b2", 125), ("cw2", 32), ("cb2", 8), ("ba", 8), ("bx", 8), ("lam", 8), ("pos", 64),
    ("gnq", 1), ("gnk", 1), ("gfq", 1), ("gfk", 1), ("ln2", 16), ("pleg", 16),
    ("ident", 128), ("tri", 256), ("tri01", 128), ("cmask", 60),
]
CO = {}
_o = 0
for _n, _k in CST:
    CO[_n] = _o
    _o += _k
NCST = _o


class At:

    def __init__(self, base, *terms):
        self.base, self.terms = base, terms

    def __add__(self, n):
        return At(self.base + n, *self.terms)

    def slot(self, n):
        return self.base % n

    def times(self, k, add=0):
        v = self.base * k + add
        for reg, stride in self.terms:
            v = reg * (stride * k) + v
        return v

    def round(self, n, k, add=0):
        v = (self.base // n) * k + add
        for reg, stride in self.terms:
            v = reg * (stride // n * k) + v
        return v


def at(base, i, stride):
    return At(base + i * stride) if isinstance(i, int) else At(base, (i, stride))


def one(i):
    return slice(i, i + 1) if isinstance(i, int) else bass.ds(i, 1)


def span(i, n):
    return slice(i, i + n) if isinstance(i, int) else bass.ds(i, n)


def wide(i, n):
    return slice(i * n, i * n + n) if isinstance(i, int) else bass.ds(i * n, n)


def first_and_second_block(nc, w16, w11, wm, cst_d, onehot, xt, pt, wab, cw2, out):
    ctx = ExitStack()
    with ctx:
        BASE = 16512
        CSTB = BASE + 98304
        W = CSTB + 9216

        def sb(name, shape, offset, dt=F32):
            return nc.alloc_sbuf_tensor_at(name, shape, dt, offset=offset)

        def sem(name):
            return ctx.enter_context(nc.semaphore(name))

        raw = sb("raw", [P, 4, 16, P], BASE)
        whi = sb("whi", [P, 2, 16, P], BASE + 32768, F32R)
        wlo = sb("wlo", [P, 2, 16, P], BASE + 49152, F32R)
        act_hi = sb("act_hi", [P, DT, S], BASE + 65536, F32R)
        act_lo = sb("act_lo", [P, DT, S], BASE + 81920, F32R)
        cst = sb("cst", [P, NCST], CSTB)
        ones = sb("ones", [P, P], CSTB + 5376)
        modT = sb("modT", [P, 96], CSTB + 5888)
        dtn = sb("dtn", [P, 2, 64], CSTB + 6272)
        acn = sb("acn", [P, 2, 64], CSTB + 6784)
        decn = sb("decn", [P, 64], CSTB + 7296)
        gain1 = sb("gain1", [P, DT], CSTB + 7552)
        gain2 = sb("gain2", [P, DT], CSTB + 7616)
        mx = sb("mx", [P, 2, 4], CSTB + 7680)
        nmx = sb("nmx", [P, 2, 4], CSTB + 7712)
        sums = sb("sums", [P, 2, 4], CSTB + 7744)
        rsum = sb("rsum", [P, 2, 4], CSTB + 7776)
        cact = sb("cact", [P, 16], CSTB + 7808)
        aneg = sb("aneg", [P, 1], CSTB + 7872)
        nudge = sb("nudge", [P, 8], CSTB + 7904)
        spl = sb("spl", [P, 8], CSTB + 7936)
        rstd = sb("rstd", [P, S], CSTB + 8192)

        def C(name, a=0, n=1):
            return cst[:, CO[name] + a:CO[name] + a + n]

        def Cd(name, a):
            return cst[:, CO[name] + a:CO[name] + a + 1] if isinstance(a, int) else cst[:, bass.ds(a + CO[name], 1)]

        ident = C("ident", 0, 128)

        xT = sb("xT", [P, DT, S], W)
        sqT = sb("sqT", [P, DT, S], W + 16384)
        mraw_a = sb("mraw_a", [P, 4, 4, 512], W + 36864)
        mraw_b = sb("mraw_b", [P, 4, 4, 512], W + 57344)
        mraw_c = sb("mraw_c", [P, 2, 4, 512], W + 73728)
        macc = sb("macc", [P, 512], W + 98304)
        macp = sb("macp", [P, 512], W + 100352)
        macc1 = sb("macc1", [P, 512], W + 69632)
        macp1 = sb("macp1", [P, 512], W + 71680)
        qkv = sb("qkv", [P, 36, S], W)
        vnat = sb("vnat", [P, 2, 12, P], W + 36864)
        att_hi = sb("att_hi", [P, 4, S], W + 49152, F32R)
        att_lo = sb("att_lo", [P, 4, S], W + 53248, F32R)
        dtr = sb("dtr", [64, S], W + 57344)
        dts = sb("dts", [64, 6, S], W + 58368)
        biasT = sb("biasT", [P, 2, 3, S], W + 75776)
        lgt = sb("lgt", [P, 2, 4, S], W + 81920)
        pT = sb("pT", [P, 2, 8, P], W + 90112)
        ovec = sb("ovec", [P, 2, P], W + 64512)
        gsb = sb("gsb", [P, 8, S], W + 65536)
        gsr = sb("gsr", [P, 8, S], W + 49152)
        brow = sb("brow", [4, 3, 512], W + 98304)
        oneh = sb("oneh", [33, 3, 512], W + 81920)
        y_hi = sb("y_hi", [P, 16, S], W, F32R)
        y_lo = sb("y_lo", [P, 16, S], W + 16384, F32R)
        accS = sb("accS", [P, DT, S], W + 32768)
        Z = W + 57344
        ub = sb("ub", [P, 2, 259], Z)
        cv = sb("cv", [P, 2, S], Z + 2080)
        bct = sb("bct", [P, 2, 2, S], Z + 4128)
        xs = sb("xs", [P, 2, 4, S], Z + 8224)
        sz = sb("sz", [P, 4, S], Z + 16416)
        acb = sb("acb", [P, 8, 2, P], Z + 20512)
        dec = sb("dec", [P, 8, 2, P], Z + 28704)
        xdt = sb("xdt", [P, 2, 512], Z + 36896)
        xdd = sb("xdd", [P, 512], Z + 40992)
        st0 = sb("st0", [P, 512], Z + 43040)
        cbm = sb("cbm", [P, 2, P], Z + 45088)
        bnat = sb("bnat", [P, P], Z + 46112)
        sq = sb("sq", [P, S], Z + 46624)
        accA = sb("accA", [P, DT, S], W + 16384)
        mg_hi = sb("mg_hi", [P, DT, S], W, F32R)
        mg_lo = sb("mg_lo", [P, DT, S], W + 75776, F32R)
        tm = sb("tm", [P, 4, S], W + 92160)
        t2 = sb("t2", [P, 2, S], W + 96256)
        x1 = sb("x1", [P, DT, S], W + 32768)
        xq = sb("xq", [P, DT, S], W)
        sq1 = sb("sq1", [P, DT, S], W + 16384)
        hid_hi = sb("hid_hi", [P, FF_T, S], W, F32R)
        hid_lo = sb("hid_lo", [P, FF_T, S], W + 45056, F32R)
        tf = sb("tf", [P, 4, S], W + 90112)
        hf = sb("hf", [P, 2, S], W + 94208)
        x1r = sb("x1r", [P, DT, S], BASE + 65536)
        ssum = sb("ssum", [P, 2, S], W + 96256)

        x2T = sb("x2T", [P, DT, S], W)
        accM = sb("accM", [P, DT, S], W + 16384)
        sqF = sb("sqF", [P, DT, S], W + 49152)
        yb_hi = sb("yb_hi", [P, 8, S], W + 32768, F32R)
        yb_lo = sb("yb_lo", [P, 8, S], W + 40960, F32R)
        gate = sb("gate", [P, 8, S], W + 40960)
        R2 = W + 49152
        proj = sb("proj", [P, DT, S], R2)
        tm2 = sb("tm2", [P, 4, S], W + 98304)
        t3 = sb("t3", [P, 2, S], W + 102400)
        uc = sb("uc", [P, 8, S], R2)
        gl = sb("gl", [P, 4, S], R2 + 8192)
        lr, li, lt, la, lw = (sb(n, [P, 4, S], R2 + 12288 + 4096 * k) for k, n in enumerate(("lr", "li", "lt", "la", "lw")))
        wabs = sb("wabs", [P, 4, 2, P], R2 + 32768)
        ub2 = sb("ub2", [P, 2, 259], R2 + 36864)
        lcon = sb("lcon", [P, 6, 8], CSTB + 7968)
        zf = sb("zf", [P, S], CSTB + 6272)
        gn = sb("gn", [P, 2, 24], CSTB + 7296)
        cn = sb("cn", [P, 2, 8], CSTB + 7488)
        sft = sb("sft", [P, 5, S], W + 32768)
        nk = sb("nk", [P, 20, S], R2)
        kp = sb("kp", [P, 2, 32, 30], R2 + 20480)
        kp_hi = sb("kp_hi", [P, 2, 32, 30], R2 + 28160, F32R)
        kp_lo = sb("kp_lo", [P, 2, 32, 30], R2 + 35840, F32R)
        cw2s = sb("cw2s", [P, 2, 2, P], R2 + 43520)
        hc = sb("hc", [P, 2, 2, 30], R2 + 45568)
        hct = sb("hct", [30, 2, 256], R2 + 20480)
        vcn = sb("vcn", [15, 2, P], R2 + 46080)
        kcT = sb("kcT", [P, 30], R2 + 47104)
        kcs = sb("kcs", [P, 5, 30], R2 + 47232)
        hq_ = sb("hsq", [P, 2, 512], W + 32768)
        hr_, hv_, ht_, he_ = (sb(n, [P, 512], W + 36864 + 2048 * k) for k, n in enumerate(("hroot", "hval", "htmp", "hrec")))
        lg2 = sb("lg2", [P, 2, 4, S], R2 + 20480)
        pT2 = sb("pT2", [P, 2, 8, P], R2 + 28672)
        vn2 = sb("vn2", [P, 2, 4, P], R2 + 36864)
        fx = sb("fx", [P, 24, S], R2)
        vn3 = sb("vn3", [P, 2, 8, P], R2 + 24576)
        lg3 = sb("lg3", [P, 2, 4, S], R2 + 32768)
        pT3 = sb("pT3", [P, 2, 8, P], R2 + 40960)
        m2_hi = sb("m2_hi", [P, DT, S], W + 65536, F32R)
        m2_lo = sb("m2_lo", [P, DT, S], W + 81920, F32R)
        eT = sb("eT", [P, DT, S], W + 16384)
        p_in = sb("p_in", [P, 2, S], W + 32768)
        p_hi = sb("p_hi", [P, 2, S], W + 34816, F32R)
        p_lo = sb("p_lo", [P, 2, S], W + 36864, F32R)

        accp = ctx.enter_context(nc.psum_tensor("accp", [P, 2, 512], F32))
        pw = ctx.enter_context(nc.psum_tensor("pw", [P, 6, 512], F32))

        x1_d = nc.dram_tensor("x1_d", [P, DT * S], F32, kind="Internal").ap()
        ac_d = nc.dram_tensor("ac_d", [SG, 8 * S], F32, kind="Internal").ap()
        gs_d = nc.dram_tensor("gs_d", [P, DT * S], F32, kind="Internal").ap()
        br_d = nc.dram_tensor("br_d", [4, 3 * 512], F32, kind="Internal").ap()
        bw_d = nc.dram_tensor("bw_d", [4, P, 3 * 512], F32, kind="Internal").ap()

        raw_in = [sem(f"raw_in{i}") for i in range(4)]
        hi_done = sem("hi_done")
        lo_a = sem("lo_a")
        lo_b = sem("lo_b")
        used = sem("used")
        evac = sem("evac")
        post = sem("post")
        cst_in = sem("cst_in")
        x_in = sem("x_in")
        ones_ok = sem("ones_ok")
        mod_in = [sem(f"mod_in{j}") for j in range(4)]
        mod_used = sem("mod_used")
        modp_used = sem("modp_used")
        quarter = sem("quarter")
        quarter_hi = sem("quarter_hi")
        quarter_lo = sem("quarter_lo")
        cact_ok = sem("cact_ok")
        macc_ok = sem("macc_ok")
        mod_mm = sem("mod_mm")
        mod_ok = sem("mod_ok")
        rq, rm, rv, rs = sem("rms_squares"), sem("rms_sum"), sem("rms_recip"), sem("rms_root")
        acts_ok = sem("acts_ok")
        spx, spe = sem("sp_abs"), sem("sp_exp")
        tp_mm, tp_ev = sem("tp_mm"), sem("tp_ev")
        aL, aA, aX, aB, aT, aC, aO, aF = (sem("att_" + n) for n in (
            "logits", "biased", "exp", "scaled", "turned", "copied", "out", "moved"))
        brow_mm, brow_ev, brow_st = sem("brow_mm"), sem("brow_ev"), sem("brow_st")
        oneh_in = sem("oneh_in")
        bias_in = [sem("bias_in0"), sem("bias_in1")]
        ac_ok, ac_st, acb_in = sem("ac_ok"), sem("ac_st"), sem("acb_in")
        dt_mm, dt_ev, dt_ex = sem("dt_mm"), sem("dt_ev"), sem("dt_ex")
        conv_d, silu_d = sem("conv_done"), sem("silu_done")
        dec_in, dec_ex = sem("dec_ready"), sem("dec_exp")
        cb_mm, cb_ev = sem("cb_mm"), sem("cb_ev")
        m_ok, ce_ok = sem("m_ok"), sem("ce_ok")
        xt_mm, xt_ev = sem("xt_mm"), sem("xt_ev")
        xdd_ok, s0_mm, s0_ev = sem("xdd_ok"), sem("s0_mm"), sem("s0_ev")
        y_mm, y_ev, sq_ok = sem("y_mm"), sem("y_ev"), sem("sq_ok")
        ssq_mm, ssq_v, ssq_r, grp = sem("ssq_mm"), sem("ssq_v"), sem("ssq_r"), sem("grp_done")
        gs_st, gs_in = sem("gs_st"), [sem("gs_in0"), sem("gs_in1")]
        x1_st, x1_in = sem("x1_st"), sem("x1_in")
        pad_ok = sem("pad_ok")
        out_ok, out_st = sem("out_ok"), sem("out_st")

        uc_ok, wab_in, lru_mm, lru_g, lru_l, lru_e, lru_w, lru_q, lru_y = (sem("lru_" + n) for n in (
            "conv", "weights", "mm", "gates", "logs", "exps", "squares", "roots", "y"))
        lam_x = sem("lam")
        yb_ok = sem("yb_ok")
        zf_ok, gn_mm, gn_ok = sem("zf_ok"), sem("gn_mm"), sem("gn_ok")
        kp_ok, cw2_in, kc_mm, kc_ev = sem("kp_ok"), sem("cw2_in"), sem("kc_mm"), sem("kc_ev")
        hq, hm, hv, hr = sem("head_squares"), sem("head_sum"), sem("head_recip"), sem("head_root")
        hn_ok = sem("head_normed")
        hct_mm, hct_ev = sem("hidden_turned"), sem("hidden_moved")
        p_ok, p_land, h_ok = sem("p_ok"), sem("p_land"), sem("h_ok")
        POST0, _p = {}, 0
        for name, n in (("sp1", 16), ("ga", 16), ("wo", 16), ("fi", 88), ("fo", 16),
                        ("lx", 8), ("mga", 16), ("mgb", 16), ("mgc", 16), ("w2", 16), ("pg", 16)):
            POST0[name] = _p
            _p += n
        NMOD1 = 8
        YB = (3, 4, 0, 1)
        B2, _b = {}, 0
        for name, n in (("lx", 8), ("lg", 8), ("mga", 16), ("bf", 1), ("nq", 20), ("ng", 8), ("mgb", 16),
                        ("fx", 24), ("fg", 8), ("mgc", 16)):
            B2[name] = _b
            _b += n
        NSA_N = [0, 2, 4, 6, 12, 16]
        BATCH = [(kind, 4 * g, q) for g in range(2) for q in (1, 0) for kind in range(3)]
        BATCH += [(3, 4 * g, q) for g in range(2) for q in (1, 0)]
        NSA_B = 12
        RIDES = {b: [b + 1] for b in range(1, 7)} | {NSA_B + b: [2 * b, 2 * b + 1] for b in range(4)}
        CLOSED = [n for n, b in enumerate(BATCH) if b[0] >= 2]
        UNITS = [(j, q) for j in range(4) for q in (1, 0)]
        GS = [[3 + 2 * u, 4 + 2 * u] if u < 5 else [8 + u] for u in range(8)]

        block = ctx.enter_context(nc.Block())

        @block.sync
        def _(sp):
            sp.dma_start(cst[:, :], cst_d).then_inc(cst_in, 16)

            def piece(b, j, ring=4):
                src = wm[one(b), j].rearrange("a p k n -> p (a k) n")
                if ring == 4 and not (isinstance(b, int) and b == 0):
                    sp.wait_ge(modp_used if j == 3 else mod_used, b if j == 3 else b * 3 + (j - 2))
                elif ring == 2 and j == 1:
                    sp.wait_ge(modp_used, b)
                elif ring == 2:
                    sp.wait_ge(mod_used, b * 3 + (0, 0, 1, 2)[j])
                buf = (mraw_a, mraw_b, mraw_c)[stage]
                sp.dma_start(buf[:, j % ring], src).then_inc(mod_in[j], 16)

            def load(c, src, k=16, free=True):
                if free:
                    sp.wait_ge(lo_a, c.times(1, -3))
                    sp.wait_ge(lo_b, c.times(1, -3))
                sp.dma_start(raw[:, c.slot(4), 0:k, :], src.rearrange("a p k n -> p (a k) n")).then_inc(raw_in[c.slot(4)], 16)

            stage = 0
            for b in range(2):
                for j in (3, 0, 1, 2):
                    piece(b, j)
            sp.dma_start(xT[:, :, :], xt).then_inc(x_in, 16)
            with sp.Fori(2, NMOD1 - 1) as b:
                for j in (0, 3, 1, 2):
                    piece(b, j)
            load(At(0), w16[0:1], free=False)
            for j in (3, 0, 1, 2):
                piece(NMOD1 - 1, j)
            for j in range(1, 4):
                load(At(j), w16[j:j + 1], free=False)

            def riding(n, c0, b0, js, ring=4):
                with sp.Fori(0, n) as i:
                    for j in range(8):
                        load(at(c0 + j, i, 8), w16[one(i * 8 + (c0 + j))])
                        if j in js:
                            n = js.index(j)
                            piece(i + b0, (0, 3, 1, 2)[n] if ring == 4 else n, ring)

            def plain(a, b, arr=None, off=0, k=16):
                arr = w16 if arr is None else arr
                n = (b - a) // 4
                if n > 0:
                    with sp.Fori(0, n) as i:
                        for j in range(4):
                            load(at(a + j, i, 4), arr[one(i * 4 + (a + j - off))], k)
                for c in range(a + 4 * n, b):
                    load(At(c), arr[c - off:c - off + 1], k)

            riding(4, 4, 8, (0, 1, 2, 3))
            plain(36, C0["sp0"] + 4)
            stage = 1
            for h in range(2):
                sp.wait_ge(grp, 4 * h + 5)
                riding(2, C0[f"sp{h}"] + 4, 12 + 2 * h, (0, 1, 2, 3))
                plain(C0[f"sp{h}"] + 20, C0["sp1"] + 4 if h == 0 else C0["ga"])
            for n, ph in enumerate(("ga", "wo")):
                riding(2, C0[ph], 16 + 2 * n, (0, 2, 4, 6), 2)
            plain(C0["fi"], C0["fi"] + 4)
            stage = 2
            sp.wait_ge(used, 2 * C0["fi"])
            riding(4, C0["fi"] + 4, 20, (0, 2, 4, 6), 2)
            plain(C0["fi"] + 36, C0["fo"])
            plain(C0["fo"], C0["fo"] + NFO, w11, C0["fo"], KFO)
            plain(C0["lx"], CHUNKS, w16, NFO)
            for n in range(4):
                sp.wait_ge(out_ok, n + 1)
                if n:
                    sp.wait_ge(out_st, 16 * n)
                sp.dma_start(out[:, n * 4 * S:(n + 1) * 4 * S],
                             x2T[:, 4 * n:4 * n + 4, :].rearrange("p k n -> p (k n)")).then_inc(out_st, 16)
            sp.wait_ge(out_st, 64)

        NRUN = CHUNKS

        @block.gpsimd
        def _(pool):
            def lo(c):
                pool.wait_ge(hi_done, c.times(2, 1))
                nc.gpsimd.tensor_tensor(wlo[:, c.slot(2), 0:8, :], raw[:, c.slot(4), 0:8, :],
                                        whi[:, c.slot(2), 0:8, :].bitcast(F32), ALU.subtract).then_inc(lo_a, 1)

            def run(a, b):
                n = (b - a) // 16
                if n > 0:
                    with pool.Fori(0, n) as i:
                        for j in range(16):
                            lo(at(a + j, i, 16))
                for c in range(a + 16 * n, b):
                    lo(At(c))

            def mod_scale(b, buf, slot=3):
                pool.wait_ge(mod_in[3], b * 16 + 16)
                nc.gpsimd.tensor_tensor(buf[:, slot, :, :], buf[:, slot, :, :],
                                        cact[:, 12:16].rearrange("p (k a) -> p k a", a=1).to_broadcast([P, 4, 512]), ALU.mult)
                pool.drain()

            def mod_add(b, buf, slot=3, acc=None, ahead=0):
                nc.gpsimd.tensor_tensor(buf[:, slot, 0:2, :], buf[:, slot, 0:2, :], buf[:, slot, 2:4, :], ALU.add)
                pool.drain()
                if not isinstance(b, int) or b > ahead:
                    pool.wait_ge(mod_mm, b - ahead)
                nc.gpsimd.tensor_tensor((acc or macp)[:, :], buf[:, slot, 0, :], buf[:, slot, 1, :], ALU.add).then_inc(modp_used, 1)

            def lo_quarter(n, src):
                pool.wait_ge(quarter_hi, n + 1)
                t = slice(4 * (n % 4), 4 * (n % 4) + 4)
                nc.gpsimd.tensor_tensor(act_lo[:, t, :], src[:, t, :], act_hi[:, t, :].bitcast(F32), ALU.subtract).then_inc(quarter_lo, 1)

            pool.wait_ge(cact_ok, 1)
            for b in range(NMOD1):
                mod_scale(b, mraw_a)
                mod_add(b, mraw_a, 3, (macp, macp1)[b % 2], 1)
                if b == 7:
                    lo(At(0))
                if b >= 5:
                    lo_quarter(b - 5, xT)
            lo_quarter(3, xT)

            def riding(n, c0, b0, j0, buf, slot=3):
                with pool.Fori(0, n) as i:
                    for j in range(8):
                        lo(at(c0 + 1 + j, i, 8))
                        if j == j0:
                            mod_scale(i + b0, buf, slot)
                        if j == j0 + 2:
                            mod_add(i + b0, buf, slot)

            riding(4, 0, 8, 3, mraw_a)
            run(33, C0["sp0"] + 1)
            for h in range(2):
                pool.wait_ge(grp, 4 * h + 5)
                riding(2, C0[f"sp{h}"], 12 + 2 * h, 3, mraw_b)
                run(C0[f"sp{h}"] + 17, C0["sp1"] + 1 if h == 0 else C0["ga"] + 1)
            for n, ph in enumerate(("ga", "wo")):
                riding(2, C0[ph], 16 + 2 * n, 4, mraw_b, 1)
            for m in range(4, 8):
                lo_quarter(m, sq1)
            run(C0["fi"] + 1, C0["fi"] + 5)
            riding(4, C0["fi"] + 4, 20, 4, mraw_c, 1)
            run(C0["fi"] + 37, C0["lx"] + 1)
            for m in range(8, 12):
                lo_quarter(m, accM)
            run(C0["lx"] + 1, CHUNKS)

        @block.tensor
        def _(pe):
            def chunk(c, e, rhs, nk=16, start=True, stop=True, n=S):
                if start and (e.terms or e.base >= 2):
                    pe.wait_ge(evac, e.times(1, -1))
                acc = accp[:, e.slot(2), 0:n]
                for h in range(2):
                    pe.wait_ge(lo_b if h else lo_a, c.times(1, 1))
                    for k in range(8 * h, min(nk, 8 * h + 8)):
                        xh, xl = rhs(k)
                        wh, wl = whi[:, c.slot(2), k, :], wlo[:, c.slot(2), k, :]
                        first = start and k == 0
                        last = stop and k == nk - 1
                        pe.matmul(acc, wh, xh, start=first, stop=False)
                        pe.matmul(acc, wh, xl, start=False, stop=False)
                        mm = pe.matmul(acc, wl, xh, start=False, stop=last)
                    mm.then_inc(used, 1)

            def acts(k):
                return act_hi[:, k, :], act_lo[:, k, :]

            def mod_block(b, mc=None, mp=None):
                pe.wait_ge(macc_ok, b + 1)
                pe.wait_ge(modp_used, b + 1)
                mc, mp = mc or macc, mp or macp
                if not (isinstance(b, int) and b == 0):
                    pe.wait_ge(mod_ok, b)
                for j in range(4):
                    pe.matmul(pw[:, 5, j:j + 1], mc[:, j * P:(j + 1) * P], ones[:, 0:1], start=True, stop=False)
                    mm = pe.matmul(pw[:, 5, j:j + 1], mp[:, j * P:(j + 1) * P], ones[:, 0:1], start=False, stop=True)
                mm.then_inc(mod_mm, 1)

            def first_chunk(c, e, n):
                def rhs(k):
                    if k % 4 == 0:
                        pe.wait_ge(quarter_lo, 4 * n + k // 4 + 1)
                    return acts(k)
                chunk(c, e, rhs)

            def rms(n, src):
                pe.wait_ge(rq, n)
                for k in range(DT):
                    mm = pe.matmul(pw[:, 4, 0:S], ones[:, :], src[:, k, :], start=k == 0, stop=k == DT - 1)
                mm.then_inc(rm, 1)

            def rms_summed(n, cols):
                pe.wait_ge(rq, n)
                pe.matmul(pw[:, 4, 0:cols], ones[:, :], ssum[:, :, :].rearrange("p a n -> p (a n)")[:, 0:cols],
                          start=True, stop=True).then_inc(rm, 1)

            pe.wait_ge(ones_ok, 1)
            for b in range(NMOD1):
                if b == 2:
                    rms(1, sqT)
                mod_block(b, (macc, macc1)[b % 2], (macp, macp1)[b % 2])
            first_chunk(At(0), At(0), 0)

            def qkv_part(i):
                for j in range(8):
                    if not (isinstance(i, int) and j == 0):
                        chunk(at(j, i, 8), at(j, i, 8), acts)
                    if j == 7:
                        mod_block(i + 8)

            qkv_part(0)
            with pe.Fori(1, 4) as i:
                qkv_part(i)
            for c in range(32, 37):
                chunk(At(c), At(c), acts)

            pe.wait_ge(oneh_in, 16)
            pe.wait_ge(mod_ok, 12)
            for g in range(3):
                mm = pe.matmul(pw[0:4, g, :], C("rel", 4 * g, 4)[0:33, :], oneh[0:33, g, :], start=True, stop=True)
            mm.then_inc(brow_mm, 1)
            def gs_chunk(c):
                chunk(At(C0["gs"] + c), At(E0["gs"] + c), acts)

            gs_chunk(0)
            for n in range(6):
                if n >= 2:
                    pe.wait_ge(tp_ev, n - 1)
                for m in range(2):
                    for t in range(2):
                        mm = pe.transpose(pw[:, 4 + n % 2, (2 * m + t) * P:(2 * m + t + 1) * P],
                                          qkv[:, 24 + 2 * n + m, t * P:(t + 1) * P], ident)
                mm.then_inc(tp_mm, 1)

            def logits(u):
                j, q = UNITS[u]
                nk = P * (q + 1)
                if u == 0:
                    pe.wait_ge(brow_ev, 1)
                else:
                    pe.wait_ge(aA, u)
                flat = pw[:, 0:2, :].rearrange("p b n -> p (b n)")
                for g in range(3):
                    mm = pe.matmul(flat[:, g * S:g * S + nk], qkv[:, 4 * g + j, q * P:(q + 1) * P],
                                   qkv[:, 12 + 4 * g + j, 0:nk], start=True, stop=True)
                mm.then_inc(aL, 1)

            def turn(u):
                j, q = UNITS[u]
                pe.wait_ge(aB, u + 1)
                if u:
                    pe.wait_ge(aC, u)
                flat = pw[:, 2:4, :].rearrange("p b n -> p (b n)")
                for g in range(3):
                    for t in range(q + 1):
                        mm = pe.transpose(flat[:, (2 * g + t) * P:(2 * g + t + 1) * P],
                                          lgt[:, u % 2, g, t * P:(t + 1) * P], ident)
                mm.then_inc(aT, 1)

            def values(u):
                j, q = UNITS[u]
                pe.wait_ge(aC, u + 1)
                if u:
                    pe.wait_ge(aF, u)
                else:
                    pe.wait_ge(tp_ev, 6)
                n = 0
                for g in range(3):
                    for t in range(q + 1):
                        n += 1
                        mm = pe.matmul(pw[:, 4, 0:P], vnat[:, t, 4 * g + j, :], pT[:, u % 2, 2 * g + t, :],
                                       start=n == 1, stop=n == 3 * (q + 1))
                mm.then_inc(aO, 1)

            gs_chunk(1)
            logits(0)
            gs_chunk(2)
            for u in range(8):
                if u + 1 < 8:
                    logits(u + 1)
                for c in GS[u][1:]:
                    gs_chunk(c - 1)
                if u:
                    values(u - 1)
                gs_chunk(GS[u][-1])
                turn(u)
            values(7)
            pe.wait_ge(dt_ex, 1)
            pe.wait_ge(aA, 8)
            for t in range(2):
                pe.transpose(pw[:, 0, 64 * t:64 * t + 64], dts[:, 0, t * P:(t + 1) * P], ident[0:64, 0:64])
                pe.transpose(pw[:, 0, 128 + 64 * t:192 + 64 * t], dts[:, 1, t * P:(t + 1) * P], ident[0:64, 0:64])
            pe.transpose(pw[:, 0, 256:320], dts[:, 2, 0:P], ident[0:64, 0:64]).then_inc(dt_mm, 1)

            def group(i, h, gg):
                g = at(4 * h + gg, i, 2)
                ph = f"ssm{h}"
                bc, x = bct[:, gg], xs[:, gg]
                for j in range(10):
                    chunk(at(C0[ph] + 10 * gg + j, i, 20), at(E0[ph] + 10 * gg + j, i, 20), acts)
                    if j == 2:
                        pe.wait_ge(silu_d, g.times(6, 2 + 2))
                        pe.wait_ge(cb_ev, g.times(1, 1))
                        pe.wait_ge(y_ev, g.times(4, 1))
                        for t in range(2):
                            pe.matmul(pw[:, 0, t * P:(t + 1) * P], bc[:, 0, t * P:(t + 1) * P],
                                      bc[:, 1, t * P:(t + 1) * P], start=True, stop=True)
                        pe.transpose(pw[:, 0, 256:384], bc[:, 0, 0:P], ident).then_inc(cb_mm, 1)
                    if 4 <= j < 8:
                        t = j - 4
                        pe.wait_ge(silu_d, g.times(6, 2 + 3 + t))
                        pe.wait_ge(xt_ev, g.times(4, t + 1))
                        for q in range(2):
                            mm = pe.transpose(pw[:, 5 if t % 2 else 1, q * P:(q + 1) * P],
                                              x[:, t, q * P:(q + 1) * P], ident)
                        mm.then_inc(xt_mm, 1)
                    if j == 8:
                        pe.wait_ge(xdd_ok, g.times(1, 1))
                        pe.wait_ge(s0_ev, g.times(1, 1))
                        pe.matmul(pw[:, 2, :], bnat[:, :], xdd[:, :], start=True, stop=True).then_inc(s0_mm, 1)
                pe.wait_ge(m_ok, g.times(1, 1))
                pe.wait_ge(ce_ok, g.times(1, 1))
                pe.wait_ge(s0_ev, g.times(1, 2))
                pe.wait_ge(y_ev, g.times(4, 1))
                for t in range(4):
                    for r in range(2):
                        hh = 2 * t + r
                        o = pw[64 * r:64 * r + 64, YB[t], 0:S]
                        hc = slice(hh * 64, hh * 64 + 64)
                        pe.matmul(o[:, 0:P], xdt[:, 0, hc], dec[:, hh, 0, :], start=True, stop=True)
                        pe.matmul(o[:, P:S], xdt[:, 1, hc], dec[:, hh, 1, :], start=True, stop=False)
                        mm = pe.matmul(o[:, P:S], st0[:, hc], acb[:, hh, 1, :], start=False, stop=True)
                    mm.then_inc(y_mm, 1)
                for t in range(4):
                    pe.wait_ge(sq_ok, g.times(4, t + 1))
                    pe.matmul(pw[:, 5, 0:S], ones[:, :], sq[:, :], start=t == 0, stop=t == 3).then_inc(ssq_mm, 1)

            def eight(ph, b0, rhs, first=None):
                def part(i):
                    for j in range(8):
                        chunk(at(C0[ph] + j, i, 8), at(E0[ph] + j, i, 8), first if first and isinstance(i, int) and j == 0 else rhs)
                    mod_block(i + b0)
                part(0)
                with pe.Fori(1, 2) as i:
                    part(i)

            def late(rhs, k0, sm, n):
                def f(k):
                    if k == k0:
                        pe.wait_ge(sm, n)
                    return rhs(k)
                return f

            def ys(k):
                return y_hi[:, k, :], y_lo[:, k, :]

            for h in range(2):
                with pe.Fori(0, 2) as i:
                    group(i, h, 0)
                    group(i, h, 1)
                pe.wait_ge(grp, 4 * h + 4)

                eight(f"sp{h}", 12 + 2 * h, ys, late(ys, 12, grp, 4 * h + 5))
                pe.wait_ge(mod_ok, 14 + 2 * h)

            for c in range(4):
                for h in range(2):
                    e = E0["ap"] + 2 * c + h
                    pe.wait_ge(evac, e - 1)
                    pe.wait_ge(lo_b if h else lo_a, C0["ap"] + c + 1)
                    for m in range(2):
                        for k in range(4):
                            kk, s2 = 8 * h + 4 * m + k, (C0["ap"] + c) % 2
                            acc = accp[:, e % 2, m * S:(m + 1) * S]
                            pe.matmul(acc, whi[:, s2, kk, :], att_hi[:, k, :], start=k == 0, stop=False)
                            pe.matmul(acc, whi[:, s2, kk, :], att_lo[:, k, :], start=False, stop=False)
                            mm = pe.matmul(acc, wlo[:, s2, kk, :], att_hi[:, k, :], start=False, stop=k == 3)
                    mm.then_inc(used, 1)
            eight("ga", 16, acts)
            merged = lambda k: (mg_hi[:, k, :], mg_lo[:, k, :])
            pe.wait_ge(post, 4 + POST0["wo"])
            eight("wo", 18, merged, late(merged, 15, acts_ok, 2))
            rms_summed(2, S)
            first_chunk(At(C0["fi"]), At(E0["fi"]), 1)
            for j in range(1, 4):
                chunk(At(C0["fi"] + j), At(E0["fi"] + j), acts)
            with pe.Fori(0, 4) as i:
                for j in range(8):
                    chunk(at(C0["fi"] + 4 + j, i, 8), at(E0["fi"] + 4 + j, i, 8), acts)
                mod_block(i + 20)
            with pe.Fori(3, 2 * FF_T // 12) as i:
                for j in range(12):
                    chunk(at(C0["fi"] + j, i, 12), at(E0["fi"] + j, i, 12), acts)
            for j in range(2 * FF_T // 12 * 12, 2 * FF_T):
                chunk(At(C0["fi"] + j), At(E0["fi"] + j), acts)
            def down(i):
                for m in range(2):
                    for q in range(4):
                        rhs = lambda k, q=q: (hid_hi[:, KFO * q + k, :], hid_lo[:, KFO * q + k, :])
                        if isinstance(i, int) and m == 0 and q == 3:
                            rhs = late(rhs, KFO - 1, acts_ok, 4)
                        chunk(at(C0["fo"] + 4 * m + q, i, 8), at(E0["fo"] + m, i, 2), rhs,
                              nk=KFO, start=q == 0, stop=q == 3)

            pe.wait_ge(post, 4 + POST0["fo"])
            down(0)
            with pe.Fori(1, 8) as i:
                down(i)

            rms_summed(3, 2 * S)

            def sixteen(ph, rhs=acts, first=None):
                def part(i):
                    for j in range(8):
                        chunk(at(C0[ph] + j, i, 8), at(E0[ph] + j, i, 8), first if first and isinstance(i, int) and j == 0 else rhs)
                part(0)
                with pe.Fori(1, 2) as i:
                    part(i)

            def halves(c, e, rhs, kts, ms=1):
                for h in range(2):
                    pe.wait_ge(lo_b if h else lo_a, c.times(1, 1))
                    n = 8 // kts // ms
                    for r in range(n):
                        eh = e + (h * n + r)
                        pe.wait_ge(evac, eh.times(1, -1))
                        for m in range(ms):
                            for k in range(kts):
                                kk = 8 * h + (r * ms + m) * kts + k
                                xh, xl = rhs(k)
                                acc = accp[:, eh.slot(2), m * S:(m + 1) * S]
                                pe.matmul(acc, whi[:, c.slot(2), kk, :], xh, start=k == 0, stop=False)
                                pe.matmul(acc, whi[:, c.slot(2), kk, :], xl, start=False, stop=False)
                                mm = pe.matmul(acc, wlo[:, c.slot(2), kk, :], xh, start=False, stop=k == kts - 1)
                    mm.then_inc(used, 1)

            def branch(ph, n):
                if n == 7:
                    pe.wait_ge(acts_ok, n)

                def half(i):
                    for j in range(4):
                        def rhs(k):
                            if n > 7 and isinstance(i, int) and j == 0 and k % 4 == 0:
                                pe.wait_ge(yb_ok, 2 * (n - 8) + k // 4 + 1)
                            return yb_hi[:, k, :], yb_lo[:, k, :]
                        halves(at(C0["wb" + ph] + j, i, 4), at(E0["wb" + ph] + 2 * j, i, 8), rhs, 8)

                half(0)
                with pe.Fori(1, 2) as i:
                    half(i)
                sixteen("mg" + ph)

            first_chunk(At(C0["lx"]), At(E0["lx"]), 2)
            for j in range(1, 8):
                chunk(At(C0["lx"] + j), At(E0["lx"] + j), acts)
            for i in range(2):
                chunk(At(C0["lg"] + 4 * i), At(E0["lg"] + 4 * i), acts)
                pe.wait_ge(uc_ok, 1)
                pe.wait_ge(wab_in, 16 * (i + 1))
                if i:
                    pe.wait_ge(lru_g, i)
                for t in range(4):
                    for w in range(2):
                        mm = pe.matmul(pw[:, t, w * S:(w + 1) * S], wabs[:, t, w, :], uc[:, 4 * i + t, :], start=True, stop=True)
                mm.then_inc(lru_mm, 1)
                for j in range(1, 4):
                    chunk(At(C0["lg"] + 4 * i + j), At(E0["lg"] + 4 * i + j), acts)
            branch("a", 7)
            chunk(At(C0["bf"]), At(E0["bf"]), acts)
            def head_sum(n, cols=512):
                pe.wait_ge(hq, n + 1)
                if n:
                    pe.wait_ge(hv, n)
                else:
                    pe.wait_ge(gn_ok, 1)
                src = hq_[:, n % 2, :] if cols == 512 else kcs[:, 0, :]
                pe.matmul(pw[:, 5, 0:cols], ones[:, :], src, start=True, stop=True).then_inc(hm, 1)

            def transposes(srcs, n0):
                for n in range(len(srcs) // 2):
                    if n0 + n >= 2:
                        pe.wait_ge(tp_ev, n0 + n - 1)
                    for m in range(2):
                        for t in range(2):
                            mm = pe.transpose(pw[:, 2 + (n0 + n) % 2, (2 * m + t) * P:(2 * m + t + 1) * P],
                                              srcs[2 * n + m][:, t * P:(t + 1) * P], ident)
                    mm.then_inc(tp_mm, 1)

            for c in range(20):
                chunk(At(C0["nq"] + c), At(E0["nq"] + c), acts)
                if c == 1:
                    pe.wait_ge(zf_ok, 2)
                    for t in range(2):
                        mm = pe.transpose(pw[:, 5, t * P:(t + 1) * P], zf[:, t * P:(t + 1) * P], ident)
                    mm.then_inc(gn_mm, 1)
                if c - 2 in NSA_N:
                    head_sum(NSA_N.index(c - 2))
            pe.wait_ge(kp_ok, 1)
            for j in range(8):
                x, c, e = j // 4, C0["cmp"] + j, E0["cmp"] + j // 4
                acc = accp[0:30, e % 2, 0:256]
                for h in range(2):
                    pe.wait_ge(lo_b if h else lo_a, c + 1)
                    if j % 4 == 0 and h == 0:
                        pe.wait_ge(evac, e - 1)
                    for k in range(4 * h, 4 * h + 4):
                        kk = 8 * (j % 4) + k
                        wh, wl = (w[:, c % 2, 2 * k:2 * k + 2, :].rearrange("p a n -> p (a n)") for w in (whi, wlo))
                        pe.matmul(acc, kp_hi[:, x, kk, :], wh, start=kk == 0, stop=False)
                        pe.matmul(acc, kp_lo[:, x, kk, :], wh, start=False, stop=False)
                        mm = pe.matmul(acc, kp_hi[:, x, kk, :], wl, start=False, stop=kk == 31)
                    mm.then_inc(used, 1)
            pe.wait_ge(evac, E0["cmp"] + 2)
            for n in range(4):
                mm = pe.transpose(pw[:, 4, 30 * n:30 * n + 30], hct[0:30, n // 2, n % 2 * P:n % 2 * P + P], ident[0:30, 0:30])
            mm.then_inc(hct_mm, 1)
            chunk(At(C0["ng"]), At(E0["ng"]), acts)
            pe.wait_ge(cw2_in, 16)
            pe.wait_ge(hct_ev, 1)
            for m in range(2):
                pe.matmul(pw[:, 0, 0:30], cw2s[:, 0, m, :], hc[:, 0, m, :], start=m == 0, stop=m == 1)
            for x in range(2):
                for m in range(2):
                    mm = pe.matmul(pw[0:15, 1, x * P:(x + 1) * P], hc[:, 1, m, 15 * x:15 * x + 15], cw2s[:, 1, m, :], start=m == 0, stop=m == 1)
            mm.then_inc(kc_mm, 1)
            transposes([nk[:, n, :] for n in (14, 15, 18, 19)], 6)
            chunk(At(C0["ng"] + 1), At(E0["ng"] + 1), acts)
            head_sum(6, 30)

            def att_logits(b):
                kind, h0, q = BATCH[b]
                n = P * (q + 1) if kind else 15
                if b in (0, NSA_B):
                    pe.wait_ge(hn_ok, 7 if b == 0 else 15)
                    pe.wait_ge(tp_ev, 8 if b == 0 else 12)
                if b:
                    pe.wait_ge(aA, 8 + b)
                for r in range(4):
                    h = h0 + r
                    kv = h0 // 4
                    o = pw[:, r // 2, (r % 2) * S:(r % 2) * S + n]
                    qq = (fx if kind == 3 else nk)[:, h, q * P:(q + 1) * P]
                    kk = (kcT[:, 15 * kv:15 * kv + 15], nk[:, 12 + kv, 0:n], nk[:, 16 + kv, 0:n], fx[:, 8 + h, 0:n])[kind]
                    mm = pe.matmul(o, qq, kk, start=True, stop=kind != 3)
                    if kind == 3:
                        mm = pe.matmul(o, nudge[:, h:h + 1].to_broadcast([P, P]), zf[:, 0:n], start=False, stop=True)
                mm.then_inc(aL, 1)

            def att_turn(b):
                kind, h0, q = BATCH[b]
                pe.wait_ge(aB, 8 + b + 1)
                pe.wait_ge(aC, 8 + b)
                src = (lg3 if kind == 3 else lg2)[:, b % 2]
                for r in range(4):
                    for t in range(q + 1 if kind else 1):
                        rows, n = (P, P) if kind else (15, 15)
                        mm = pe.transpose(pw[0:rows, 2 + r // 2, (2 * (r % 2) + t) * P:(2 * (r % 2) + t + 1) * P],
                                          src[:, r, t * P:t * P + n], ident)
                mm.then_inc(aT, 1)

            def att_values(b):
                kind, h0, q = BATCH[b]
                kv = h0 // 4
                pe.wait_ge(aC, 8 + b + 1)
                opens = kind in (0, 3)
                if opens:
                    pe.wait_ge(aF, 8 + sum(x < b for x in CLOSED))
                for r in range(4):
                    o = pw[:, 4, r * P:(r + 1) * P]
                    ts = range(q + 1 if kind else 1)
                    for t in ts:
                        if kind == 0:
                            l, x = vcn[0:15, kv, :], pT2[0:15, b % 2, 2 * r, :]
                        elif kind == 3:
                            l, x = vn3[:, t, h0 + r, :], pT3[:, b % 2, 2 * r + t, :]
                        else:
                            l, x = vn2[:, t, 2 * (kind - 1) + kv, :], pT2[:, b % 2, 2 * r + t, :]
                        mm = pe.matmul(o, l, x, start=opens and r == 0 and t == 0,
                                       stop=kind >= 2 and t == q and r == 3, skip_group_check=True)
                mm.then_inc(aO, 1)

            def attention(b0, b1, ph):
                att_logits(b0)
                for b in range(b0, b1):
                    if b + 1 < b1:
                        att_logits(b + 1)
                    rides = RIDES.get(b, [])
                    for c in rides[1:]:
                        chunk(At(C0[ph] + c - 1), At(E0[ph] + c - 1), acts)
                    if b > b0:
                        att_values(b - 1)
                    for c in rides[-1:]:
                        chunk(At(C0[ph] + c), At(E0[ph] + c), acts)
                    att_turn(b)
                att_values(b1 - 1)

            attention(0, NSA_B, "ng")
            branch("b", 8)
            for c in range(25):
                if c < 24:
                    chunk(At(C0["fx"] + c), At(E0["fx"] + c), acts)
                if 2 <= c < 18 and c % 2 == 0:
                    head_sum(6 + c // 2)
                if c >= 18 and c % 2 == 0:
                    pe.wait_ge(evac, E0["fx"] + c)
                    transposes([fx[:, c - 2, :], fx[:, c - 1, :]], c // 2 - 1)
            attention(NSA_B, len(BATCH), "fg")
            branch("c", 9)
            merged2 = lambda k: (m2_hi[:, k, :], m2_lo[:, k, :])
            pe.wait_ge(post, 4 + POST0["w2"])
            sixteen("w2", merged2, late(merged2, 15, acts_ok, 10))
            pe.wait_ge(p_ok, 1)
            for c in range(2):
                halves(At(C0["ple"] + c), At(E0["ple"] + 4 * c), lambda k: (p_hi[:, k, :], p_lo[:, k, :]), 2, ms=2)
            pe.wait_ge(h_ok, 1)
            chunk(At(C0["pg"]), At(E0["pg"]), acts)
            rms(4, sqF)
            for j in range(1, 4):
                chunk(At(C0["pg"] + j), At(E0["pg"] + j), acts)
            with pe.Fori(1, 4) as i:
                for j in range(4):
                    chunk(at(C0["pg"] + j, i, 4), at(E0["pg"] + j, i, 4), acts)

        @block.scalar
        def _(act):
            def hi_half(c, h):
                if not c.terms and c.base >= NRUN:
                    return
                if h == 0:
                    act.wait_ge(raw_in[c.slot(4)], c.round(4, 16, 16))
                if c.terms or c.base >= 2:
                    act.wait_ge(used, c.times(2, h - 3))
                act.activation(whi[:, c.slot(2), 8 * h:8 * h + 8, :], raw[:, c.slot(4), 8 * h:8 * h + 8, :],
                               ACT.Copy).then_inc(hi_done, 1)

            def split_hi(c):
                hi_half(c, 1)
                hi_half(c + 1, 0)

            def take(c, e, out, func=ACT.Copy, n=S, rows=P, **kw):
                act.wait_ge(used, c.times(2, 2))
                act.activation(out, accp[0:rows, e.slot(2), 0:n], func, **kw).then_inc(evac, 1)

            def root(n, o, v):
                act.wait_ge(rv, n)
                act.activation(o, v, ACT.Sqrt).then_inc(rs, 1)

            def warm_root():
                act.activation(spl[:, 0:1], C("ident"), ACT.Sqrt)

            act.wait_ge(cst_in, 16)
            act.activation(cact[:, :], C("c", 0, 16), ACT.Silu).then_inc(cact_ok, 1)
            act.wait_ge(x_in, 16)
            act.activation(sqT[:, :, :], xT[:, :, :], ACT.Square).then_inc(rq, 1)
            for n in range(2):
                act.activation(nudge[:, n:n + 1], C("c", n, 1), ACT.Copy).then_inc(silu_d, 1)
            act.activation(nudge[:, 2:3], C("c"), ACT.Copy).then_inc(s0_ev, 1)
            root(1, rstd[:, :], sqT[:, 0, :])

            def hi_quarter(n, src):
                act.wait_ge(quarter, n + 1)
                t = slice(4 * (n % 4), 4 * (n % 4) + 4)
                act.activation(act_hi[:, t, :], src[:, t, :], ACT.Copy).then_inc(quarter_hi, 1)

            hi_quarter(0, xT)
            hi_quarter(1, xT)
            hi_half(At(0), 0)
            split_hi(At(0))
            hi_quarter(2, xT)
            hi_quarter(3, xT)

            def qkv_part(i):
                for j in range(4):
                    c = at(j, i, 4)
                    split_hi(c + 1)
                    take(c, c, qkv[:, one(i * 4 + j), :])

            qkv_part(0)
            with act.Fori(1, 9) as i:
                qkv_part(i)
            act.wait_ge(mod_ok, 12)
            act.dma_start(oneh[:, :, :], onehot).then_inc(oneh_in, 16)
            split_hi(At(37))
            act.wait_ge(mod_ok, 12)
            take(At(36), At(36), dtr[:, :], ACT.Identity, rows=64, bias=C("dtb")[0:64, :])
            act.wait_ge(spx, 1)
            act.activation(dts[:, 2, :], dts[:, 1, :], ACT.Exp, scale=-1.0).then_inc(spe, 1)
            act.activation(aneg[0:64, :], C("alog")[0:64, :], ACT.Exp).then_inc(spe, 1)
            act.wait_ge(brow_mm, 1)
            for g in range(3):
                ins = act.activation(brow[:, g, :], pw[0:4, g, :], ACT.Copy)
            ins.then_inc(brow_ev, 1)
            act.wait_ge(brow_ev, 1)
            act.dma_start(br_d, brow[:, :, :].rearrange("j g n -> j (g n)")).then_inc(brow_st, 16)

            def gs_take(c):
                if c % 4 == 0 and c >= 8:
                    act.wait_ge(gs_st, 16 * (c // 4 - 1))
                split_hi(At(C0["gs"] + c + 1))
                take(At(C0["gs"] + c), At(E0["gs"] + c), gsb[:, c % 8, :], ACT.Sigmoid)
                if c % 4 == 3:
                    n = c // 4
                    act.wait_ge(evac, E0["gs"] + c + 1)
                    if n:
                        act.wait_ge(gs_st, 16 * n)
                    act.dma_start(gs_d[:, n * 4 * S:(n + 1) * 4 * S],
                                  gsb[:, n % 2 * 4:n % 2 * 4 + 4, :].rearrange("p k n -> p (k n)")).then_inc(gs_st, 16)

            gs_take(0)
            act.wait_ge(brow_st, 16)
            for j in range(4):
                act.dma_start(bw_d[j], br_d[j:j + 1, :].to_broadcast([P, 1536])).then_inc(brow_st, 16)
            for n in range(6):
                act.wait_ge(tp_mm, n + 1)
                act.activation(vnat[:, :, 2 * n:2 * n + 2, :].rearrange("p t m d -> p m t d"),
                               pw[:, 4 + n % 2, :].rearrange("p (m t d) -> p m t d", m=2, t=2),
                               ACT.Copy).then_inc(tp_ev, 1)

            def bias(u):
                j, q = UNITS[u]
                nk = P * (q + 1)
                src = bass.AP(tensor=bw_d.tensor, offset=bw_d.offset + j * P * 1536 + 255 - P * q,
                              ap=[[1535, P], [512, 3], [1, nk]])
                act.dma_start(biasT[:, u % 2, :, 0:nk], src).then_inc(bias_in[u % 2], 16)

            gs_take(1)
            act.wait_ge(brow_st, 80)
            bias(0)
            gs_take(2)
            for u in range(8):
                if u + 1 < 8:
                    if u:
                        act.wait_ge(aA, u)
                    bias(u + 1)
                j, q = UNITS[u]
                act.wait_ge(aA, u + 1)
                act.activation(lgt[:, u % 2, 0:3, 0:P * (q + 1)], lgt[:, u % 2, 0:3, 0:P * (q + 1)], ACT.Exp,
                               bias=nmx[:, u % 2, 0:1], accum_out=sums[:, u % 2, 0:1]).then_inc(aX, 1)
                for c in GS[u]:
                    gs_take(c)
                act.wait_ge(aT, u + 1)
                if u >= 2:
                    act.wait_ge(aO, u - 1)
                flat = pw[:, 2:4, :].rearrange("p b n -> p (b n)")
                act.activation(pT[:, u % 2, 0:6, :].rearrange("p (g t) n -> p g t n", t=2)[:, :, 0:q + 1, :],
                               flat[:, 0:768].rearrange("p (g t n) -> p g t n", g=3, t=2)[:, :, 0:q + 1, :],
                               ACT.Copy).then_inc(aC, 1)
            act.wait_ge(gs_st, 64)
            act.wait_ge(ac_ok, 1)
            act.activation(dts[:, 2, 0:P], dts[:, 2, 0:P], ACT.Exp).then_inc(dt_ex, 1)
            act.dma_start(ac_d.rearrange("g (r n) -> (g r) n", r=8), dts[:, 1, :]).then_inc(ac_st, 16)
            act.wait_ge(ac_st, 16)

            def group(i, h, gg):
                g = at(4 * h + gg, i, 2)
                ph = f"ssm{h}"
                act.wait_ge(y_ev, g.times(4, 1))
                act.dma_start(acb[:, :, :, :].rearrange("p r t n -> p (r t n)"),
                              ac_d[one(g.times(1)), :].to_broadcast([P, 2048])).then_inc(acb_in, 16)
                for j in range(10):
                    c, e = at(C0[ph] + 10 * gg + j, i, 20), at(E0[ph] + 10 * gg + j, i, 20)
                    split_hi(c + 1)
                    if 1 <= j <= 6:
                        act.wait_ge(conv_d, g.times(6, 2 + j))
                        o = bct[:, gg, j - 1, :] if j <= 2 else xs[:, gg, j - 3, :]
                        act.activation(o, cv[:, (j - 1) % 2, :], ACT.Silu).then_inc(silu_d, 1)
                    if j == 4:
                        act.wait_ge(dec_in, g.times(1, 1))
                        act.activation(dec[:, :, :, :], dec[:, :, :, :], ACT.Exp).then_inc(dec_ex, 1)
                        act.activation(acb[:, :, 1, :], acb[:, :, 1, :], ACT.Exp).then_inc(dec_ex, 1)
                    if j == 9:
                        act.wait_ge(s0_mm, g.times(1, 1))
                        act.activation(st0[:, :], pw[:, 2, :], ACT.Copy).then_inc(s0_ev, 1)
                    if j < 6:
                        act.wait_ge(conv_d, g.times(6, 1 + j))
                        take(c, e, ub[:, j % 2, 3:259])
                    else:
                        if j == 6:
                            act.wait_ge(grp, g.times(1, 1))
                        take(c, e, sz[:, j - 6, :], ACT.Silu)
                for t in range(4):
                    act.wait_ge(y_ev, g.times(4, t + 2))
                    if t:
                        act.wait_ge(ssq_mm, g.times(4, t))
                    act.activation(sq[:, :], sz[:, t, :], ACT.Square).then_inc(sq_ok, 1)
                act.wait_ge(ssq_v, g.times(1, 1))
                act.activation(rstd[:, :], cv[:, 0, :], ACT.Sqrt).then_inc(ssq_r, 1)

            def to_tm(ph, j, i, stride, base, c, e, buf, **kw):
                idx = at(POST0[ph] + base, i, stride)
                act.wait_ge(post, idx.times(1, 1))
                take(c, e, buf[:, idx.slot(4), :], **kw)

            for h in range(2):
                if h:
                    act.wait_ge(mod_ok, 14)
                with act.Fori(0, 2) as i:
                    group(i, h, 0)
                    group(i, h, 1)
                ph = f"sp{h}"
                with act.Fori(0, 4) as i:
                    for j in range(4):
                        c, e = at(C0[ph] + j, i, 4), at(E0[ph] + j, i, 4)
                        split_hi(c + 1)
                        if h == 0:
                            take(c, e, accS[:, one(i * 4 + j), :])
                        else:
                            to_tm(ph, j, i, 4, j, c, e, tm)
            act.wait_ge(lam_x, 1)
            act.activation(lcon[:, 2, :], lcon[:, 1, :], ACT.Exp, scale=-1.0).then_inc(spe, 1)
            for c in range(4):
                split_hi(At(C0["ap"] + c + 1))
                for h in range(2):
                    act.wait_ge(used, 2 * (C0["ap"] + c) + h + 1)
                    act.activation(accA[:, 4 * c + 2 * h:4 * c + 2 * h + 2, :],
                                   accp[:, (E0["ap"] + 2 * c + h) % 2, :].rearrange("p (m n) -> p m n", m=2),
                                   ACT.Copy).then_inc(evac, 1)

            def temps(ph, n, buf, func_of, last=False, first=0):
                def four(i):
                    for j in range(4):
                        c, e = at(C0[ph] + j, i, 4), at(E0[ph] + j, i, 4)
                        split_hi(c + 1)
                        to_tm(ph, j, i, 4, j, c, e, buf, func=func_of(j))
                with act.Fori(first, n - last) as i:
                    four(i)
                if last:
                    four(n - 1)

            act.wait_ge(used, 2 * C0["ga"])

            def gs_load(n):
                act.dma_start(gsr[:, n % 2 * 4:n % 2 * 4 + 4, :].rearrange("p k n -> p (k n)"),
                              gs_d[:, n * 4 * S:(n + 1) * 4 * S]).then_inc(gs_in[n % 2], 16)

            gs_load(0)
            gs_load(1)
            for i in range(4):
                if i in (1, 2):
                    act.wait_ge(post, 4 + POST0["ga"] + 4 * i)
                    gs_load(i + 1)
                temps("ga", i + 1, tm, lambda j: ACT.Sigmoid, first=i)
            act.wait_ge(acts_ok, 2)
            act.dma_start(x1[:, :, :], xt).then_inc(x_in, 16)
            temps("wo", 4, tm, lambda j: ACT.Copy)
            warm_root()
            act.wait_ge(post, 4 + POST0["fi"])
            act.dma_start(x1_d, x1[:, :, :].rearrange("p k n -> p (k n)")).then_inc(x1_st, 16)
            root(2, rstd[:, :], xq[:, 0, :])
            for n in range(4, 8):
                hi_quarter(n, sq1)
            act.wait_ge(acts_ok, 3)
            temps("fi", FF_T // 2, tf, lambda j: ACT.Copy if j % 2 else ACT.Silu)
            act.wait_ge(acts_ok, 4)
            act.wait_ge(used, 2 * C0["fo"])
            act.wait_ge(x1_st, 16)
            act.dma_start(x1r[:, :, :].rearrange("p k n -> p (k n)"), x1_d).then_inc(x1_in, 16)
            with act.Fori(0, 8) as i:
                for m in range(2):
                    for q in range(4):
                        c = at(C0["fo"] + 4 * m + q, i, 8)
                        split_hi(c + 1)
                    e = at(E0["fo"] + m, i, 2)
                    idx = at(POST0["fo"] + m, i, 2)
                    act.wait_ge(post, idx.times(1, 3))
                    take(c, e, tf[:, idx.slot(2), :])


            act.wait_ge(post, 4 + POST0["lx"])
            warm_root()
            root(3, sqF[:, 3, :], sqF[:, 0, :])
            root(4, rstd[:, :], sqF[:, 4, :])
            for n in range(8, 12):
                hi_quarter(n, accM)

            def biased(ph, n, dst, func, lead=True, ring=4):
                with act.Fori(0, n) as i:
                    for j in range(4):
                        c, e = at(C0[ph] + j, i, 4), at(E0[ph] + j, i, 4)
                        split_hi(c + 1)
                        idx = at(POST0[ph] + j, i, 4) if ph in POST0 else None
                        if idx is not None:
                            act.wait_ge(post, idx.times(1, 5 - ring))
                        take(c, e, dst(i, j, idx.slot(4) if idx is not None else 0), func, bias=Cd("b2", i * 4 + (B2[ph] + j)))

            def branch(ph):
                with act.Fori(0, 2) as i:
                    for j in range(4):
                        c = at(C0["wb" + ph] + j, i, 4)
                        split_hi(c + 1)
                        for h in range(2):
                            e = at(E0["wb" + ph] + 2 * j + h, i, 8)
                            act.wait_ge(used, c.times(2, h + 1))
                            act.activation(proj[:, one(i * 8 + (2 * j + h)), :], accp[:, e.slot(2):e.slot(2) + 1, 0:S], ACT.Copy).then_inc(evac, 1)
                biased("mg" + ph, 4, lambda i, j, s: tm2[:, s, :], ACT.Sigmoid)

            act.wait_ge(pad_ok, 1)
            act.dma_start(wabs[:, :, :, :], wab[:, 0:4]).then_inc(wab_in, 16)
            biased("lx", 2, lambda i, j, s: ub2[:, j % 2, 3:259], ACT.Identity, ring=2)
            for i in range(2):
                for j in range(4):
                    c, e = At(C0["lg"] + 4 * i + j), At(E0["lg"] + 4 * i + j)
                    split_hi(c + 1)
                    if j == 1:
                        act.wait_ge(lru_l, i + 1)
                        act.activation(lt[:, :, :], lr[:, :, :], ACT.Tanh)
                        act.activation(la[:, :, :], lr[:, :, :], ACT.Exp, scale=-1.0).then_inc(lru_e, 1)
                    if j == 2:
                        act.wait_ge(lru_w, i + 1)
                        act.activation(lw[:, :, :], lw[:, :, :], ACT.Sqrt).then_inc(lru_q, 1)
                    if i and j == 0:
                        act.wait_ge(lru_y, 1)
                    take(c, e, gl[:, j, :], ACT.Silu, bias=C("b2", B2["lg"] + 4 * i + j))
                    if j == 0:
                        act.wait_ge(lru_mm, i + 1)
                        if not i:
                            act.dma_start(wabs[:, :, :, :], wab[:, 4:8]).then_inc(wab_in, 16)
                        for t in range(4):
                            act.activation(lr[:, t, :], pw[:, t, 0:S], ACT.Sigmoid, bias=C("ba", 4 * i + t))
                            ins = act.activation(li[:, t, :], pw[:, t, S:2 * S], ACT.Sigmoid, bias=C("bx", 4 * i + t))
                        ins.then_inc(lru_g, 1)
            act.wait_ge(acts_ok, 7)
            branch("a")
            c, e = At(C0["bf"]), At(E0["bf"])
            split_hi(c + 1)
            take(c, e, zf[:, :], ACT.Identity, bias=C("b2", B2["bf"]))
            split_hi(c + 2)
            act.wait_ge(spx, 2)
            act.activation(sft[32:40, 1, :], sft[32:40, 0, :], ACT.Exp, scale=-1.0).then_inc(spe, 1)
            act.wait_ge(evac, E0["bf"] + 1)
            act.activation(zf[0:24, :], zf[0:24, :], ACT.Sigmoid).then_inc(zf_ok, 1)

            def head_squares(n, src):
                if n >= 2:
                    act.wait_ge(hm, n - 1)
                act.activation(hq_[:, n % 2, :], src, ACT.Square).then_inc(hq, 1)

            def head_root(n, o, v):
                act.wait_ge(hv, n + 1)
                if n:
                    act.wait_ge(hn_ok, n)
                act.activation(o, v, ACT.Sqrt).then_inc(hr, 1)

            two = lambda t, n: t[:, n:n + 2, :].rearrange("p k n -> p (k n)")
            for c in range(20):
                if c:
                    split_hi(At(C0["nq"] + c + 1))
                if c - 3 in NSA_N:
                    head_root(NSA_N.index(c - 3), hr_[:, :], he_[:, :])
                if c - 2 in NSA_N:
                    if c == 2:
                        act.wait_ge(gn_ok, 1)
                    act.wait_ge(evac, E0["nq"] + c)
                    head_squares(NSA_N.index(c - 2), two(nk, c - 2))
                take(At(C0["nq"] + c), At(E0["nq"] + c), nk[:, c, :], ACT.Identity, bias=C("b2", B2["nq"] + c))
            act.dma_start(cw2s[:, :, :, :], cw2).then_inc(cw2_in, 16)
            for j in range(8):
                split_hi(At(C0["cmp"] + j + 1))
                if j % 4 == 3:
                    c, e = C0["cmp"] + j, E0["cmp"] + j // 4
                    take(At(c), At(e), hct[0:30, j // 4, :], ACT.Silu, n=256, rows=30)

            def gate_of(ph, c):
                split_hi(At(C0[ph] + c + 1))
                take(At(C0[ph] + c), At(E0[ph] + c), gate[:, c, :], ACT.Silu, bias=C("b2", B2[ph] + c))

            act.wait_ge(hct_mm, 1)
            act.activation(hc[:, :, :, :].rearrange("p x m n -> p (x m n)"), pw[:, 4, 0:120], ACT.Copy).then_inc(hct_ev, 1)
            gate_of("ng", 0)

            def copy_out(n, dst):
                act.wait_ge(tp_mm, n + 1)
                act.activation(dst.rearrange("p t m d -> p m t d"),
                               pw[:, 2 + n % 2, :].rearrange("p (m t d) -> p m t d", m=2, t=2), ACT.Copy).then_inc(tp_ev, 1)

            act.wait_ge(kc_mm, 1)
            act.activation(kcT[:, :], pw[:, 0, 0:30], ACT.Copy)
            act.activation(kcs[:, 0, :], pw[:, 0, 0:30], ACT.Square).then_inc(hq, 1)
            act.activation(vcn[:, :, :].rearrange("p a n -> p (a n)"), pw[0:15, 1, 0:256], ACT.Copy).then_inc(kc_ev, 1)
            for n in range(2):
                copy_out(6 + n, vn2[:, :, 2 * n:2 * n + 2, :])
            gate_of("ng", 1)
            head_root(6, kcs[:, 1, :], kcs[:, 2, :])

            def attention(b0, b1, ph):
                for b in range(b0, b1):
                    kind, h0, q = BATCH[b]
                    n = P * (q + 1) if kind else 15
                    l = (lg3 if kind == 3 else lg2)[:, b % 2]
                    act.wait_ge(aA, 8 + b + 1)
                    for r in range(4):
                        kw = {"accum_out": sums[:, b % 2, r:r + 1]} if kind else {}
                        ins = act.activation(l[:, r, 0:n], l[:, r, 0:n], ACT.Exp, bias=nmx[:, b % 2, r:r + 1], **kw)
                    ins.then_inc(aX, 1)
                    for c in RIDES.get(b, []):
                        gate_of(ph, c)
                    act.wait_ge(aT, 8 + b + 1)
                    if b - b0 >= 2:
                        act.wait_ge(aO, 8 + b - 1)
                    pt = (pT3 if kind == 3 else pT2)[:, b % 2].rearrange("p (r t) n -> p r t n", t=2)
                    rows, k = (P, q + 1) if kind else (15, 1)
                    act.activation(pt[0:rows, :, 0:k, :],
                                   pw[0:rows, 2:4, :].rearrange("p b (r t n) -> p (b r) t n", r=2, t=2)[:, :, 0:k, :],
                                   ACT.Copy).then_inc(aC, 1)

            attention(0, NSA_B, "ng")
            act.wait_ge(acts_ok, 8)
            branch("b")
            split_hi(At(C0["fx"] + 1))
            act.wait_ge(post, 4 + POST0["mgc"])
            for c in range(25):
                if 0 < c < 24:
                    split_hi(At(C0["fx"] + c + 1))
                if 3 <= c < 19 and c % 2:
                    head_root(7 + (c - 3) // 2, hr_[:, :], he_[:, :])
                if 2 <= c < 18 and c % 2 == 0:
                    act.wait_ge(evac, E0["fx"] + c)
                    head_squares(6 + c // 2, two(fx, c - 2))
                if c >= 19 and c % 2:
                    copy_out(8 + (c - 19) // 2, vn3[:, :, c - 19:c - 17, :])
                if c < 24:
                    take(At(C0["fx"] + c), At(E0["fx"] + c), fx[:, c, :], ACT.Identity, bias=C("b2", B2["fx"] + c))
            copy_out(11, vn3[:, :, 6:8, :])
            attention(NSA_B, len(BATCH), "fg")
            act.wait_ge(acts_ok, 9)
            branch("c")
            act.wait_ge(acts_ok, 10)
            act.dma_start(p_in[:, :, :], pt).then_inc(p_land, 16)
            temps("w2", 4, tm2, lambda j: ACT.Copy)
            for c in range(2):
                split_hi(At(C0["ple"] + c + 1))
                for h in range(2):
                    act.wait_ge(used, 2 * (C0["ple"] + c) + h + 1)
                    for r in range(2):
                        e = E0["ple"] + 4 * c + 2 * h + r
                        m = 8 * c + 4 * h + 2 * r
                        act.activation(eT[:, m:m + 2, :], accp[:, e % 2, :].rearrange("p (m n) -> p m n", m=2), ACT.Copy).then_inc(evac, 1)
            act.wait_ge(evac, E0["pg"])
            act.activation(sqF[:, :, :], eT[:, :, :], ACT.Square).then_inc(rq, 1)
            for j in range(4):
                c, e = At(C0["pg"] + j), At(E0["pg"] + j)
                split_hi(c + 1)
                to_tm("pg", j, 0, 4, j, c, e, tm2, func=ACT.Sigmoid)
                if j == 0:
                    root(5, rstd[:, :], sqF[:, 0, :])
            temps("pg", 4, tm2, lambda j: ACT.Sigmoid, last=True, first=1)

        @block.vector
        def _(dve):
            def split_lo(c):
                if not c.terms and c.base >= NRUN:
                    return
                dve.wait_ge(hi_done, c.times(2, 2))
                dve.tensor_tensor(wlo[:, c.slot(2), 8:16, :], raw[:, c.slot(4), 8:16, :],
                                  whi[:, c.slot(2), 8:16, :].bitcast(F32), ALU.subtract).then_inc(lo_b, 1)

            def pair(hi, lo, src):
                dve.tensor_copy(hi, src)
                dve.drain()
                return dve.tensor_tensor(lo, src, hi.bitcast(F32), ALU.subtract)

            def rms_root(n, ss, v, width, r=None, sems=None):
                r = rstd[:, :] if r is None else r
                sm, sv, sr, tmp, rec = sems
                dve.wait_ge(sm[0], sm[1])
                dve.tensor_scalar(v, ss, 1.0 / width, EPS, ALU.mult, ALU.add)
                dve.drain()
                dve.reciprocal(rec, v).then_inc(sv, 1)
                dve.wait_ge(sr[0], sr[1])
                newton(r, v, tmp)

            def newton(r, v, tmp):
                dve.tensor_tensor(tmp, r, r, ALU.mult)
                dve.drain()
                dve.tensor_tensor(tmp, tmp, v, ALU.mult)
                dve.drain()
                dve.tensor_scalar(tmp, tmp, -0.5, 1.5, ALU.mult, ALU.add)
                dve.drain()
                dve.tensor_tensor(r, r, tmp, ALU.mult)
                dve.drain()

            def mod_piece(b, j, buf, ring=4, acc=None):
                acc = acc or macc
                dve.wait_ge(mod_in[j], b * 16 + 16)
                for k in range(4):
                    a = 4 * j + k
                    if a == 0:
                        ins = dve.tensor_scalar(acc[:, :], buf[:, 0, 0, :], cact[:, 0:1], None, ALU.mult)
                    else:
                        ins = dve.scalar_tensor_tensor(acc[:, :], buf[:, j % ring, k, :], cact[:, a:a + 1],
                                                       acc[:, :], ALU.mult, ALU.add)
                    if k < 3:
                        dve.drain()
                ins.then_inc(mod_used, 1)
                if j < 2:
                    dve.drain()
                else:
                    dve.drain().then_inc(macc_ok, 1)

            def mod_finish(b):
                dve.wait_ge(mod_mm, b + 1)
                dve.tensor_tensor(modT[:, wide(b, 4)], pw[:, 5, 0:4],
                                  cst[:, bass.ds(b * 4 + CO["bmod"], 4)] if not isinstance(b, int) else C("bmod", 4 * b, 4),
                                  ALU.add).then_inc(mod_ok, 1)

            def softplus(x, t, o, n, x_ok=None):
                ax, e, s, s2 = t
                dve.scalar_tensor_tensor(ax, x, -1.0, x, ALU.mult, ALU.max).then_inc(x_ok or spx, 1)
                dve.wait_ge(spe, n)
                dve.tensor_scalar(s, e, 2.0, None, ALU.add)
                dve.drain()
                dve.reciprocal(s, s)
                dve.drain()
                dve.tensor_tensor(s, s, e, ALU.mult)
                dve.drain()
                dve.tensor_tensor(s2, s, s, ALU.mult)
                dve.drain()
                dve.tensor_scalar(e, s2, 1.0 / 15, None, ALU.mult)
                for d in (13, 11, 9, 7, 5, 3):
                    dve.drain()
                    dve.scalar_tensor_tensor(e, e, 1.0 / d, s2, ALU.add, ALU.mult)
                dve.drain()
                dve.scalar_tensor_tensor(e, e, 1.0, s, ALU.add, ALU.mult)
                dve.tensor_scalar(ax, x, 0.0, None, ALU.max)
                dve.drain()
                dve.scalar_tensor_tensor(o, e, 2.0, ax, ALU.mult, ALU.add)
                dve.drain()

            dve.memset(ones[:, :], 1.0).then_inc(ones_ok, 1)
            for s_, n in ((post, 4), (cb_ev, 1), (xt_ev, 2), (y_ev, 1), (grp, 1)):
                for _ in range(n):
                    dve.memset(nudge[:, 4:5], 0.0).then_inc(s_, 1)
                    dve.drain()
            dve.wait_ge(cact_ok, 1)
            def modulate(m, src, gain, norm, sh, sc):
                t = slice(4 * m, 4 * m + 4)
                dve.drain()
                dve.scalar_tensor_tensor(gain[:, t], modT[:, sc + 4 * m:sc + 4 * m + 4], 1.0, norm[:, t], ALU.add, ALU.mult)
                dve.drain()
                for k in range(4 * m, 4 * m + 4):
                    ins = dve.tensor_scalar(src[:, k, :], src[:, k, :], gain[:, k:k + 1], modT[:, sh + k:sh + k + 1],
                                            ALU.mult, ALU.add)
                ins.then_inc(quarter, 1)

            for b in range(NMOD1):
                for j in range(3):
                    mod_piece(b, j, mraw_a, 4, (macc, macc1)[b % 2])
                    if j == 0 and b == 3:
                        rms_root(1, pw[:, 4, 0:S], sqT[:, 1, :], D, sems=((rm, 1), rv, (rs, 1), sqT[:, 2, :], sqT[:, 0, :]))
                    if j == 0 and b > 3:
                        t = slice(4 * b - 16, 4 * b - 12)
                        dve.tensor_tensor(xT[:, t, :], xT[:, t, :], rstd[:, :].rearrange("p (a n) -> p a n", a=1).to_broadcast([P, 4, S]), ALU.mult)
                    if j == 1 and b:
                        mod_finish(b - 1)
                        if b > 4:
                            modulate(b - 5, xT, gain1, C("n1", 0, 16), 0, 16)
            split_lo(At(0))
            mod_finish(NMOD1 - 1)
            modulate(3, xT, gain1, C("n1", 0, 16), 0, 16)
            dve.drain().then_inc(acts_ok, 1)

            with dve.Fori(0, 4) as i:
                for j in range(8):
                    split_lo(at(j + 1, i, 8))
                    if j in (3, 5, 7):
                        mod_piece(i + 8, (j - 3) // 2, mraw_a)
                    if j == 7:
                        mod_finish(i + 8)
            for c in range(33, 37):
                split_lo(At(c))
            split_lo(At(37))
            dve.wait_ge(evac, 37)
            softplus(dtr[:, :], [dts[:, k, :] for k in (1, 2, 3, 4)], dts[:, 0, :], 2)
            split_lo(At(38))
            dve.tensor_scalar(aneg[0:64, :], aneg[0:64, :], -1.0, None, ALU.mult)
            dve.drain()
            dve.tensor_scalar(dts[:, 3, :], dts[:, 0, :], aneg[0:64, 0:1], None, ALU.mult)
            dve.memset(dts[:, 4, :], 1.0)
            dve.drain()
            for t in range(2):
                dve.tensor_tensor_scan(dts[:, 1, t * P:(t + 1) * P], dts[:, 4, 0:P], dts[:, 3, t * P:(t + 1) * P],
                                       0.0, ALU.mult, ALU.add)
            dve.drain()
            dve.tensor_scalar(dts[:, 2, 0:P], dts[:, 1, 0:P], dts[:, 1, P - 1:P], -1.0, ALU.subtract, ALU.mult).then_inc(ac_ok, 1)

            def biased(u):
                j, q = UNITS[u]
                nk = P * (q + 1)
                dve.wait_ge(aL, u + 1)
                dve.wait_ge(bias_in[u % 2], 16 * (u // 2 + 1))
                if u >= 2:
                    dve.wait_ge(aT, u - 1)
                else:
                    dve.wait_ge(brow_ev, 1)
                flat = pw[:, 0:2, :].rearrange("p b n -> p (b n)")[:, 0:768].rearrange("p (g n) -> p g n", g=3)[:, :, 0:nk]
                l = lgt[:, u % 2, 0:3, 0:nk]
                dve.scalar_tensor_tensor(l, flat, ATT_SCALE, biasT[:, u % 2, :, 0:nk], ALU.mult, ALU.add)
                dve.drain()
                dve.tensor_reduce(mx[:, u % 2, 0:1], l, AX.XY, ALU.max)
                dve.drain()
                dve.tensor_scalar(nmx[:, u % 2, 0:1], mx[:, u % 2, 0:1], -1.0, None, ALU.mult).then_inc(aA, 1)

            def moved(u):
                j, q = UNITS[u]
                dve.wait_ge(aO, u + 1)
                dve.tensor_copy(ovec[:, u % 2, :], pw[:, 4, 0:P]).then_inc(aF, 1)
                dve.drain()
                pair(att_hi[:, j, q * P:(q + 1) * P], att_lo[:, j, q * P:(q + 1) * P], ovec[:, u % 2, :])

            split_lo(At(39))
            split_lo(At(40))
            biased(0)
            for u in range(8):
                if u + 1 < 8:
                    biased(u + 1)
                j, q = UNITS[u]
                l = lgt[:, u % 2, 0:3, 0:P * (q + 1)]
                dve.wait_ge(aX, u + 1)
                dve.reciprocal(rsum[:, u % 2, 0:1], sums[:, u % 2, 0:1])
                dve.drain()
                dve.tensor_scalar(l, l, rsum[:, u % 2, 0:1], None, ALU.mult).then_inc(aB, 1)
                for c in GS[u][1:]:
                    split_lo(At(C0["gs"] + c))
                if u:
                    moved(u - 1)
                split_lo(At(C0["gs"] + GS[u][-1] + 1))
            moved(7)
            dve.wait_ge(dt_mm, 1)
            dve.tensor_copy(dtn[:, :, :].rearrange("p t h -> p (t h)"), pw[:, 0, 0:128])
            dve.tensor_copy(acn[:, :, :].rearrange("p t h -> p (t h)"), pw[:, 0, 128:256])
            dve.wait_ge(ac_st, 16)
            dve.tensor_copy(decn[:, :], pw[:, 0, 256:320]).then_inc(dt_ev, 1)
            for n in range(2):
                dve.memset(ub[:, n, 0:3], 0.0).then_inc(conv_d, 1)
            dve.drain()

            def group(i, h, gg):
                g = at(4 * h + gg, i, 2)
                ph = f"ssm{h}"
                bc, x = bct[:, gg], xs[:, gg]
                gv = g.times(1)

                def convolve(j):
                    dve.wait_ge(evac, at(E0[ph] + 10 * gg + j, i, 20).times(1, 1))
                    dve.wait_ge(silu_d, g.times(6, j + 1))
                    tile = g.times(1, 32 + 8 * j) if j < 2 else g.times(4, j - 2)
                    u, o = ub[:, j % 2, :], cv[:, j % 2, :]
                    dve.tensor_scalar(o, u[:, 0:S], Cd("cw", tile * 4), Cd("cb", tile), ALU.mult, ALU.add)
                    for k in range(1, 4):
                        dve.drain()
                        ins = dve.scalar_tensor_tensor(o, u[:, k:k + S], Cd("cw", tile * 4 + k), o, ALU.mult, ALU.add)
                    ins.then_inc(conv_d, 1)

                def stepped(t):
                    dve.wait_ge(xt_mm, g.times(4, t + 1))
                    dve.tensor_tensor(xdt[:, :, t * P:(t + 1) * P].rearrange("p c (r n) -> p c r n", r=2),
                                      pw[:, 5 if t % 2 else 1, 0:S].rearrange("p (c r n) -> p c r n", c=2, r=2),
                                      dtn[:, :, span(gv * 8 + 2 * t, 2)].rearrange("p c (r a) -> p c r a", a=1).to_broadcast([P, 2, 2, 64]), ALU.mult).then_inc(xt_ev, 1)

                for j in range(10):
                    split_lo(at(C0[ph] + 10 * gg + j + 1, i, 20))
                    if j < 6:
                        convolve(j)
                    if j == 2:
                        dve.wait_ge(acb_in, g.times(16, 16))
                        for r in range(8):
                            for t in range(2):
                                ins = dve.tensor_scalar(dec[:, r, t, :], acb[:, r, t, :],
                                                        acn[:, t, one(gv * 8 + r)],
                                                        0.0, ALU.subtract, ALU.min)
                        ins.then_inc(dec_in, 1)
                    if j == 3:
                        dve.wait_ge(cb_mm, g.times(1, 1))
                        dve.tensor_tensor(cbm[:, :, :], pw[:, 0, 0:S].rearrange("p (t n) -> p t n", t=2),
                                          C("tri01", 0, 128).rearrange("p (a n) -> p a n", a=1).to_broadcast([P, 2, P]), ALU.mult)
                        dve.tensor_copy(bnat[:, :], pw[:, 0, 256:384]).then_inc(cb_ev, 1)
                        dve.drain()
                    if j == 4:
                        dve.wait_ge(dec_ex, g.times(2, 1))
                        dve.tensor_tensor(dec[:, :, :, :].rearrange("p r t n -> p r (t n)"), dec[:, :, :, :].rearrange("p r t n -> p r (t n)"),
                                          cbm[:, :, :].rearrange("p t n -> p (t n)").rearrange("p (a n) -> p a n", a=1).to_broadcast([P, 8, S]),
                                          ALU.mult).then_inc(m_ok, 1)
                    if j == 5:
                        dve.wait_ge(dec_ex, g.times(2, 2))
                        dve.tensor_tensor(acb[:, :, 1, :], acb[:, :, 1, :],
                                          bc[:, 1, P:S].rearrange("p (a n) -> p a n", a=1).to_broadcast([P, 8, P]),
                                          ALU.mult).then_inc(ce_ok, 1)
                    if 5 <= j < 9:
                        stepped(j - 5)
                    if j == 8:
                        dve.drain()
                        dve.tensor_tensor(xdd[:, :].rearrange("p (r n) -> p r n", r=8),
                                          xdt[:, 0, :].rearrange("p (r n) -> p r n", r=8),
                                          decn[:, wide(gv, 8)].rearrange("p (r a) -> p r a", a=1).to_broadcast([P, 8, 64]),
                                          ALU.mult).then_inc(xdd_ok, 1)
                dve.wait_ge(evac, at(E0[ph] + 10 * gg + 9, i, 20).times(1, 1))
                for t in range(4):
                    dve.wait_ge(y_mm, g.times(4, t + 1))
                    dve.scalar_tensor_tensor(x[:, t, :], x[:, t, :], Cd("dsk", g.times(4, t)),
                                             pw[:, YB[t], 0:S], ALU.mult, ALU.add)
                    dve.drain()
                    dve.tensor_tensor(sz[:, t, :], sz[:, t, :], x[:, t, :], ALU.mult).then_inc(y_ev, 1)
                rms_root(None, pw[:, 5, 0:S], cv[:, 1, :], 512,
                         sems=((ssq_mm, g.times(4, 4)), ssq_v, (ssq_r, g.times(1, 1)), xdd[:, 0:S], cv[:, 0, :]))
                for t in range(4):
                    dve.scalar_tensor_tensor(sz[:, t, :], sz[:, t, :], Cd("ssmn", g.times(4, t)), rstd[:, :],
                                             ALU.mult, ALU.mult)
                dve.drain()
                k = wide(i * 2 + gg, 4)
                dve.tensor_copy(y_hi[:, k, :], sz[:, :, :])
                dve.drain()
                dve.tensor_tensor(y_lo[:, k, :], sz[:, :, :], y_hi[:, k, :].bitcast(F32), ALU.subtract).then_inc(grp, 1)

            def posts8(ph, b0, f, ring=2, n=2, off=0, buf=None):
                with dve.Fori(0, n) as i:
                    for j in range(8):
                        jj = 4 * off + j
                        split_lo(at(C0[ph] + jj + 1, i, 8))
                        late = 3 if ring == 4 else 0
                        if j - late in (0, 2, 4):
                            mod_piece(i + b0, (j - late) // 2, buf or mraw_b, ring)
                        if f is not None:
                            dve.wait_ge(evac, at(E0[ph] + jj, i, 8).times(1, 1))
                            f(i * 2 + off, j, at(POST0[ph] + jj, i, 8).slot(4))
                        if j == 7:
                            mod_finish(i + b0)

            def posts(ph, n, f, last=False, first=0):
                def four(i):
                    for j in range(4):
                        split_lo(at(C0[ph] + j + 1, i, 4))
                        dve.wait_ge(evac, at(E0[ph] + j, i, 4).times(1, 1))
                        f(i, j, at(POST0[ph] + j, i, 4).slot(4))
                if last:
                    four(0)
                with dve.Fori(first or int(last), n - last) as i:
                    four(i)
                if last:
                    four(n - 1)

            for h in range(2):
                with dve.Fori(0, 2) as i:
                    group(i, h, 0)
                    group(i, h, 1)

                def add_s(i, j, s):
                    m = one(i * 4 + j)
                    dve.tensor_tensor(accS[:, m, :], accS[:, m, :], tm[:, s:s + 1, :], ALU.add).then_inc(post, 1)

                posts8(f"sp{h}", 12 + 2 * h, add_s if h else None, 4)
                if h == 0:
                    for n in range(2):
                        dve.memset(ub[:, n, 0:3], 0.0)
                    dve.drain()
            dve.drain()
            dve.tensor_scalar(lcon[:, 0, :], C("lam", 0, 8), -1.0, None, ALU.mult)
            dve.drain()
            softplus(lcon[:, 0, :], [lcon[:, k, :] for k in (1, 2, 3, 4)], lcon[:, 5, :], 3, lam_x)
            dve.tensor_scalar(lcon[:, 5, :], lcon[:, 5, :], 8.0, None, ALU.mult)
            for c in range(4):
                split_lo(At(C0["ap"] + c + 1))

            def gate_a(i, j, s):
                m = one(i * 4 + j)
                if j % 4 == 0:
                    dve.wait_ge(gs_in[j // 4], i * 8 + 16)
                dve.tensor_tensor(accS[:, m, :], accS[:, m, :], gsr[:, j:j + 1, :], ALU.mult)
                dve.tensor_tensor(t2[:, j % 2, :].rearrange("p (a n) -> p a n", a=1), accA[:, m, :], tm[:, s:s + 1, :], ALU.mult).then_inc(post, 1)
                dve.drain()
                dve.tensor_tensor(t2[:, j % 2, :].rearrange("p (a n) -> p a n", a=1), t2[:, j % 2, :].rearrange("p (a n) -> p a n", a=1), accS[:, m, :], ALU.add)
                dve.drain()
                pair(mg_hi[:, m, :], mg_lo[:, m, :], t2[:, j % 2, :].rearrange("p (a n) -> p a n", a=1))

            posts8("ga", 16, gate_a)
            dve.drain().then_inc(acts_ok, 1)
            dve.wait_ge(x_in, 32)

            def add_x(i, j, s):
                m = one(i * 4 + j)
                dve.scalar_tensor_tensor(x1[:, m, :], tm[:, s:s + 1, :], modT[:, one(i * 4 + (32 + j))], x1[:, m, :],
                                         ALU.mult, ALU.add).then_inc(post, 1)
                dve.drain()
                dve.tensor_tensor(sq1[:, 14:15, :], x1[:, m, :], x1[:, m, :], ALU.mult)
                dve.drain()
                dve.tensor_tensor(ssum[:, 0:1, :], ssum[:, 0:1, :], sq1[:, 14:15, :], ALU.add)

            dve.memset(ssum[:, :, :], 0.0)
            dve.drain()
            posts8("wo", 18, add_x)
            dve.drain().then_inc(rq, 1)
            rms_root(2, pw[:, 4, 0:S], xq[:, 1, :], D, sems=((rm, 2), rv, (rs, 2), xq[:, 2, :], xq[:, 0, :]))
            wide_rstd = rstd[:, :].rearrange("p (a n) -> p a n", a=1).to_broadcast([P, 4, S])
            for m in range(4):
                dve.tensor_tensor(sq1[:, 4 * m:4 * m + 4, :], x1[:, 4 * m:4 * m + 4, :], wide_rstd, ALU.mult)
                modulate(m, sq1, gain2, C("n2", 0, 16), 48, 64)
            dve.wait_ge(x1_st, 16)
            dve.drain().then_inc(acts_ok, 1)

            def hidden(i, j, s):
                if j % 2:
                    f = one(i * 2 + j // 2)
                    o = hf[:, j // 2 % 2:j // 2 % 2 + 1, :]
                    dve.tensor_tensor(o, tf[:, s - 1:s, :], tf[:, s:s + 1, :], ALU.mult).then_inc(post, 1)
                    dve.drain()
                    dve.tensor_copy(hid_hi[:, f, :], o).then_inc(post, 1)
                    dve.drain()
                    dve.tensor_tensor(hid_lo[:, f, :], o, hid_hi[:, f, :].bitcast(F32), ALU.subtract)

            posts("fi", 1, hidden)
            posts8("fi", 20, hidden, n=4, off=1, buf=mraw_c)
            posts("fi", FF_T // 2, hidden, first=9)
            dve.drain().then_inc(acts_ok, 1)
            dve.wait_ge(x1_in, 16)
            dve.memset(ssum[:, :, :], 0.0)
            dve.drain()
            sqt = hf[:, 0:1, :]
            with dve.Fori(0, 8) as i:
                for m in range(2):
                    for q in range(4):
                        c = at(C0["fo"] + 4 * m + q, i, 8)
                        split_lo(c + 1)
                    dve.wait_ge(evac, at(E0["fo"] + m, i, 2).times(1, 1))
                    k = one(i * 2 + m)
                    dve.scalar_tensor_tensor(x1r[:, k, :], tf[:, (POST0["fo"] + m) % 2:(POST0["fo"] + m) % 2 + 1, :],
                                             modT[:, one(i * 2 + (80 + m))], x1r[:, k, :], ALU.mult, ALU.add).then_inc(post, 1)
                    dve.drain()
                    fin = Cd("fin", i * 2 + m)
                    dve.tensor_tensor(sqt, x1r[:, k, :], x1r[:, k, :], ALU.mult)
                    dve.drain()
                    dve.tensor_tensor(ssum[:, 0:1, :], ssum[:, 0:1, :], sqt, ALU.add)
                    dve.tensor_scalar(sqt, sqt, fin, None, ALU.mult)
                    dve.drain()
                    dve.scalar_tensor_tensor(ssum[:, 1:2, :], sqt, fin, ssum[:, 1:2, :], ALU.mult, ALU.add)
            dve.drain().then_inc(rq, 1)
            v3, rec3, tmp, root3, rec4, w, v4, both = (sqF[:, k, :] for k in (1, 0, 2, 3, 4, 5, 7, 8))
            dve.wait_ge(rm, 3)
            dve.tensor_scalar(v3, pw[:, 4, 0:S], 1.0 / D, EPS, ALU.mult, ALU.add)
            dve.drain()
            dve.reciprocal(rec3, v3).then_inc(rv, 1)
            dve.tensor_scalar(w, pw[:, 4, S:2 * S], 1.0 / D, None, ALU.mult)
            dve.tensor_tensor(lcon[:, 0:2, :].rearrange("p a k -> p (a k)"), C("fin", 0, 16), C("ln2", 0, 16), ALU.mult)
            dve.drain()
            dve.scalar_tensor_tensor(w, v3, EPS, w, ALU.mult, ALU.add)
            dve.drain()
            dve.reciprocal(rec4, w)
            dve.drain()
            dve.tensor_tensor(rec4, rec4, v3, ALU.mult).then_inc(rv, 1)
            dve.tensor_tensor(v4, w, rec3, ALU.mult)
            dve.wait_ge(rs, 3)
            newton(root3, v3, tmp)
            dve.wait_ge(rs, 4)
            newton(rstd[:, :], v4, tmp)
            dve.tensor_tensor(both, root3, rstd[:, :], ALU.mult)
            dve.drain()
            for m in range(4):
                for k in range(4 * m, 4 * m + 4):
                    ins = dve.scalar_tensor_tensor(accM[:, k, :], x1r[:, k, :], lcon[:, k // 8, k % 8:k % 8 + 1], both, ALU.mult, ALU.mult)
                for k in range(4 * m, 4 * m + 4):
                    ins2 = dve.scalar_tensor_tensor(x2T[:, k, :], x1r[:, k, :], C("fin", k), root3, ALU.mult, ALU.mult)
                ins2.then_inc(quarter, 1)
            for _ in range(2):
                dve.drain().then_inc(acts_ok, 1)
            for n in range(2):
                ins = dve.memset(ub2[:, n, 0:3], 0.0)
            dve.drain().then_inc(pad_ok, 1)

            def conv2(i, j, s):
                t = i * 4 + j
                u, o = ub2[:, j % 2:j % 2 + 1, :], uc[:, one(t), :]
                dve.tensor_scalar(o, u[:, :, 0:S], Cd("cw2", t * 4), Cd("cb2", t), ALU.mult, ALU.add)
                for k in range(1, 4):
                    dve.drain()
                    ins = dve.scalar_tensor_tensor(o, u[:, :, k:k + S], Cd("cw2", t * 4 + k), o, ALU.mult, ALU.add)
                ins.then_inc(post, 1)

            posts("lx", 2, conv2)
            dve.drain().then_inc(uc_ok, 1)
            for i in range(2):
                split_lo(At(C0["lg"] + 4 * i + 1))
                dve.wait_ge(lru_g, i + 1)
                for t in range(4):
                    dve.tensor_scalar(lr[:, t, :], lr[:, t, :], lcon[:, 5, 4 * i + t:4 * i + t + 1], None, ALU.mult)
                dve.drain().then_inc(lru_l, 1)
                split_lo(At(C0["lg"] + 4 * i + 2))
                dve.wait_ge(lru_e, i + 1)
                dve.tensor_scalar(lw[:, :, :], lt[:, :, :], 1.0, None, ALU.add)
                dve.drain()
                dve.reciprocal(lw[:, :, :], lw[:, :, :])
                dve.drain()
                dve.scalar_tensor_tensor(lw[:, :, :], lt[:, :, :], 2.0, lw[:, :, :], ALU.mult, ALU.mult).then_inc(lru_w, 1)
                dve.tensor_tensor(li[:, :, :], li[:, :, :], uc[:, 4 * i:4 * i + 4, :], ALU.mult)
                split_lo(At(C0["lg"] + 4 * i + 3))
                dve.wait_ge(lru_q, i + 1)
                dve.drain()
                dve.tensor_tensor(lw[:, :, :], lw[:, :, :], li[:, :, :], ALU.mult)
                dve.drain()
                for t in range(4):
                    dve.tensor_tensor_scan(lt[:, t, :], la[:, t, :], lw[:, t, :], 0.0, ALU.mult, ALU.add)
                split_lo(At(C0["lg"] + 4 * i + 4))
                dve.drain()
                for t in range(4):
                    dve.wait_ge(evac, E0["lg"] + 4 * i + t + 1)
                    dve.tensor_tensor(gl[:, t, :], gl[:, t, :], lt[:, t, :], ALU.mult)
                    dve.drain()
                    ins = pair(yb_hi[:, 4 * i + t, :], yb_lo[:, 4 * i + t, :], gl[:, t, :])
                ins.then_inc(lru_y, 1)
            dve.drain().then_inc(acts_ok, 1)

            def quiet(ph, n):
                with dve.Fori(0, n) as i:
                    for j in range(4):
                        split_lo(at(C0[ph] + j + 1, i, 4))

            def branch(ph):
                quiet("wb" + ph, 2)

                def merge(i, j, s):
                    m = one(i * 4 + j)
                    o = accM[:, m, :] if ph == "a" else t3[:, j % 2:j % 2 + 1, :]
                    dve.tensor_tensor(o, proj[:, m, :], tm2[:, s:s + 1, :], ALU.mult).then_inc(post, 1)
                    if ph != "a":
                        dve.drain()
                        dve.tensor_tensor(o if ph == "c" else accM[:, m, :], o, accM[:, m, :], ALU.add)
                    if ph == "c":
                        dve.drain()
                        pair(m2_hi[:, m, :], m2_lo[:, m, :], o)

                posts("mg" + ph, 4, merge)

            branch("a")
            split_lo(At(C0["bf"] + 1))
            split_lo(At(C0["nq"] + 1))
            dve.wait_ge(evac, E0["bf"] + 1)
            f = slice(32, 40)
            dve.tensor_scalar(zf[f, :], zf[f, :], -1.0, None, ALU.mult)
            dve.drain()
            softplus(zf[f, :], [sft[f, k, :] for k in (0, 1, 2, 3)], sft[f, 4, :], 4)
            dve.tensor_scalar(sft[f, 4, :], sft[f, 4, :], -1.0, None, ALU.mult)
            dve.memset(sft[f, 0, :], 1.0)
            dve.drain()
            dve.tensor_tensor_scan(zf[f, :], sft[f, 0, :], sft[f, 4, :], 0.0, ALU.mult, ALU.add)
            dve.tensor_scalar(nudge[:, :], cst[:, CO["ident"] + 32:CO["ident"] + 40], -1.0, None, ALU.mult)
            dve.drain().then_inc(zf_ok, 1)
            split_lo(At(C0["nq"] + 2))
            dve.wait_ge(gn_mm, 1)
            dve.tensor_copy(gn[:, :, :], pw[:, 5, 0:S].rearrange("p (t n) -> p t n", t=2)[:, :, 0:24])
            dve.tensor_copy(cn[:, :, :], pw[:, 5, 0:S].rearrange("p (t n) -> p t n", t=2)[:, :, 32:40])
            dve.tensor_scalar(C("gnq"), C("gnq"), ATT_SCALE, None, ALU.mult)
            dve.tensor_scalar(C("gfq"), C("gfq"), ATT_SCALE, None, ALU.mult)
            dve.drain().then_inc(gn_ok, 1)
            def head_norm(n, tiles, gain):
                rms_root(None, pw[:, 5, 0:512], hv_[:, :], P, hr_[:, :],
                         sems=((hm, n + 1), hv, (hr, n + 1), ht_[:, :], he_[:, :]))
                ins = dve.scalar_tensor_tensor(tiles, tiles, gain, hr_[:, :], ALU.mult, ALU.mult)
                dve.drain().then_inc(hn_ok, 1)

            def block_tokens():
                for x in range(2):
                    for v in range(2):
                        src = nk[:, 8 + 2 * x + v, :].rearrange("p (c t) -> p t c", t=16)
                        for r in range(2):
                            dve.tensor_tensor(kp[:, x, 16 * r:16 * r + 16, 15 * v:15 * v + 15], src[:, :, r:r + 15],
                                              C("pos", 32 * x + 16 * r, 16).rearrange("p (t a) -> p t a", a=1).to_broadcast([P, 16, 15]),
                                              ALU.add)
                dve.drain()

            kall = lambda t: t[:, :, :, :].rearrange("p x t c -> p (x t c)")
            two = lambda t, n: t[:, n:n + 2, :].rearrange("p k n -> p (k n)")
            for c in range(2, 20):
                split_lo(At(C0["nq"] + c + 1))
                if c - 3 in NSA_N:
                    n = NSA_N.index(c - 3)
                    head_norm(n, two(nk, c - 3), C("gnq") if n < 4 else C("gnk"))
                if c == 12:
                    dve.wait_ge(evac, E0["nq"] + 12)
                    block_tokens()
                if c == 13:
                    dve.tensor_copy(kall(kp_hi), kall(kp))
                    dve.drain()
                if c == 14:
                    dve.tensor_tensor(kall(kp_lo), kall(kp), kall(kp_hi).bitcast(F32), ALU.subtract).then_inc(kp_ok, 1)
            for j in range(8):
                split_lo(At(C0["cmp"] + j + 1))
            split_lo(At(C0["ng"] + 1))
            split_lo(At(C0["ng"] + 2))
            dve.wait_ge(kc_ev, 1)
            rms_root(None, pw[:, 5, 0:30], kcs[:, 3, :], P, kcs[:, 1, :], sems=((hm, 7), hv, (hr, 7), kcs[:, 4, :], kcs[:, 2, :]))
            dve.scalar_tensor_tensor(kcT[:, :], kcT[:, :], C("gnk"), kcs[:, 1, :], ALU.mult, ALU.mult)
            dve.drain().then_inc(hn_ok, 1)

            def att_bias(b):
                kind, h0, q = BATCH[b]
                n = P * (q + 1) if kind else 15
                dve.wait_ge(aL, 8 + b + 1)
                if b % 100 and b not in (NSA_B, NSA_B + 1) and b >= 2:
                    dve.wait_ge(aT, 8 + b - 1)
                l = (lg3 if kind == 3 else lg2)[:, b % 2, :, 0:n]
                flat = pw[:, 0:2, :].rearrange("p b (r n) -> p (b r) n", r=2)[:, :, 0:n]
                mask = (C("tri", 0, 256) if q else C("tri", 128, 128)) if kind else C("cmask", 15 * q, 15)
                if kind == 3:
                    for r in range(4):
                        dve.scalar_tensor_tensor(l[:, r, :], flat[:, r, :], cn[:, q, h0 + r:h0 + r + 1], mask, ALU.add, ALU.add)
                else:
                    dve.tensor_tensor(l, flat, mask.rearrange("p (a n) -> p a n", a=1).to_broadcast([P, 4, n]), ALU.add)
                dve.drain()
                dve.tensor_reduce(mx[:, b % 2, :], l, AX.X, ALU.max)
                dve.drain()
                dve.tensor_scalar(nmx[:, b % 2, :], mx[:, b % 2, :], -1.0, None, ALU.mult).then_inc(aA, 1)

            def att_scale(b):
                kind, h0, q = BATCH[b]
                n = P * (q + 1) if kind else 15
                l = (lg3 if kind == 3 else lg2)[:, b % 2, :, 0:n]
                s_, r_ = sums[:, b % 2, :], rsum[:, b % 2, :]
                dve.wait_ge(aX, 8 + b + 1)
                if kind == 0:
                    dve.tensor_tensor(l, l, C("cmask", 30 + 15 * q, 15).rearrange("p (a n) -> p a n", a=1).to_broadcast([P, 4, 15]), ALU.mult)
                    dve.drain()
                    dve.tensor_reduce(s_, l, AX.X, ALU.add)
                    dve.drain()
                dve.tensor_scalar(s_, s_, 1e-30, None, ALU.max)
                dve.drain()
                dve.reciprocal(r_, s_)
                dve.drain()
                if kind < 3:
                    dve.tensor_tensor(r_, r_, gn[:, q, 3 * h0 + kind:3 * h0 + kind + 10:3], ALU.mult)
                    dve.drain()
                for r in range(4):
                    ins = dve.tensor_scalar(l[:, r, :], l[:, r, :], r_[:, r:r + 1], None, ALU.mult)
                ins.then_inc(aB, 1)

            def att_moved(b):
                kind, h0, q = BATCH[b]
                if kind < 2:
                    return
                dve.wait_ge(aO, 8 + b + 1)
                dve.tensor_copy((fx if kind == 3 else nk)[:, h0:h0 + 4, q * P:(q + 1) * P],
                                pw[:, 4, :].rearrange("p (r n) -> p r n", r=4)).then_inc(aF, 1)

            def gated(ph, src, g):
                t = slice(4 * g, 4 * g + 4)
                dve.wait_ge(evac, E0[ph] + 4 * g + 4)
                dve.drain()
                dve.tensor_tensor(src[:, t, :], src[:, t, :], gate[:, t, :], ALU.mult)
                dve.drain()
                pair(yb_hi[:, t, :], yb_lo[:, t, :], src[:, t, :]).then_inc(yb_ok, 1)

            def attention(b0, b1, ph, src):
                att_bias(b0)
                for b in range(b0, b1):
                    if b + 1 < b1:
                        att_bias(b + 1)
                    att_scale(b)
                    rides = RIDES.get(b, [])
                    for c in rides[1:]:
                        split_lo(At(C0[ph] + c))
                    if b > b0:
                        att_moved(b - 1)
                    for c in rides[-1:]:
                        split_lo(At(C0[ph] + c + 1))
                    if b == (b0 + b1) // 2 + 1:
                        gated(ph, src, 0)
                att_moved(b1 - 1)
                gated(ph, src, 1)
                dve.drain().then_inc(acts_ok, 1)

            attention(0, NSA_B, "ng", nk)
            branch("b")
            for c in range(24):
                split_lo(At(C0["fx"] + c + 1))
                if 3 <= c < 19 and c % 2:
                    n = (c - 3) // 2
                    head_norm(7 + n, two(fx, 2 * n), C("gfq") if n < 4 else C("gfk"))
            attention(NSA_B, len(BATCH), "fg", fx)
            branch("c")
            dve.drain().then_inc(acts_ok, 1)

            def add_x2(i, j, s):
                m = one(i * 4 + j)
                dve.tensor_tensor(x2T[:, m, :], x2T[:, m, :], tm2[:, s:s + 1, :], ALU.add).then_inc(post, 1)
                dve.drain()
                pair(act_hi[:, m, :], act_lo[:, m, :], x2T[:, m, :])

            dve.wait_ge(p_land, 16)
            pair(p_hi[:, :, :], p_lo[:, :, :], p_in[:, :, :]).then_inc(p_ok, 1)
            posts("w2", 4, add_x2)
            dve.drain().then_inc(h_ok, 1)
            for c in range(2):
                split_lo(At(C0["ple"] + c + 1))

            def finish(i, j, s):
                m = one(i * 4 + j)
                o = t3[:, j % 2:j % 2 + 1, :]
                if isinstance(i, int) and i + j == 0:
                    rms_root(5, pw[:, 4, 0:S], sqF[:, 1, :], D, sems=((rm, 4), rv, (rs, 5), sqF[:, 2, :], sqF[:, 0, :]))
                dve.scalar_tensor_tensor(o, eT[:, m, :], Cd("pleg", i * 4 + j), rstd[:, :].rearrange("p (a n) -> p a n", a=1), ALU.mult, ALU.mult)
                dve.drain()
                dve.tensor_tensor(o, o, tm2[:, s:s + 1, :], ALU.mult).then_inc(post, 1)
                dve.drain()
                dve.tensor_tensor(x2T[:, m, :], x2T[:, m, :], o, ALU.add)
                if j == 3:
                    dve.drain().then_inc(out_ok, 1)

            posts("pg", 4, finish, last=True)


def tiles(w, kt=16):
    k, m = w.shape
    return w.reshape(k // P // kt, kt, P, m // P, P).transpose(3, 0, 2, 1, 4)


def padded(w, cols):
    out = np.zeros((w.shape[0], cols), w.dtype)
    out[:, :w.shape[1]] = w
    return out


def per_tile(v):
    return v.reshape(-1, P).T


def feature_major(x):
    return np.ascontiguousarray(x.T.reshape(-1, P, x.shape[0]).transpose(1, 0, 2))


def distance_buckets():
    out = np.zeros((33, 3, 512), np.float32)
    for g, (window, dil) in enumerate(((128, 1), (512, 4), (2048, 16))):
        for i in range(512):
            d = 255 - i
            if d < 0 or d % dil or d > window:
                out[32, g, i] = 1
                continue
            n = np.float32(max(d, 1))
            large = 16 + int(np.float32(np.log(n / np.float32(16))) / np.float32(np.log(2048 / 16)) * np.float32(16))
            out[d if d < 16 else min(large, 31), g, i] = 1
    return out


def pack(a):
    f = lambda n: np.asarray(a[n])
    w_in = f("w_in")[0]
    chunks = [tiles(w_in[:, 0:4608])]
    chunks.append(tiles(padded(w_in[:, 14848:14912], P)))
    chunks.append(tiles(w_in[:, 16960:19008]))
    tz, tx = tiles(w_in[:, 4608:8704]), tiles(w_in[:, 8704:14848])
    sp = f("w_ssm_proj")[0]
    for h in range(2):
        for g in range(4 * h, 4 * h + 4):
            chunks += [tx[32 + g:33 + g], tx[40 + g:41 + g], tx[4 * g:4 * g + 4], tz[4 * g:4 * g + 4]]
        chunks.append(tiles(sp[2048 * h:2048 * h + 2048]))
    ap = f("w_attn_proj")[0].reshape(4, P, 4, 4, P)
    chunks.append(ap.transpose(2, 1, 3, 0, 4).reshape(4, 1, P, 16, P))
    chunks.append(tiles(w_in[:, 14912:16960]))
    chunks.append(tiles(f("w_out")[0]))
    ff = tiles(f("w_ffn_in")[0])
    chunks.append(np.stack([ff[0:FF_T], ff[FF_T:]], 1).reshape(2 * FF_T, 1, P, 16, P))
    w2 = f("w_in_2")[0]
    b2 = f("b_in_2")[0]
    o2, at2 = {}, 0
    for name, n in (("lx", 1024), ("lg", 1024), ("q", 1024), ("kv", 1536), ("bg", 24), ("ng", 1024),
                    ("fx", 3072), ("ff", 8), ("fg", 1024), ("mg", 6144)):
        o2[name] = slice(at2, at2 + n)
        at2 += n
    mg = [slice(o2["mg"].start + 2048 * b, o2["mg"].start + 2048 * b + 2048) for b in range(3)]

    def gates(v):
        out = np.zeros(v.shape[:-1] + (P,), v.dtype)
        out[..., 0:24] = v[..., o2["bg"]]
        out[..., 32:40] = v[..., o2["ff"]]
        return out

    wb = f("w_branch_2")[0]

    def branch(b):
        return wb[b].reshape(8, P, 8, 2, P).transpose(2, 1, 3, 0, 4).reshape(8, P, 16, P)

    hidden = f("cmp_w1_2")[0].reshape(8, 8, P, 256).transpose(0, 2, 1, 3).reshape(8, 1, P, 16, P)
    chunks += [tiles(w2[:, o2["lx"]]), tiles(w2[:, o2["lg"]]), branch(0), tiles(w2[:, mg[0]]),
               tiles(gates(w2)), tiles(w2[:, o2["q"]]), tiles(w2[:, o2["kv"]]), hidden,
               tiles(w2[:, o2["ng"]]), branch(1), tiles(w2[:, mg[1]]),
               tiles(w2[:, o2["fx"]]), tiles(w2[:, o2["fg"]]), branch(2), tiles(w2[:, mg[2]]),
               tiles(f("w_out_2")[0]),
               f("w_ple_2")[0].reshape(2, P, 2, 8, P).transpose(2, 1, 3, 0, 4).reshape(2, P, 16, P),
               tiles(f("w_ple_gate_2")[0])]
    w16 = np.concatenate([c.reshape(-1, P, 16, P) for c in chunks])
    w11 = np.ascontiguousarray(tiles(f("w_ffn_out")[0], KFO).reshape(NFO, P, KFO, P))
    wm = np.ascontiguousarray(f("w_mod")[0].reshape(4, 4, P, 24, 512).transpose(3, 0, 2, 1, 4))
    cst = np.zeros((P, NCST), np.float32)

    def put(name, v):
        v = np.asarray(v)
        cst[:v.shape[0], CO[name]:CO[name] + v.shape[1]] = v

    put("c", per_tile(f("c")[0]))
    put("bmod", per_tile(f("b_mod")[0]))
    put("n1", per_tile(f("norm1_w")[0]))
    put("n2", per_tile(f("norm2_w")[0]))
    put("fin", per_tile(f("final_norm_w")))
    put("cw", f("conv_w")[0].reshape(4, 48, P).transpose(2, 1, 0).reshape(P, 192))
    put("cb", per_tile(f("conv_b")[0]))
    put("dtb", f("dt_bias")[0][:, None])
    put("alog", f("a_log")[0][:, None])
    put("dsk", per_tile(np.repeat(f("d_skip")[0], 64)))
    put("ssmn", per_tile(f("ssm_norm_w")[0]))
    put("rel", np.concatenate([f("rel_bias"), np.full((1, 12), NEG, np.float32)]))
    put("ident", np.eye(P))
    order = [b2[o2["lx"]], b2[o2["lg"]], b2[mg[0]], gates(b2), b2[o2["q"]], b2[o2["kv"]], b2[o2["ng"]],
             b2[mg[1]], b2[o2["fx"]], b2[o2["fg"]], b2[mg[2]]]
    put("b2", per_tile(np.concatenate(order)))
    put("cw2", f("conv_w_2")[0].reshape(4, 8, P).transpose(2, 1, 0).reshape(P, 32))
    put("cb2", per_tile(f("conv_b_2")[0]))
    put("ba", per_tile(f("lru_ba_2")[0]))
    put("bx", per_tile(f("lru_bx_2")[0]))
    put("lam", per_tile(f("lru_lambda_2")[0]))
    put("pos", f("cmp_pos_2")[0].transpose(2, 0, 1).reshape(P, 64))
    for name, src in (("gnq", "nsa_q_gain_2"), ("gnk", "nsa_k_gain_2"), ("gfq", "fox_q_gain_2"), ("gfk", "fox_k_gain_2")):
        put(name, f(src)[0][:, None])
    put("ln2", per_tile(f("ln_gain_2")[0]))
    put("pleg", per_tile(f("ple_gain_2")[0]))
    i = np.arange(P)
    tri = np.zeros((P, 256), np.float32)
    tri[:, 128:] = np.where(i[None, :] <= i[:, None], 0, NEG)
    put("tri", tri)
    seen = (np.arange(15) * 16 + 31)[None, None, :] <= i[:, None, None] + P * np.arange(2)[None, :, None]
    put("cmask", np.concatenate([np.where(seen, 0, NEG).reshape(P, 30), seen.reshape(P, 30)], 1).astype(np.float32))
    wab = np.zeros((P, 8, 2, P), np.float32)
    for n, name in enumerate(("lru_wa_2", "lru_wx_2")):
        v = f(name)[0].reshape(8, 2, 64, 64)
        for r in range(2):
            wab[64 * r:64 * r + 64, :, n, 64 * r:64 * r + 64] = v[:, r].transpose(1, 0, 2)
    cw2 = np.ascontiguousarray(f("cmp_w2_2")[0].reshape(2, 2, P, P).transpose(2, 0, 1, 3))
    put("tri01", (i[None, :] >= i[:, None]).astype(np.float32))
    return {"w16": w16, "w11": w11, "wm": wm, "cst": cst, "onehot": distance_buckets(),
            "xt": feature_major(f("x")[0]), "pt": feature_major(f("p_2")[0, 0]), "wab": wab, "cw2": cw2}


_NAMES = ["w16", "w11", "wm", "cst", "onehot", "xt", "pt", "wab", "cw2"]


def kernel(**inputs):
    import numpy as _np
    import concourse.bacc as _bacc
    from concourse import mybir as _mybir
    from concourse.bass_utils import run_bass_kernel_spmd as _run

    arrays = {k: _np.ascontiguousarray(v) for k, v in pack(inputs).items()}
    nc = _bacc.Bacc("TRN2", target_bir_lowering=False, num_devices=1)
    args = [nc.dram_tensor(k, arrays[k].shape, _mybir.dt.float32, kind="ExternalInput").ap() for k in _NAMES]
    args.append(nc.dram_tensor("out_dram", (P, DT * S), _mybir.dt.float32, kind="ExternalOutput").ap())
    first_and_second_block(nc, *args)
    r = _run(nc, [arrays], core_ids=[0])
    got = r.results[0]["out_dram"]
    return got.reshape(P, DT, S).transpose(2, 1, 0).reshape(1, S, D)
```
